# Optimizing a Trainium2 kernel written in Bass

```python
import jax, jax.numpy as jnp
from jax import lax
import numpy as np

D_MODEL = 1024
BATCH = 1
SEQ = 256
DEPTH = 2

GRID_W = 64
HEAD_DIM = 64
EPS = 1e-6
ROPE_THETA = 10000.0
Q_BLOCK = 128
NEG_INF = -1e30
NA_HEADS = 4
NA_WIN_ROWS = 8
NA_WIN_COLS = 16
GQA_Q_HEADS = 6
GQA_KV_HEADS = 2
DIL_GROUPS = ((128, 1), (512, 4), (2048, 16))
DIL_HEADS_PER_GROUP = 2
DIL_HEADS = len(DIL_GROUPS) * DIL_HEADS_PER_GROUP
QA_W = NA_HEADS * HEAD_DIM
QB_W = GQA_Q_HEADS * HEAD_DIM
QC_W = DIL_HEADS * HEAD_DIM
KA_W = NA_HEADS * HEAD_DIM
KB_W = GQA_KV_HEADS * HEAD_DIM
KC_W = DIL_HEADS * HEAD_DIM
Q_W = QA_W + QB_W + QC_W
KV_W = KA_W + KB_W + KC_W
N_BRANCHES = 3
GATE_W = N_BRANCHES * D_MODEL
IN_W = Q_W + 2 * KV_W + GATE_W
BR_A = NA_HEADS * HEAD_DIM
BR_B = GQA_Q_HEADS * HEAD_DIM
BR_C = DIL_HEADS_PER_GROUP * HEAD_DIM
BRANCH_W = BR_A + BR_B + BR_C
FFN_DIM = 2816
N_EXPERTS = 8
TOP_K = 2
EXPERT_DIM = 3584

kernel_name = 'hybrid_gated_mixer_encoder'

def rms_norm(x, g):
    xf = x.astype(jnp.float32)
    y = xf * lax.rsqrt(jnp.mean(xf * xf, axis=-1, keepdims=True) + EPS)
    return (y * g.astype(jnp.float32)).astype(x.dtype)

def rope_angles(pos, dim):
    inv_freq = ROPE_THETA ** (-jnp.arange(0, dim, 2, dtype=jnp.float32) / dim)
    return pos.astype(jnp.float32)[:, None] * inv_freq[None, :]

def apply_rope(x, ang):
    half = x.shape[-1] // 2
    cos = jnp.cos(ang).astype(x.dtype)
    sin = jnp.sin(ang).astype(x.dtype)
    x1, x2 = x[..., :half], x[..., half:]
    return jnp.concatenate([x1 * cos - x2 * sin, x2 * cos + x1 * sin], axis=-1)

def axial_rope(x, ang_row, ang_col):
    half = x.shape[-1] // 2
    return jnp.concatenate([apply_rope(x[..., :half], ang_row), apply_rope(x[..., half:], ang_col)], axis=-1)

def to_heads(t, n):
    b, s, _ = t.shape
    return t.reshape(b, s, n, HEAD_DIM).transpose(0, 2, 1, 3)

def from_heads(t):
    b, h, s, dh = t.shape
    return t.transpose(0, 2, 1, 3).reshape(b, s, h * dh)

def neighbourhood_attention(q, k, v, rpb):
    b, h, s, dh = q.shape
    rows = s // GRID_W
    kh = min(NA_WIN_ROWS, rows)
    kw = NA_WIN_COLS
    scale = HEAD_DIM ** -0.5
    qg = q.reshape(b, h, rows, GRID_W, dh).astype(jnp.float32)
    kg = k.reshape(b, h, rows, GRID_W, dh).astype(jnp.float32)
    vg = v.reshape(b, h, rows, GRID_W, dh)
    r = jnp.arange(rows)
    row_start = jnp.clip(r - kh // 2, 0, rows - kh)
    key_rows = row_start[:, None] + jnp.arange(kh)[None, :]
    c = jnp.arange(GRID_W)
    col_start = jnp.clip(c - kw // 2, 0, GRID_W - kw)
    col_mask = (c[None, :] >= col_start[:, None]) & (c[None, :] < col_start[:, None] + kw)
    k_band = kg[:, :, key_rows]
    v_band = vg[:, :, key_rows]
    sc = jnp.einsum('bhrqd,bhrkcd->bhrqkc', qg, k_band) * scale
    dr_idx = key_rows - r[:, None] + NA_WIN_ROWS - 1
    dc_idx = jnp.clip(c[None, :] - c[:, None], -(kw - 1), kw - 1) + NA_WIN_COLS - 1
    bias = rpb.astype(jnp.float32)[:, dr_idx[:, None, :, None], dc_idx[None, :, None, :]]
    sc = jnp.where(col_mask[:, None, :], sc + bias, NEG_INF)
    p = jax.nn.softmax(sc.reshape(b, h, rows, GRID_W, kh * GRID_W), axis=-1)
    p = p.reshape(b, h, rows, GRID_W, kh, GRID_W).astype(v.dtype)
    o = jnp.einsum('bhrqkc,bhrkcd->bhrqd', p, v_band)
    return o.reshape(b, h, s, dh)

def gqa_attention(q, k, v):
    b, hq, s, dh = q.shape
    hkv = k.shape[1]
    g = hq // hkv
    nb = s // Q_BLOCK
    scale = HEAD_DIM ** -0.5
    kf = k.astype(jnp.float32)
    qb = q.reshape(b, hkv, g, nb, Q_BLOCK, dh).transpose(3, 0, 1, 2, 4, 5)

    def block(qi):
        sc = jnp.einsum('bkgqd,bksd->bkgqs', qi.astype(jnp.float32), kf) * scale
        p = jax.nn.softmax(sc, axis=-1).astype(v.dtype)
        return jnp.einsum('bkgqs,bksd->bkgqd', p, v)

    o = lax.map(block, qb)
    return o.transpose(1, 2, 3, 0, 4, 5).reshape(b, hq, s, dh)

def dilated_attention(q, k, v):
    b, h, s, dh = q.shape
    hpg = DIL_HEADS_PER_GROUP
    nb = s // Q_BLOCK
    scale = HEAD_DIM ** -0.5
    k_groups = [k[:, gi * hpg:(gi + 1) * hpg].astype(jnp.float32) for gi in range(len(DIL_GROUPS))]
    v_groups = [v[:, gi * hpg:(gi + 1) * hpg] for gi in range(len(DIL_GROUPS))]
    qb = q.reshape(b, h, nb, Q_BLOCK, dh).transpose(2, 0, 1, 3, 4)

    def block(args):
        qi, bi = args
        t = bi * Q_BLOCK + jnp.arange(Q_BLOCK)
        outs, lses = [], []
        for gi, (window, dil) in enumerate(DIL_GROUPS):
            side = window // dil // 2
            pos = t[:, None] + dil * jnp.arange(-side, side + 1)[None, :]
            valid = (pos >= 0) & (pos < s)
            pos = jnp.clip(pos, 0, s - 1)
            kgat = k_groups[gi][:, :, pos]
            vgat = v_groups[gi][:, :, pos]
            qg = qi[:, gi * hpg:(gi + 1) * hpg].astype(jnp.float32)
            sc = jnp.einsum('bhqd,bhqnd->bhqn', qg, kgat) * scale
            sc = jnp.where(valid, sc, NEG_INF)
            lse = jax.nn.logsumexp(sc, axis=-1)
            p = jnp.exp(sc - lse[..., None]).astype(v.dtype)
            outs.append(jnp.einsum('bhqn,bhqnd->bhqd', p, vgat).astype(jnp.float32))
            lses.append(lse)
        w = jax.nn.softmax(jnp.stack(lses), axis=0)
        o = jnp.sum(w[..., None] * jnp.stack(outs), axis=0)
        return o.astype(v.dtype)

    o = lax.map(block, (qb, jnp.arange(nb)))
    return o.transpose(1, 2, 0, 3, 4).reshape(b, hpg, s, dh)

def swiglu(h, w_gu, w_down):
    gu = h @ w_gu
    g, u = jnp.split(gu, 2, axis=-1)
    return (jax.nn.silu(g) * u) @ w_down

def moe_swiglu(h, w_router, w_gu, w_down):
    b, s, d = h.shape
    ht = h.reshape(b * s, d)
    logits = (ht @ w_router).astype(jnp.float32)
    top_val, top_idx = lax.top_k(logits, TOP_K)
    top_w = jax.nn.softmax(top_val, axis=-1)
    gates = jnp.sum(jax.nn.one_hot(top_idx, N_EXPERTS, dtype=jnp.float32) * top_w[..., None], axis=1)
    gates = gates.astype(h.dtype)
    out = jnp.zeros_like(ht)
    for e in range(N_EXPERTS):
        out = out + gates[:, e:e + 1] * swiglu(ht, w_gu[e], w_down[e])
    return out.reshape(b, s, d)

def setup_inputs(seed: int = 0) -> dict:
    key = jax.random.key(seed)
    ks = jax.random.split(key, 12)
    n_dense = (DEPTH + 1) // 2
    n_moe = DEPTH // 2
    f32 = jnp.float32
    nrm = jax.random.normal
    x = nrm(ks[0], (BATCH, SEQ, D_MODEL), f32)
    norm_gains = 1.0 + 0.1 * nrm(ks[1], (DEPTH, 2, D_MODEL), f32)
    w_in = nrm(ks[2], (DEPTH, D_MODEL, IN_W), f32) * D_MODEL ** -0.5
    qk_gains = 1.0 + 0.1 * nrm(ks[3], (DEPTH, 3, 2, HEAD_DIM), f32)
    na_rpb = 0.1 * nrm(ks[4], (DEPTH, NA_HEADS, 2 * NA_WIN_ROWS - 1, 2 * NA_WIN_COLS - 1), f32)
    branch_scale = jnp.concatenate([
        jnp.full((BR_A,), BR_A ** -0.5, f32),
        jnp.full((BR_B,), BR_B ** -0.5, f32),
        jnp.full((BR_C,), BR_C ** -0.5, f32)])
    w_branch = nrm(ks[5], (DEPTH, BRANCH_W, D_MODEL), f32) * branch_scale[None, :, None]
    w_out = nrm(ks[6], (DEPTH, D_MODEL, D_MODEL), f32) * D_MODEL ** -0.5
    ffn_w_gu = nrm(ks[7], (n_dense, D_MODEL, 2 * FFN_DIM), f32) * D_MODEL ** -0.5
    ffn_w_down = nrm(ks[8], (n_dense, FFN_DIM, D_MODEL), f32) * FFN_DIM ** -0.5
    moe_router = nrm(ks[9], (n_moe, D_MODEL, N_EXPERTS), f32) * D_MODEL ** -0.5
    moe_w_gu = nrm(ks[10], (n_moe, N_EXPERTS, D_MODEL, 2 * EXPERT_DIM), f32) * D_MODEL ** -0.5
    moe_w_down = nrm(ks[11], (n_moe, N_EXPERTS, EXPERT_DIM, D_MODEL), f32) * EXPERT_DIM ** -0.5
    return {'x': x, 'norm_gains': norm_gains, 'w_in': w_in, 'qk_gains': qk_gains,
            'na_rpb': na_rpb, 'w_branch': w_branch, 'w_out': w_out,
            'ffn_w_gu': ffn_w_gu, 'ffn_w_down': ffn_w_down, 'moe_router': moe_router,
            'moe_w_gu': moe_w_gu, 'moe_w_down': moe_w_down}

def reference(x, norm_gains, w_in, qk_gains, na_rpb, w_branch, w_out,
              ffn_w_gu, ffn_w_down, moe_router, moe_w_gu, moe_w_down):
    b, s, d = x.shape
    pos = jnp.arange(s)
    ang_1d = rope_angles(pos, HEAD_DIM)
    ang_row = rope_angles(pos // GRID_W, HEAD_DIM // 2)
    ang_col = rope_angles(pos % GRID_W, HEAD_DIM // 2)
    for layer in range(DEPTH):
        h = rms_norm(x, norm_gains[layer, 0])
        proj = h @ w_in[layer]
        q_all = proj[..., :Q_W]
        k_all = proj[..., Q_W:Q_W + KV_W]
        v_all = proj[..., Q_W + KV_W:Q_W + 2 * KV_W]
        gate = proj[..., Q_W + 2 * KV_W:]
        qk = qk_gains[layer]
        qa = rms_norm(to_heads(q_all[..., :QA_W], NA_HEADS), qk[0, 0])
        ka = rms_norm(to_heads(k_all[..., :KA_W], NA_HEADS), qk[0, 1])
        va = to_heads(v_all[..., :KA_W], NA_HEADS)
        oa = neighbourhood_attention(qa, ka, va, na_rpb[layer])
        qb = axial_rope(rms_norm(to_heads(q_all[..., QA_W:QA_W + QB_W], GQA_Q_HEADS), qk[1, 0]), ang_row, ang_col)
        kb = axial_rope(rms_norm(to_heads(k_all[..., KA_W:KA_W + KB_W], GQA_KV_HEADS), qk[1, 1]), ang_row, ang_col)
        vb = to_heads(v_all[..., KA_W:KA_W + KB_W], GQA_KV_HEADS)
        ob = gqa_attention(qb, kb, vb)
        qc = apply_rope(rms_norm(to_heads(q_all[..., QA_W + QB_W:], DIL_HEADS), qk[2, 0]), ang_1d)
        kc = apply_rope(rms_norm(to_heads(k_all[..., KA_W + KB_W:], DIL_HEADS), qk[2, 1]), ang_1d)
        vc = to_heads(v_all[..., KA_W + KB_W:], DIL_HEADS)
        oc = dilated_attention(qc, kc, vc)
        wb = w_branch[layer]
        ya = from_heads(oa) @ wb[:BR_A]
        yb = from_heads(ob) @ wb[BR_A:BR_A + BR_B]
        yc = from_heads(oc) @ wb[BR_A + BR_B:]
        gt = jax.nn.sigmoid(gate.astype(jnp.float32)).astype(x.dtype).reshape(b, s, N_BRANCHES, d)
        merged = gt[:, :, 0] * ya + gt[:, :, 1] * yb + gt[:, :, 2] * yc
        x = x + merged @ w_out[layer]
        h2 = rms_norm(x, norm_gains[layer, 1])
        if layer % 2 == 0:
            x = x + swiglu(h2, ffn_w_gu[layer // 2], ffn_w_down[layer // 2])
        else:
            i = layer // 2
            x = x + moe_swiglu(h2, moe_router[i], moe_w_gu[i], moe_w_down[i])
    return x


_drawn_inputs = setup_inputs


def setup_inputs(seed=0):
    import zlib

    import numpy as np

    out = dict(_drawn_inputs(seed))
    spreads = {}
    factors = {}
    for name, (base, spread) in spreads.items():
        noise = np.random.default_rng([zlib.crc32(name.encode()), seed]).standard_normal(out[name].shape)
        drawn = base * np.exp(spread * noise) if base else spread * noise
        out[name] = __import__('jax').numpy.asarray(drawn.astype(out[name].dtype))
    for name, factor in factors.items():
        out[name] = (out[name] * factor).astype(out[name].dtype)
    return out
```

```python
from contextlib import ExitStack

import numpy as np

import concourse.bass as bass
from concourse import mybir

F32 = mybir.dt.float32
I32 = mybir.dt.int32
ALU = mybir.AluOpType
ACT = mybir.ActivationFunctionType
AX_X = mybir.AxisListType.X

P = 128
SEQ, D_MODEL, DEPTH = 256, 1024, 2
BLOCKS = SEQ // P
DC = D_MODEL // P
HEAD = 64
GRID_W = 64
GRID_ROWS = SEQ // GRID_W
EPS = 1e-6
SCALE = HEAD ** -0.5
NEG = -1e30
NA_HEADS, NA_WIN_ROWS, NA_WIN_COLS = 4, 8, 16
RPB_ROWS, RPB_COLS = 2 * NA_WIN_ROWS - 1, 2 * NA_WIN_COLS - 1
GQA_Q, GQA_KV = 6, 2
GQA_REP = GQA_Q // GQA_KV
DIL_GROUPS = ((128, 1), (512, 4), (2048, 16))
DIL_PER_GROUP = 2
DIL_HEADS = len(DIL_GROUPS) * DIL_PER_GROUP
Q_HEADS = NA_HEADS + GQA_Q + DIL_HEADS
K_HEADS = NA_HEADS + GQA_KV + DIL_HEADS
QK_HEADS = Q_HEADS + K_HEADS
Q_W, KV_W = Q_HEADS * HEAD, K_HEADS * HEAD
QK_W = Q_W + KV_W
QKV_W = Q_W + 2 * KV_W
GATE_W = 3 * D_MODEL
BRANCH_W = (NA_HEADS + GQA_Q + DIL_PER_GROUP) * HEAD
OC = BRANCH_W // P
FFN = 2816
EXPERTS, EXPERT_DIM = 8, 3584
SLOTS = 96
ROUNDS = -(-SEQ // SLOTS)

TILE = 4096
COLS = 512
QKV_TILES = QKV_W // COLS
GATE_TILES = GATE_W // COLS
ATTN_TILES = QKV_TILES + GATE_TILES + 2 + 2
FFN_COLS = 256
FFN_STEPS = FFN // FFN_COLS
FFN_TILES = 2 * FFN_STEPS
DENSE_TILES = DEPTH * ATTN_TILES + FFN_TILES
DENSE_RING = 5
MOE_RING = 7
FBLOCKS = EXPERT_DIM // COLS
MOE_TILES = 3 * FBLOCKS
JB = COLS // P

C_IDENT = 0
C_TRI = C_IDENT + P
C_ONES = C_TRI + P
C_IOTA = C_ONES + P
C_IOTA8 = C_IOTA + SLOTS
C_BAND = C_IOTA8 + EXPERTS
C_MOD4 = C_BAND + BLOCKS * SEQ
C_MOD16 = C_MOD4 + 4
C_COLM = C_MOD16 + 16
C_ROPE = C_COLM + GRID_W
C_END = C_ROPE + 2 * 2 * BLOCKS * HEAD


def softmax_units():
    v0 = QK_W
    units = []
    for c in range(DIL_PER_GROUP):
        tiles = [((NA_HEADS + GQA_Q) // 2 + g, Q_HEADS // 2 + (NA_HEADS + GQA_KV) // 2 + g, c)
                 for g in range(len(DIL_GROUPS))]
        vcols = [v0 + (NA_HEADS + GQA_KV + g * DIL_PER_GROUP + c) * HEAD for g in range(len(DIL_GROUPS))]
        units.append((tiles, vcols, (NA_HEADS + GQA_Q + c) * HEAD, "C"))
    for h in range(NA_HEADS):
        units.append(([(h // 2, Q_HEADS // 2 + h // 2, h % 2)], [v0 + h * HEAD], h * HEAD, f"A{h}"))
    for j in range(GQA_REP):
        for kv in range(GQA_KV):
            units.append(([(NA_HEADS // 2 + j, (Q_HEADS + NA_HEADS) // 2, kv)],
                          [v0 + (NA_HEADS + kv) * HEAD],
                          (NA_HEADS + kv * GQA_REP + j) * HEAD, "B"))
    return units


UNITS = softmax_units()
NU = len(UNITS)
SCORE_TILES = [(u, g) for u, unit in enumerate(UNITS) for g in range(len(unit[0]))]
NS = len(SCORE_TILES)
MASKED_TILES = [i for i, (u, g) in enumerate(SCORE_TILES) if UNITS[u][3] != "B"]
GATE_PAIRS = GATE_W // (2 * P)
EARLY_PAIRS = 2


def dense_tiles():
    tiles = []
    for layer in range(DEPTH):
        tiles += [("in", layer, n) for n in range(QKV_TILES + GATE_TILES)]
        tiles += [("branch", layer, n) for n in range(2)]
        tiles += [("out", layer, n) for n in range(2)]
        if layer % 2 == 0:
            for s in range(FFN_STEPS):
                tiles.append(("gate_up", layer // 2, s))
                if s:
                    tiles.append(("down", layer // 2, s - 1))
            tiles.append(("down", layer // 2, FFN_STEPS - 1))
    return tiles


def moe_tiles():
    tiles = []
    for f in range(FBLOCKS):
        tiles += [("g", f), ("u", f)]
        if f:
            tiles.append(("d", f - 1))
    return tiles + [("d", FBLOCKS - 1)]


def build(nc, x_in, norm_gains, w_in, qk_gains, na_rpb, w_branch, w_out, ffn_w_gu, ffn_w_down,
          moe_router, moe_w_gu, moe_w_down, constants, out):
    dense, moe = dense_tiles(), moe_tiles()
    assert len(dense) == DENSE_TILES and len(moe) == MOE_TILES and MOE_TILES % MOE_RING == 0
    slot_order = [(DENSE_TILES + j) % DENSE_RING for j in range(DENSE_RING)] + list(range(DENSE_RING, MOE_RING))
    dense_loads, slot_loads = [], [0] * MOE_RING
    for n, (kind, _, _) in enumerate(dense):
        slot_loads[n % DENSE_RING] += 2 if kind == "gate_up" else 1
        dense_loads.append(slot_loads[n % DENSE_RING])

    with ExitStack() as ctx:
        def sb(name, cols, dt=F32):
            return ctx.enter_context(nc.sbuf_tensor(name, [P, cols], dt))

        def sem(name):
            return ctx.enter_context(nc.semaphore(name))

        bank = [ctx.enter_context(nc.psum_tensor(f"bank{i}", [P, 512], F32)) for i in range(8)]

        ring = sb("ring", DENSE_RING * TILE)
        attention_area = sb("attention_area", BLOCKS * QKV_W + 3 * DC * SEQ)
        x_sb = sb("x_sb", BLOCKS * D_MODEL)
        h_sb = sb("h_sb", BLOCKS * D_MODEL)
        hT_sb = sb("hT_sb", DC * SEQ)
        qkT_area = sb("qkT_area", QK_HEADS // 2 * SEQ)
        bias_sb = sb("bias_sb", BLOCKS * NA_HEADS * SEQ)
        cst = sb("cst", C_END)
        score_area = sb("score_area", BLOCKS * 3 * SEQ)
        prob_area = sb("prob_area", BLOCKS * 3 * SEQ)
        probT_area = sb("probT_area", 6 * SEQ)
        rope_tab = sb("rope_tab", 4 * 2 * BLOCKS * HEAD)
        qk_gain = sb("qk_gain", 6 * HEAD)
        gain_rows = sb("gain_rows", P)
        gainT = sb("gainT", 2 * DEPTH * DC)
        router_sb = sb("router_sb", DC * EXPERTS)
        neg_half = sb("neg_half", BLOCKS * QK_HEADS)
        sumsq = sb("sumsq", BLOCKS)
        rstd = sb("rstd", BLOCKS)
        head_ss = sb("head_ss", BLOCKS * QK_HEADS)
        head_rstd = sb("head_rstd", BLOCKS * QK_HEADS)
        neg_max = sb("neg_max", NU * BLOCKS)
        exp_sum = sb("exp_sum", NU * BLOCKS)
        exp_rsum = sb("exp_rsum", NU * BLOCKS)
        route = sb("route", 12 * BLOCKS * EXPERTS)
        pick = sb("pick", 16 * BLOCKS)
        most = sb("most", 1, I32)

        slot = [ring[:, s * TILE:(s + 1) * TILE] for s in range(DENSE_RING)]
        slot += [attention_area[:, i * TILE:(i + 1) * TILE] for i in range(MOE_RING - DENSE_RING)]
        qkv = attention_area[:, 0:BLOCKS * QKV_W].rearrange("p (b n) -> p b n", b=BLOCKS)
        gatesT = attention_area[:, BLOCKS * QKV_W:].rearrange("p (i t) -> p i t", t=SEQ)
        x = x_sb[:, :].rearrange("p (b n) -> p b n", b=BLOCKS)
        h = h_sb[:, :].rearrange("p (b n) -> p b n", b=BLOCKS)
        o = h
        hT = hT_sb[:, :].rearrange("p (c t) -> p c t", c=DC)
        mergedT = hT
        qkT = qkT_area[:, :].rearrange("p (c t) -> p c t", t=SEQ)
        oT = qkT
        bias = bias_sb[:, :].rearrange("p (b h k) -> p b h k", b=BLOCKS, h=NA_HEADS)
        square = [score_area[:, i * COLS:(i + 1) * COLS] for i in range(2)]
        gate_y = [a[:, 0:2 * SEQ].rearrange("p (b t) -> p b t", b=2) for a in (score_area, prob_area)]
        gate_yc = [a[:, 2 * SEQ:3 * SEQ] for a in (score_area, prob_area)]
        gate_yab = [a[:, 3 * SEQ:4 * SEQ] for a in (score_area, prob_area)]
        rope_a, rope_b = prob_area[:, :], probT_area[:, :]
        probT = probT_area[:, :].rearrange("p (c t) -> p c t", t=SEQ)
        tab = rope_tab[:, :].rearrange("p (k s b d) -> p k s b d", k=4, s=2, b=BLOCKS)
        qkg = qk_gain[:, :].rearrange("p (a b d) -> p a b d", a=3, b=2)
        gains = gainT[:, :].rearrange("p (k c) -> p k c", c=DC)
        router = router_sb[:, :].rearrange("p (c e) -> p c e", c=DC)
        ss = head_ss[:, :].rearrange("p (b h) -> p b h", b=BLOCKS)
        hr = head_rstd[:, :].rearrange("p (b h) -> p b h", b=BLOCKS)
        nmax = neg_max[:, :].rearrange("p (u b) -> p u b", b=BLOCKS)
        esum = exp_sum[:, :].rearrange("p (u b) -> p u b", b=BLOCKS)
        rsum = exp_rsum[:, :].rearrange("p (u b) -> p u b", b=BLOCKS)
        ident = cst[:, C_IDENT:C_IDENT + P]
        tri = cst[:, C_TRI:C_TRI + P]
        ones = cst[:, C_ONES:C_ONES + P]
        iota = cst[:, C_IOTA:C_IOTA + SLOTS]
        iota8 = cst[:, C_IOTA8:C_IOTA8 + EXPERTS]
        band = cst[:, C_BAND:C_MOD4].rearrange("p (b k) -> p b k", b=BLOCKS)
        mod4 = cst[:, C_MOD4:C_MOD16]
        mod16 = cst[:, C_MOD16:C_COLM]
        colmask = cst[:, C_COLM:C_ROPE]
        rope_cs = cst[:, C_ROPE:C_END].rearrange("p (r s b d) -> p r s b d", r=2, s=2, b=BLOCKS)
        ffn_actT = score_area[:, 0:2 * 2 * SEQ].rearrange("p (s j t) -> p s j t", s=2, j=2)
        ffn_silu = score_area[:, 4 * SEQ:6 * SEQ].rearrange("p (i t) -> p i t", i=2)
        at = [0]

        def cut(area, n):
            at[0] += n
            assert at[0] <= area.shape[1]
            return area[:, at[0] - n:at[0]]

        pickedT = cut(qkT_area, DC * SLOTS).rearrange("p (c t) -> p c t", c=DC)
        yT = cut(qkT_area, DC * SLOTS).rearrange("p (c t) -> p c t", c=DC)
        y_sb = cut(qkT_area, D_MODEL)
        actT = cut(qkT_area, 2 * JB * SLOTS).rearrange("p (f j t) -> p f j t", f=2, j=JB)
        at = [0]
        moe_silu = cut(score_area, 2 * SLOTS).rearrange("p (i t) -> p i t", i=2)
        choose = cut(score_area, BLOCKS * SLOTS).rearrange("p (b t) -> p b t", b=BLOCKS)
        weigh = cut(score_area, BLOCKS * SLOTS).rearrange("p (b t) -> p b t", b=BLOCKS)
        weighT = cut(score_area, SEQ)
        rank_e = cut(score_area, BLOCKS)
        gate_e = cut(score_area, BLOCKS)

        def route_tile(i):
            return route[:, i * BLOCKS * EXPERTS:(i + 1) * BLOCKS * EXPERTS].rearrange("p (b e) -> p b e", b=BLOCKS)

        def pick_tile(i):
            return pick[:, i * BLOCKS:(i + 1) * BLOCKS]

        x_loaded, cst_loaded, gains_loaded = sem("x_loaded"), sem("cst_loaded"), sem("gains_loaded")
        router_loaded = sem("router_loaded")
        qk_gain_loaded, bias_loaded = sem("qk_gain_loaded"), sem("bias_loaded")
        slot_landed = [sem(f"slot{i}_landed") for i in range(MOE_RING)]
        out_half = sem("out_half")
        gainT_done, gainT_ready = sem("gainT_done"), sem("gainT_ready")
        half_ready = sem("half_ready")
        sumsq_done, norm_var, rstd_ready = sem("sumsq_done"), sem("norm_var"), sem("rstd_ready")
        h_ready, xT_done, hT_ready = sem("h_ready"), sem("xT_done"), sem("hT_ready")
        qkv_done, square_done, ss_done, qkv_copied = sem("qkv_done"), sem("square_done"), sem("ss_done"), sem("qkv_copied")
        head_var, head_rstd_ready = sem("head_var"), sem("head_rstd_ready")
        tab_ready, bias_ready = sem("tab_ready"), sem("bias_ready")
        qk_ready = sem("qk_ready")
        qkT_done, qkT_ready = sem("qkT_done"), sem("qkT_ready")
        gate_done, gate_copied = sem("gate_done"), sem("gate_copied")
        score_done, score_masked = sem("score_done"), sem("score_masked")
        max_ready, exp_done = sem("max_ready"), sem("exp_done")
        probT_done, probT_ready = sem("probT_done"), sem("probT_ready")
        pv_done, rsum_ready, o_ready = sem("pv_done"), sem("rsum_ready"), sem("o_ready")
        oT_done, oT_ready = sem("oT_done"), sem("oT_ready")
        sigmoid_done, y_done, y_read, merged_ready = sem("sigmoid_done"), sem("y_done"), sem("y_read"), sem("merged_ready")
        residual_done, x_ready = sem("residual_done"), sem("x_ready")
        ffn_gu_done, ffn_silu_done, ffn_act_ready, ffn_down_done = (
            sem("ffn_gu_done"), sem("ffn_silu_done"), sem("ffn_act_ready"), sem("ffn_down_done"))
        logits_done, gap_ready, gap_exp, sel_ready, rank_done, most_ready = (
            sem("logits_done"), sem("gap_ready"), sem("gap_exp"), sem("sel_ready"), sem("rank_done"), sem("most_ready"))
        expert_cols, choose_ready, picked_done, picked_ready = (
            sem("expert_cols"), sem("choose_ready"), sem("picked_done"), sem("picked_ready"))
        weighT_done, weighT_ready = sem("weighT_done"), sem("weighT_ready")
        gu_done, silu_done, act_ready, down_done = sem("gu_done"), sem("silu_done"), sem("act_ready"), sem("down_done")
        yT_ready, ytok_done, ytok_ready, scattered, added = (
            sem("yT_ready"), sem("ytok_done"), sem("ytok_ready"), sem("scattered"), sem("added"))
        dve_step = sem("dve_step")
        pool_step = sem("pool_step")
        expert_rank = sem("expert_rank")
        x_final, stored = sem("x_final"), sem("stored")

        block = ctx.enter_context(nc.Block())
        OVER = ROUNDS > 1

        def dense_tile_used(n):
            kind, layer, i = dense[n]
            if kind == "in" and i < QKV_TILES:
                return qkv_done, 2 * QKV_TILES * layer + 2 * (i + 1)
            if kind == "in":
                return gate_done, GATE_PAIRS * layer + 2 * (i - QKV_TILES + 1)
            if kind == "branch":
                return y_done, DC * (layer + 1)
            if kind == "out":
                return (out_half, layer + 1) if i == 0 else (residual_done, 4 * (2 * layer + 1))
            if kind == "down" and i == FFN_STEPS - 1:
                return residual_done, 4 * (2 * 2 * layer + 2)
            return (ffn_gu_done, 2 * (i + 1)) if kind == "gate_up" else (ffn_down_done, i + 1)

        def moe_tile_used(j):
            kind, f = moe[j]
            return (down_done, f + 1, FBLOCKS) if kind == "d" else (gu_done, (f + 1) * JB, FBLOCKS * JB)

        def tile_wait(eng, n):
            eng.wait_ge(slot_landed[n % DENSE_RING], 16 * dense_loads[n])

        def dense_slot(n):
            return slot[n % DENSE_RING]

        def moe_slot(j):
            return slot[slot_order[j % MOE_RING]]

        def moe_tile_wait(eng, item, j):
            s = slot_order[j % MOE_RING]
            per = MOE_TILES // MOE_RING
            eng.wait_ge(slot_landed[s], item * (16 * per) + 16 * (slot_loads[s] + j // MOE_RING + 1))

        def passes(eng, body):
            with eng.Fori(0, EXPERTS) as e:
                body(e, e)
            if OVER:
                eng.wait_ge(most_ready, 1)
                count = eng.value_load(most[0:1, 0:1], min_val=0, max_val=SEQ)
                with eng.If(count > SLOTS):
                    with eng.Fori(1, ROUNDS) as r:
                        with eng.Fori(0, EXPERTS) as e:
                            body(r * EXPERTS + e, e)

        @block.sync
        def _(sp):
            def source(kind, layer, n):
                if kind == "in":
                    return w_in[layer].rearrange("(c p) n -> p c n", p=P)[:, :, n * COLS:(n + 1) * COLS]
                if kind == "branch":
                    w = w_branch[layer].rearrange("(c p) n -> p c n", p=P)
                    return w[:, 0:4, :] if n == 0 else w[:, 4:OC, :]
                if kind == "out":
                    return w_out[layer].rearrange("(c p) n -> p c n", p=P)[:, 4 * n:4 * n + 4, :]
                if kind == "gate_up":
                    w = ffn_w_gu[layer].rearrange("(c p) (g n) -> p c g n", p=P, g=2)
                    return w[:, :, :, n * FFN_COLS:(n + 1) * FFN_COLS]
                w = ffn_w_down[layer].rearrange("(c p) n -> p c n", p=P)
                return w[:, 2 * n:2 * n + 2, :]

            for n, (kind, layer, i) in enumerate(dense):
                src = source(kind, layer, i)
                cols = int(np.prod(src.shape[1:]))
                dst = dense_slot(n)[:, 0:cols]
                if n >= DENSE_RING:
                    sp.wait_ge(*dense_tile_used(n - DENSE_RING))
                if kind == "gate_up":
                    dst = dst.rearrange("p (c g n) -> p c g n", c=DC, g=2)
                    for g in range(2):
                        sp.dma_start(dst[:, :, g, :], src[:, :, g, :]).then_inc(slot_landed[n % DENSE_RING], 16)
                else:
                    dst = dst.rearrange("p (c n) -> p c n", c=src.shape[1])
                    sp.dma_start(dst, src).then_inc(slot_landed[n % DENSE_RING], 16)

            def load_tile(j, e):
                gu = moe_w_gu[0, e].rearrange("(c p) n -> p c n", p=P)
                dn = moe_w_down[0, e].rearrange("(c p) n -> p c n", p=P)
                kind, f = moe[j]
                if kind == "d":
                    src = dn[:, f * JB:(f + 1) * JB, :]
                else:
                    col = f * COLS + (EXPERT_DIM if kind == "u" else 0)
                    src = gu[:, :, col:col + COLS]
                dst = moe_slot(j).rearrange("p (c n) -> p c n", c=src.shape[1])
                sp.dma_start(dst, src).then_inc(slot_landed[slot_order[j % MOE_RING]], 16)

            def load_first(before, e):
                for j in range(MOE_RING):
                    used, count, growth = moe_tile_used(MOE_TILES - MOE_RING + j)
                    sp.wait_ge(used, before * growth + count)
                    load_tile(j, e)

            def load_rest(item, e):
                for j in range(MOE_RING, MOE_TILES):
                    used, count, growth = moe_tile_used(j - MOE_RING)
                    sp.wait_ge(used, item * growth + count)
                    load_tile(j, e)

            def load_round(first_item):
                with sp.Fori(0, EXPERTS - 1) as e:
                    load_rest(first_item + e, e)
                    load_first(first_item + e, e + 1)
                load_rest(first_item + (EXPERTS - 1), EXPERTS - 1)

            for j in range(DENSE_RING):
                sp.wait_ge(*dense_tile_used(DENSE_TILES - DENSE_RING + j))
                load_tile(j, 0)
            sp.wait_ge(y_read, DEPTH * DC)
            for j in range(DENSE_RING, MOE_RING):
                load_tile(j, 0)
            load_round(0)
            if OVER:
                sp.wait_ge(most_ready, 1)
                count = sp.value_load(most[0:1, 0:1], min_val=0, max_val=SEQ)
                with sp.If(count > SLOTS):
                    with sp.Fori(1, ROUNDS) as r:
                        load_first(r * EXPERTS - 1, 0)
                        load_round(r * EXPERTS)
            sp.wait_ge(x_final, 1)
            sp.dma_start(out.rearrange("(b p) n -> p b n", p=P), x).then_inc(stored, 16)
            sp.wait_ge(stored, 16)

        @block.gpsimd
        def _(pool):
            steps = [0]

            def own(ins):
                steps[0] += 1
                ins.then_inc(pool_step, 1)
                pool.wait_ge(pool_step, steps[0])

            own(nc.gpsimd.memset(neg_half[:, :], -0.5))

            def load_bias(layer):
                table = na_rpb[layer, 0:1, 0, 0:1]
                for b in range(BLOCKS):
                    for half in range(P // GRID_W):
                        r = b * (P // GRID_W) + half
                        for head in range(NA_HEADS):
                            offset = (layer * NA_HEADS + head) * RPB_ROWS * RPB_COLS \
                                + (NA_WIN_ROWS - GRID_ROWS + r) * RPB_COLS + NA_WIN_COLS - GRID_W
                            src = bass.AP(table.tensor, offset,
                                          [[1, GRID_W], [RPB_COLS, GRID_ROWS], [1, GRID_W]])
                            dst = bias[half * GRID_W:(half + 1) * GRID_W, b, head, :]
                            pool.dma_start(dst.rearrange("p (r c) -> p r c", c=GRID_W), src)\
                                .then_inc(bias_loaded, 16)

            def norm_power(k):
                pool.wait_ge(sumsq_done, BLOCKS * (k + 1))
                own(nc.gpsimd.tensor_scalar(sumsq[:, :], sumsq[:, :], 1.0 / D_MODEL, EPS, ALU.mult, ALU.add))
                nc.gpsimd.tensor_tensor(rstd[:, :], sumsq[:, :], neg_half[:, 0:BLOCKS], ALU.pow).then_inc(rstd_ready, 1)

            def head_power(layer, lo, hi, pieces):
                pool.wait_ge(ss_done, 8 * layer + pieces)
                v = ss[:, :, lo:hi]
                own(nc.gpsimd.tensor_scalar(v, v, 1.0 / HEAD, EPS, ALU.mult, ALU.add))
                half = neg_half[:, 0:BLOCKS * (hi - lo)].rearrange("p (b h) -> p b h", b=BLOCKS)
                nc.gpsimd.tensor_tensor(hr[:, :, lo:hi], v, half, ALU.pow).then_inc(head_rstd_ready, 1)

            def rope_tables(layer):
                pool.wait_ge(qk_gain_loaded, 16 * (layer + 1))
                if layer == 0:
                    pool.wait_ge(cst_loaded, 16)
                else:
                    pool.wait_ge(qk_ready, 4 * layer)
                last = None
                for br in range(2):
                    groups = 2 if br == 0 else 1
                    w = HEAD // groups // 2
                    for qk in range(2):
                        kind = 2 * br + qk
                        g = qkg[:, br + 1, qk, :]
                        nc.gpsimd.tensor_tensor(tab[:, kind, 0], rope_cs[:, br, 0],
                                                g.unsqueeze(1).broadcast_to([P, BLOCKS, HEAD]), ALU.mult)
                        for half in range(2):
                            for gr in range(groups):
                                a = gr * 2 * w + half * w
                                c = gr * 2 * w + (1 - half) * w
                                last = nc.gpsimd.tensor_tensor(
                                    tab[:, kind, 1, :, a:a + w], rope_cs[:, br, 1, :, a:a + w],
                                    g[:, c:c + w].unsqueeze(1).broadcast_to([P, BLOCKS, w]), ALU.mult)
                last.then_inc(tab_ready, 1)

            def bias_mask(layer):
                pool.wait_ge(bias_loaded, 16 * BLOCKS * 2 * NA_HEADS * (layer + 1))
                v = bias_sb[:, :].rearrange("p (n c) -> p n c", c=GRID_W)
                nc.gpsimd.tensor_tensor(v, v, colmask.unsqueeze(1).broadcast_to([P, v.shape[1], GRID_W]),
                                        ALU.add).then_inc(bias_ready, 1)

            load_bias(0)
            for layer in range(DEPTH):
                norm_power(2 * layer)
                rope_tables(layer)
                bias_mask(layer)
                head_power(layer, 0, Q_HEADS, 4)
                head_power(layer, Q_HEADS, QK_HEADS, 8)
                if layer + 1 < DEPTH:
                    pool.wait_ge(score_masked, len(MASKED_TILES) * (layer + 1))
                    load_bias(layer + 1)
                norm_power(2 * layer + 1)

        @block.scalar
        def _(act):
            act.dma_start(x, x_in.rearrange("(b p) n -> p b n", p=P)).then_inc(x_loaded, 16)
            act.dma_start(gain_rows[0:2 * DEPTH * DC, :], norm_gains.rearrange("l k (c p) -> (l k c) p", p=P))\
                .then_inc(gains_loaded, 16)
            act.dma_start(cst[:, :], constants).then_inc(cst_loaded, 16)
            for_gain = qk_gains.rearrange("l a b d -> l (a b d)")
            act.dma_start(qk_gain[:, :], for_gain[0].partition_broadcast(P)).then_inc(qk_gain_loaded, 16)
            act.dma_start(router, moe_router[0].rearrange("(c p) e -> p c e", p=P)).then_inc(router_loaded, 16)

            def norm_squares(k):
                if k == 0:
                    act.wait_ge(x_loaded, 16)
                for b in range(BLOCKS):
                    if k:
                        act.wait_ge(x_ready, 4 * (k - 1) + 2 * (b + 1))
                        act.wait_ge(rstd_ready, k)
                    nc.scalar.activation(h[:, b, :], x[:, b, :], ACT.Square,
                                         accum_out=sumsq[:, b:b + 1]).then_inc(sumsq_done, 1)

            def qkv_out(layer):
                for i in range(2 * QKV_TILES):
                    n, b = i // 2, i % 2
                    act.wait_ge(qkv_done, 2 * QKV_TILES * layer + i + 1)
                    width = min(COLS, max(0, QK_W - n * COLS))
                    if width:
                        k = 8 * layer + i
                        if k >= 2:
                            act.wait_ge(ss_done, k - 1)
                        nc.scalar.activation(square[i % 2][:, 0:width], bank[i % 4][:, 0:width],
                                             ACT.Square).then_inc(square_done, 1)
                    nc.scalar.copy(qkv[:, b, n * COLS:(n + 1) * COLS], bank[i % 4][:, :]).then_inc(qkv_copied, 1)

            def gate_out(layer, p):
                act.wait_ge(gate_done, GATE_PAIRS * layer + p + 1)
                nc.scalar.copy(gatesT[:, 2 * p:2 * p + 2, :].rearrange("p i t -> p (i t)"),
                               bank[4 + p % 2][:, :]).then_inc(gate_copied, 1)

            def exponents(layer, u):
                tiles, _, _, kind = UNITS[u]
                act.wait_ge(max_ready, NU * layer + u + 1)
                n = len(tiles) * SEQ
                for b in range(BLOCKS):
                    if kind == "B":
                        s = next(i for i, t in enumerate(SCORE_TILES) if t == (u, 0))
                        src, scale = bank[s % 3][:, b * SEQ:(b + 1) * SEQ], SCALE
                    else:
                        src, scale = score_area[:, b * n:(b + 1) * n], 1.0
                    last = nc.scalar.activation(prob_area[:, b * n:(b + 1) * n], src, ACT.Exp,
                                                bias=nmax[:, u, b:b + 1], scale=scale,
                                                accum_out=esum[:, u, b:b + 1])
                last.then_inc(exp_done, 1)

            def probT_out(layer, u):
                for g in range(len(UNITS[u][0])):
                    s = SCORE_TILES.index((u, g))
                    act.wait_ge(probT_done, NS * layer + s + 1)
                    if g == 0 and NU * layer + u:
                        act.wait_ge(pv_done, NU * layer + u)
                    nc.scalar.copy(probT[:, 2 * g:2 * g + 2, :].rearrange("p c t -> p (c t)"),
                                   bank[6 + s % 2][:, :]).then_inc(probT_ready, 1)

            def sigmoid(layer, m):
                v = gatesT[:, m:3 * DC:DC, :]
                nc.scalar.activation(v, v, ACT.Sigmoid).then_inc(sigmoid_done, 1)

            for layer in range(DEPTH):
                norm_squares(2 * layer)
                qkv_out(layer)
                if layer + 1 < DEPTH:
                    act.wait_ge(tab_ready, layer + 1)
                    act.wait_ge(qk_ready, 4 * (layer + 1))
                    act.dma_start(qk_gain[:, :], for_gain[layer + 1].partition_broadcast(P))\
                        .then_inc(qk_gain_loaded, 16)
                for p in range(EARLY_PAIRS):
                    gate_out(layer, p)
                for u in range(NU + 1):
                    if u:
                        probT_out(layer, u - 1)
                    if u < NU:
                        exponents(layer, u)
                    if EARLY_PAIRS + u < GATE_PAIRS:
                        gate_out(layer, EARLY_PAIRS + u)
                act.wait_ge(gate_copied, GATE_PAIRS * (layer + 1))
                for m in range(2):
                    sigmoid(layer, m)
                for g in range(OC // 2):
                    act.wait_ge(oT_done, OC // 2 * layer + g + 1)
                    nc.scalar.copy(oT[:, 2 * g:2 * g + 2, :].rearrange("p c t -> p (c t)"),
                                   bank[6 + g % 2][:, :]).then_inc(oT_ready, 1)
                for m in range(2, DC):
                    sigmoid(layer, m)
                norm_squares(2 * layer + 1)
                if layer % 2 == 0:
                    for i in range(2 * FFN_STEPS):
                        act.wait_ge(ffn_gu_done, i + 1)
                        if i >= 2:
                            act.wait_ge(ffn_act_ready, i - 1)
                        nc.scalar.activation(ffn_silu[:, i % 2, :], bank[4 + i % 4][:, 0:SEQ],
                                             ACT.Silu).then_inc(ffn_silu_done, 1)

            act.wait_ge(gap_ready, 1)
            nc.scalar.activation(pick_tile(5), pick_tile(4), ACT.Exp).then_inc(gap_exp, 1)

            def expert(item, e):
                for i in range(FBLOCKS * JB):
                    act.wait_ge(gu_done, item * (FBLOCKS * JB) + i + 1)
                    if i >= 2:
                        act.wait_ge(act_ready, item * (FBLOCKS * JB) + i - 1)
                    nc.scalar.activation(moe_silu[:, i % 2, :], bank[2 + i % 2][:, 0:SLOTS],
                                         ACT.Silu).then_inc(silu_done, 1)
                for g in range(2):
                    act.wait_ge(ytok_done, item * 2 + g + 1)
                    nc.scalar.copy(y_sb[0:SLOTS, g * 512:(g + 1) * 512], bank[4 + g][0:SLOTS, :]).then_inc(ytok_ready, 1)

            passes(act, expert)

        @block.vector
        def _(dve):
            steps = [0]

            def own(ins):
                steps[0] += 1
                ins.then_inc(dve_step, 1)
                dve.wait_ge(dve_step, steps[0])

            def norm_apply(k):
                dve.wait_ge(rstd_ready, k + 1)
                for b in range(BLOCKS):
                    nc.vector.tensor_scalar(h[:, b, :], x[:, b, :], rstd[:, b:b + 1], None, ALU.mult).then_inc(h_ready, 1)
                if k == 0:
                    dve.wait_ge(gainT_done, 1)
                    own(nc.vector.tensor_copy(gainT[:, :], bank[0][:, 0:2 * DEPTH * DC]))
                for g in range(DC // 2):
                    dve.wait_ge(xT_done, 4 * k + g + 1)
                    nc.vector.tensor_tensor(hT[:, 2 * g:2 * g + 2, :],
                                            bank[4 + g][:, :].rearrange("p (c t) -> p c t", c=2),
                                            gains[:, k, 2 * g:2 * g + 2].unsqueeze(2).broadcast_to([P, 2, SEQ]),
                                            ALU.mult).then_inc(hT_ready, 1)

            def head_sums(layer, i):
                n, b = i // 2, i % 2
                heads = min(8, QK_HEADS - 8 * n)
                dve.wait_ge(square_done, 8 * layer + i + 1)
                nc.vector.tensor_reduce(ss[:, b, 8 * n:8 * n + heads],
                                        square[i % 2][:, 0:heads * HEAD].rearrange("p (h d) -> p h d", d=HEAD),
                                        AX_X, ALU.add).then_inc(ss_done, 1)

            def rotate(src, dst, kind, groups, b):
                heads = src.shape[1]
                w = HEAD // groups // 2
                ra = rope_a[:, 0:heads * HEAD].rearrange("p (h d) -> p h d", d=HEAD)
                rb = rope_b[:, 0:heads * HEAD].rearrange("p (h d) -> p h d", d=HEAD)
                nc.vector.tensor_tensor(ra, src, tab[:, kind, 0, b].unsqueeze(1).broadcast_to([P, heads, HEAD]), ALU.mult)
                for gr in range(groups):
                    for half in range(2):
                        a = gr * 2 * w + half * w
                        c = gr * 2 * w + (1 - half) * w
                        last = nc.vector.tensor_tensor(
                            rb[:, :, a:a + w], src[:, :, c:c + w],
                            tab[:, kind, 1, b, a:a + w].unsqueeze(1).broadcast_to([P, heads, w]), ALU.mult)
                own(last)
                if kind == 0:
                    for kv in range(GQA_KV):
                        last = nc.vector.tensor_tensor(dst[:, kv:GQA_Q:GQA_KV, :], ra[:, kv * GQA_REP:(kv + 1) * GQA_REP, :],
                                                       rb[:, kv * GQA_REP:(kv + 1) * GQA_REP, :], ALU.add)
                    return last
                return nc.vector.tensor_tensor(dst, ra, rb, ALU.add)

            def qk_norm_rope(layer, qk):
                dve.wait_ge(head_rstd_ready, 2 * layer + qk + 1)
                dve.wait_ge(qkv_copied, 2 * QKV_TILES * layer + 4 * (qk + 1))
                if qk == 0:
                    dve.wait_ge(tab_ready, layer + 1)
                lo = 0 if qk == 0 else Q_HEADS
                na, nb, ncc = NA_HEADS, (GQA_Q if qk == 0 else GQA_KV), DIL_HEADS
                for b in range(BLOCKS):
                    v = qkv[:, b, lo * HEAD:(lo + na + nb + ncc) * HEAD].rearrange("p (h d) -> p h d", d=HEAD)
                    own(nc.vector.tensor_tensor(v, v, hr[:, b, lo:lo + na + nb + ncc].unsqueeze(2)
                                                .broadcast_to([P, na + nb + ncc, HEAD]), ALU.mult))
                    nc.vector.tensor_tensor(v[:, 0:na, :], v[:, 0:na, :],
                                            qkg[:, 0, qk, :].unsqueeze(1).broadcast_to([P, na, HEAD]), ALU.mult)
                    own(rotate(v[:, na:na + nb, :], v[:, na:na + nb, :], qk, 2, b))
                    rotate(v[:, na + nb:, :], v[:, na + nb:, :], 2 + qk, 1, b).then_inc(qk_ready, 1)
                    dve.wait_ge(qk_ready, 4 * layer + 2 * qk + b + 1)

            def masked_scores(layer, u):
                tiles, _, _, kind = UNITS[u]
                n = len(tiles) * SEQ
                if kind != "B":
                    if NU * layer + u:
                        dve.wait_ge(exp_done, NU * layer + u)
                    for g in range(len(tiles)):
                        s = SCORE_TILES.index((u, g))
                        dve.wait_ge(score_done, NS * layer + s + 1)
                        src = bank[s % 3][:, :].rearrange("p (b k) -> p b k", b=BLOCKS)
                        dst = score_area[:, 0:BLOCKS * n].rearrange("p (b k) -> p b k", b=BLOCKS)[:, :, g * SEQ:(g + 1) * SEQ]
                        if kind == "C" and DIL_GROUPS[g][1] > 1:
                            dil = DIL_GROUPS[g][1]
                            m = (mod4 if dil == 4 else mod16).unsqueeze(1).broadcast_to([P, SEQ // dil, dil])
                            for b in range(BLOCKS):
                                last = nc.vector.scalar_tensor_tensor(
                                    out=dst[:, b, :].rearrange("p (n m) -> p n m", m=dil),
                                    in0=src[:, b, :].rearrange("p (n m) -> p n m", m=dil), scalar=SCALE,
                                    in1=m, op0=ALU.mult, op1=ALU.add)
                        else:
                            if kind != "C" and u == DIL_PER_GROUP:
                                dve.wait_ge(bias_ready, layer + 1)
                            m = band if kind == "C" else bias[:, :, int(kind[1]), ::-1]
                            last = nc.vector.scalar_tensor_tensor(out=dst, in0=src, scalar=SCALE, in1=m,
                                                                  op0=ALU.mult, op1=ALU.add)
                        last.then_inc(score_masked, 1)
                    dve.wait_ge(score_masked, len(MASKED_TILES) * layer + MASKED_TILES.index(s) + 1)
                    nc.vector.tensor_reduce(nmax[:, u, :], score_area[:, 0:BLOCKS * n].rearrange("p (b k) -> p b k", b=BLOCKS),
                                            AX_X, ALU.max, negate=True).then_inc(max_ready, 1)
                else:
                    s = SCORE_TILES.index((u, 0))
                    dve.wait_ge(score_done, NS * layer + s + 1)
                    own(nc.vector.tensor_reduce(nmax[:, u, :], bank[s % 3][:, :].rearrange("p (b k) -> p b k", b=BLOCKS),
                                                AX_X, ALU.max, negate=True))
                    nc.vector.tensor_scalar(nmax[:, u, :], nmax[:, u, :], SCALE, None, ALU.mult).then_inc(max_ready, 1)

            def attention_out(layer, u):
                dve.wait_ge(exp_done, NU * layer + u + 1)
                own(nc.vector.reciprocal(rsum[:, u, :], esum[:, u, :]))
                dve.wait_ge(pv_done, NU * layer + u + 1)
                col = UNITS[u][2]
                for b in range(BLOCKS):
                    last = nc.vector.tensor_scalar(o[:, b, col:col + HEAD], bank[3][:, b * HEAD:(b + 1) * HEAD],
                                                   rsum[:, u, b:b + 1], None, ALU.mult)
                last.then_inc(o_ready, 1)

            def merge(layer, m):
                k = DC * layer + m
                dve.wait_ge(y_done, k + 1)
                dve.wait_ge(sigmoid_done, k + 1)
                if m >= 2:
                    dve.wait_ge(merged_ready, k - 1)
                ab, c, s = bank[4 + 2 * (m % 2)], bank[5 + 2 * (m % 2)], m % 2
                nc.vector.tensor_tensor(gate_y[s], ab[:, :].rearrange("p (b t) -> p b t", b=2),
                                        gatesT[:, m:2 * DC:DC, :], ALU.mult)
                nc.vector.tensor_tensor(gate_yc[s], c[:, 0:SEQ], gatesT[:, 2 * DC + m, :], ALU.mult).then_inc(y_read, 1)
                dve.wait_ge(y_read, k + 1)
                own(nc.vector.tensor_tensor(gate_yab[s], gate_y[s][:, 0, :], gate_y[s][:, 1, :], ALU.add))
                nc.vector.tensor_tensor(mergedT[:, m, :], gate_yab[s], gate_yc[s], ALU.add).then_inc(merged_ready, 1)

            def add_residual(k):
                for i in range(4):
                    dve.wait_ge(residual_done, 4 * k + i + 1)
                    v = x[:, i // 2, (i % 2) * 512:(i % 2 + 1) * 512]
                    nc.vector.tensor_tensor(v, v, bank[i][:, :], ALU.add).then_inc(x_ready, 1)

            for layer in range(DEPTH):
                norm_apply(2 * layer)
                for i in range(4):
                    head_sums(layer, i)
                for i in range(4, 6):
                    head_sums(layer, i)
                qk_norm_rope(layer, 0)
                for i in range(6, 8):
                    head_sums(layer, i)
                qk_norm_rope(layer, 1)
                for g in range(QK_HEADS // 4):
                    dve.wait_ge(qkT_done, QK_HEADS // 4 * layer + g + 1)
                    nc.vector.tensor_copy(qkT[:, 2 * g:2 * g + 2, :].rearrange("p c t -> p (c t)"),
                                          bank[6 + g % 2][:, :]).then_inc(qkT_ready, 1)
                for u in range(NU + 1):
                    if u < NU:
                        masked_scores(layer, u)
                    if u:
                        attention_out(layer, u - 1)
                for m in range(DC):
                    merge(layer, m)
                add_residual(2 * layer)
                norm_apply(2 * layer + 1)
                if layer % 2 == 0:
                    for i in range(2 * FFN_STEPS):
                        dve.wait_ge(ffn_silu_done, i + 1)
                        s = i // 2
                        if s >= 2:
                            dve.wait_ge(ffn_down_done, s - 1)
                        nc.vector.tensor_tensor(ffn_actT[:, s % 2, i % 2, :], ffn_silu[:, i % 2, :],
                                                bank[4 + i % 4][:, SEQ:2 * SEQ], ALU.mult).then_inc(ffn_act_ready, 1)
                    add_residual(2 * layer + 1)

            lg, eq, cand, first, lg2, second, sel, gate, rank, gate_t, rank_t, cnt = [route_tile(i) for i in range(12)]
            v0, i0, v1, i1, gap, ex, den, w0, w1 = [pick_tile(i) for i in range(9)]

            def spread(v):
                return v.unsqueeze(2).broadcast_to([P, BLOCKS, EXPERTS])

            def greatest(logits, value, index, onehot):
                own(nc.vector.tensor_reduce(value, logits, AX_X, ALU.max))
                own(nc.vector.tensor_tensor(eq, logits, spread(value), ALU.is_ge))
                own(nc.vector.scalar_tensor_tensor(out=cand, in0=eq, scalar=-float(EXPERTS),
                                                   in1=iota8.unsqueeze(1).broadcast_to([P, BLOCKS, EXPERTS]),
                                                   op0=ALU.mult, op1=ALU.add))
                own(nc.vector.tensor_reduce(index, cand, AX_X, ALU.min))
                own(nc.vector.tensor_tensor(onehot, cand, spread(index), ALU.is_equal))

            dve.wait_ge(logits_done, 1)
            own(nc.vector.tensor_copy(lg, bank[0][:, 0:BLOCKS * EXPERTS].rearrange("p (b e) -> p b e", b=BLOCKS)))
            greatest(lg, v0, i0, first)
            own(nc.vector.scalar_tensor_tensor(out=lg2, in0=first, scalar=-3e38, in1=lg, op0=ALU.mult, op1=ALU.add))
            greatest(lg2, v1, i1, second)
            nc.vector.tensor_tensor(gap, v1, v0, ALU.subtract).then_inc(gap_ready, 1)
            nc.vector.tensor_tensor(sel, first, second, ALU.add).then_inc(sel_ready, 1)
            dve.wait_ge(gap_exp, 1)
            own(nc.vector.tensor_scalar(den, ex, 1.0, None, ALU.add))
            own(nc.vector.reciprocal(w0, den))
            own(nc.vector.tensor_tensor(w1, ex, w0, ALU.mult))
            own(nc.vector.tensor_tensor(first, first, spread(w0), ALU.mult))
            own(nc.vector.tensor_tensor(second, second, spread(w1), ALU.mult))
            own(nc.vector.tensor_tensor(gate, first, second, ALU.add))
            dve.wait_ge(rank_done, 1)
            own(nc.vector.scalar_tensor_tensor(out=rank, in0=bank[1][:, 0:BLOCKS * EXPERTS].rearrange("p (b e) -> p b e", b=BLOCKS),
                                               scalar=1000.0, in1=sel, op0=ALU.add, op1=ALU.mult))
            by_expert = lambda v: v.rearrange("p b e -> p (b e)").rearrange("p (e b) -> p e b", b=BLOCKS)
            rank_x, gate_x = by_expert(rank_t), by_expert(gate_t)
            nc.vector.tensor_copy(gate_x, gate.rearrange("p b e -> p e b"))
            own(nc.vector.tensor_scalar(rank_x, rank.rearrange("p b e -> p e b"), -1000.0, None, ALU.add))
            nc.vector.tensor_reduce(most[:, 0:1], bank[1][:, BLOCKS * EXPERTS:(BLOCKS + 1) * EXPERTS],
                                    AX_X, ALU.max).then_inc(most_ready, 1)

            def expert(item, e):
                nc.vector.tensor_copy(rank_e, rank_x[:, e, :])
                nc.vector.tensor_copy(gate_e, gate_x[:, e, :]).then_inc(expert_cols, 1)
                dve.wait_ge(expert_cols, item + 1)
                for b in range(BLOCKS):
                    nc.vector.tensor_scalar(choose[:, b, :], iota, rank_e[:, b:b + 1], None, ALU.is_equal)
                    last = nc.vector.tensor_scalar(weigh[:, b, :], iota, rank_e[:, b:b + 1], gate_e[:, b:b + 1],
                                                   ALU.is_equal, ALU.mult)
                last.then_inc(choose_ready, 1)
                for g in range(2):
                    dve.wait_ge(picked_done, item * 2 + g + 1)
                    nc.vector.tensor_tensor(pickedT[:, 4 * g:4 * g + 4, :],
                                            bank[4 + g][:, 0:4 * SLOTS].rearrange("p (c t) -> p c t", c=4),
                                            gains[:, 3, 4 * g:4 * g + 4].unsqueeze(2).broadcast_to([P, 4, SLOTS]),
                                            ALU.mult).then_inc(picked_ready, 1)
                dve.wait_ge(weighT_done, item + 1)
                nc.vector.tensor_copy(weighT[0:SLOTS, :], bank[6][0:SLOTS, 0:SEQ]).then_inc(weighT_ready, 1)
                for i in range(FBLOCKS * JB):
                    f = i // JB
                    dve.wait_ge(silu_done, item * (FBLOCKS * JB) + i + 1)
                    if i % JB == 0 and f >= 2:
                        dve.wait_ge(down_done, item * FBLOCKS + f - 1)
                    nc.vector.tensor_tensor(actT[:, f % 2, i % JB, :], moe_silu[:, i % 2, :],
                                            bank[2 + i % 2][:, SLOTS:2 * SLOTS], ALU.mult).then_inc(act_ready, 1)
                dve.wait_ge(down_done, item * FBLOCKS + FBLOCKS)
                for g in range(2):
                    nc.vector.tensor_copy(yT[:, 4 * g:4 * g + 4, :].rearrange("p c t -> p (c t)"),
                                          bank[g][:, 0:4 * SLOTS]).then_inc(yT_ready, 1)
                for i in range(4):
                    dve.wait_ge(scattered, item * 4 + i + 1)
                    v = x[:, i // 2, (i % 2) * 512:(i % 2 + 1) * 512]
                    nc.vector.tensor_tensor(v, v, bank[4 + i][:, :], ALU.add).then_inc(added, 1)

            with dve.Fori(0, EXPERTS) as e:
                expert(e, e)
            if OVER:
                count = dve.value_load(most[0:1, 0:1], min_val=0, max_val=SEQ)
                with dve.If(count > SLOTS):
                    with dve.Fori(1, ROUNDS) as r:
                        nc.vector.tensor_scalar(rank_t, rank_t, -float(SLOTS), None, ALU.add).then_inc(expert_rank, 1)
                        with dve.Fori(0, EXPERTS) as e:
                            dve.wait_ge(expert_rank, r)
                            expert(r * EXPERTS + e, e)
            dve.drain().then_inc(x_final, 1)

        @block.tensor
        def _(pe):
            tile_no = [0]

            def next_tile():
                n = tile_no[0]
                tile_no[0] += 1
                tile_wait(pe, n)
                return dense_slot(n)

            def norm_transposes(k):
                if k == 0:
                    pe.wait_ge(cst_loaded, 16)
                    pe.wait_ge(gains_loaded, 16)
                    rows = 2 * DEPTH * DC
                    nc.tensor.transpose(bank[0][:, 0:rows], gain_rows[0:rows, :], ident[0:rows, 0:rows]).then_inc(gainT_done, 1)
                for b in range(BLOCKS):
                    pe.wait_ge(h_ready, BLOCKS * k + b + 1)
                    for c in range(DC):
                        last = nc.tensor.transpose(bank[4 + c // 2][:, (c % 2) * SEQ + b * P:(c % 2) * SEQ + (b + 1) * P],
                                                   h[:, b, c * P:(c + 1) * P], ident)
                        if b == BLOCKS - 1 and c % 2:
                            last.then_inc(xT_done, 1)

            def project(out_ap, lhs, rhs, n):
                for c in range(n):
                    last = nc.tensor.matmul(out_ap, lhs(c), rhs(c), start=(c == 0), stop=(c == n - 1))
                return last

            def gate_chunk(layer, i, w):
                p = i // 2
                if i % 2 == 0 and p >= 2:
                    pe.wait_ge(gate_copied, GATE_PAIRS * layer + p - 1)
                last = project(bank[4 + p % 2][:, (i % 2) * SEQ:(i % 2 + 1) * SEQ],
                               lambda c: w[:, c, (i % 4) * P:(i % 4 + 1) * P], lambda c: hT[:, c, :], DC)
                if i % 2:
                    last.then_inc(gate_done, 1)
                return last

            def scores(layer, u):
                for g, (qc, kc, half) in enumerate(UNITS[u][0]):
                    s = SCORE_TILES.index((u, g))
                    if s >= 3:
                        pu, pg = SCORE_TILES[s - 3]
                        if UNITS[pu][3] == "B":
                            pe.wait_ge(exp_done, NU * layer + pu + 1)
                        else:
                            pe.wait_ge(score_masked, len(MASKED_TILES) * layer + MASKED_TILES.index(s - 3) + 1)
                    rows = slice(half * HEAD, (half + 1) * HEAD)
                    for b in range(BLOCKS):
                        last = nc.tensor.matmul(bank[s % 3][:, b * SEQ:(b + 1) * SEQ], qkT[rows, qc, b * P:(b + 1) * P],
                                                qkT[rows, kc, :], start=True, stop=True)
                    last.then_inc(score_done, 1)

            def prob_transposes(layer, u):
                tiles = UNITS[u][0]
                n = len(tiles) * SEQ
                pe.wait_ge(exp_done, NU * layer + u + 1)
                for g in range(len(tiles)):
                    s = SCORE_TILES.index((u, g))
                    if s >= 2:
                        pe.wait_ge(probT_ready, NS * layer + s - 1)
                    for kc in range(2):
                        for b in range(BLOCKS):
                            col = b * n + g * SEQ + kc * P
                            last = nc.tensor.transpose(bank[6 + s % 2][:, kc * SEQ + b * P:kc * SEQ + (b + 1) * P],
                                                       prob_area[:, col:col + P], ident)
                    last.then_inc(probT_done, 1)

            def values(layer, u):
                vcols = UNITS[u][1]
                pe.wait_ge(probT_ready, NS * layer + SCORE_TILES.index((u, len(vcols) - 1)) + 1)
                if NU * layer + u:
                    pe.wait_ge(o_ready, NU * layer + u)
                for b in range(BLOCKS):
                    last = project(bank[3][:, b * HEAD:(b + 1) * HEAD],
                                   lambda c: probT[:, c, b * P:(b + 1) * P],
                                   lambda c: qkv[:, c % 2, vcols[c // 2]:vcols[c // 2] + HEAD], 2 * len(vcols))
                last.then_inc(pv_done, 1)

            def attention(layer):
                for n in range(QKV_TILES):
                    w = next_tile().rearrange("p (c n) -> p c n", c=DC)
                    for b in range(BLOCKS):
                        i = 2 * n + b
                        if i >= 4:
                            pe.wait_ge(qkv_copied, 2 * QKV_TILES * layer + i - 3)
                        elif i == 0:
                            pe.wait_ge(hT_ready, 4 * (2 * layer + 1))
                        last = project(bank[i % 4][:, :], lambda c: hT[:, c, b * P:(b + 1) * P], lambda c: w[:, c, :], DC)
                        last.then_inc(qkv_done, 1)

                gate_w = [None]

                def gates(i):
                    if i % 4 == 0:
                        gate_w[0] = next_tile().rearrange("p (c n) -> p c n", c=DC)
                    gate_chunk(layer, i, gate_w[0])

                for i in range(2 * EARLY_PAIRS):
                    gates(i)
                for g in range(QK_HEADS // 4):
                    if g == 0:
                        pe.wait_ge(qk_ready, 4 * layer + 4)
                    if g >= 2:
                        pe.wait_ge(qkT_ready, QK_HEADS // 4 * layer + g - 1)
                    for c in range(2):
                        for b in range(BLOCKS):
                            last = nc.tensor.transpose(bank[6 + g % 2][:, c * SEQ + b * P:c * SEQ + (b + 1) * P],
                                                       qkv[:, b, (2 * g + c) * P:(2 * g + c + 1) * P], ident)
                    last.then_inc(qkT_done, 1)
                pe.wait_ge(qkT_ready, QK_HEADS // 4 * (layer + 1))
                pe.wait_ge(qkv_copied, 2 * QKV_TILES * (layer + 1))
                for u in range(NU + 1):
                    pair = EARLY_PAIRS + u
                    if u:
                        prob_transposes(layer, u - 1)
                    if u < NU:
                        scores(layer, u)
                    if pair < GATE_PAIRS:
                        gates(2 * pair)
                    if u:
                        values(layer, u - 1)
                    if pair < GATE_PAIRS:
                        gates(2 * pair + 1)
                pe.wait_ge(o_ready, NU * (layer + 1))
                pe.wait_ge(gate_copied, GATE_PAIRS * (layer + 1))
                for g in range(OC // 2):
                    if g >= 2:
                        pe.wait_ge(oT_ready, OC // 2 * layer + g - 1)
                    for c in range(2):
                        for b in range(BLOCKS):
                            last = nc.tensor.transpose(bank[6 + g % 2][:, c * SEQ + b * P:c * SEQ + (b + 1) * P],
                                                       o[:, b, (2 * g + c) * P:(2 * g + c + 1) * P], ident)
                    last.then_inc(oT_done, 1)
                pe.wait_ge(oT_ready, OC // 2 * (layer + 1))

                wb = [next_tile().rearrange("p (c n) -> p c n", c=4), next_tile()[:, 0:2 * D_MODEL].rearrange("p (c n) -> p c n", c=2)]
                chunks = ((0, 2), (2, 5), (5, 6))
                wo = []

                def branch(m):
                    if m >= 2:
                        pe.wait_ge(y_read, DC * layer + m - 1)
                    places = (bank[4 + 2 * (m % 2)][:, 0:SEQ], bank[4 + 2 * (m % 2)][:, SEQ:2 * SEQ],
                              bank[5 + 2 * (m % 2)][:, 0:SEQ])
                    for place, (lo, hi) in zip(places, chunks):
                        last = project(place, lambda c: wb[(lo + c) // 4][:, (lo + c) % 4, m * P:(m + 1) * P],
                                       lambda c: oT[:, lo + c, :], hi - lo)
                    last.then_inc(y_done, 1)

                for m in range(DC + 1):
                    if m < DC:
                        branch(m)
                    if m:
                        if (m - 1) % 4 == 0:
                            wo.append(next_tile().rearrange("p (c n) -> p c n", c=4))
                        pe.wait_ge(merged_ready, DC * layer + m)
                        for i in range(4):
                            last = nc.tensor.matmul(bank[i][:, :], mergedT[:, m - 1, (i // 2) * P:(i // 2 + 1) * P],
                                                    wo[-1][:, (m - 1) % 4, (i % 2) * 512:(i % 2 + 1) * 512],
                                                    start=(m == 1), stop=(m == DC))
                            if m == DC:
                                last.then_inc(residual_done, 1)
                        if m == DC // 2:
                            last.then_inc(out_half, 1)

            def dense_ffn(layer):
                gu_w = [None]

                def gate_up(s):
                    w = next_tile().rearrange("p (c g n) -> p c g n", c=DC, g=2)
                    for j in range(2):
                        i = 2 * s + j
                        if i >= 4:
                            pe.wait_ge(ffn_act_ready, i - 3)
                        for g in range(2):
                            last = project(bank[4 + i % 4][:, g * SEQ:(g + 1) * SEQ],
                                           lambda c: w[:, c, g, j * P:(j + 1) * P], lambda c: hT[:, c, :], DC)
                        last.then_inc(ffn_gu_done, 1)

                def down(s):
                    w = next_tile()[:, 0:2 * D_MODEL].rearrange("p (c n) -> p c n", c=2)
                    pe.wait_ge(ffn_act_ready, 2 * s + 2)
                    for j in range(2):
                        for i in range(4):
                            last = nc.tensor.matmul(bank[i][:, :], ffn_actT[:, s % 2, j, (i // 2) * P:(i // 2 + 1) * P],
                                                    w[:, j, (i % 2) * 512:(i % 2 + 1) * 512],
                                                    start=(s == 0 and j == 0), stop=(s == FFN_STEPS - 1 and j == 1))
                            if s == FFN_STEPS - 1 and j == 1:
                                last.then_inc(residual_done, 1)
                    if s < FFN_STEPS - 1:
                        last.then_inc(ffn_down_done, 1)

                for s in range(FFN_STEPS):
                    gate_up(s)
                    if s:
                        down(s - 1)
                down(FFN_STEPS - 1)

            for layer in range(DEPTH):
                norm_transposes(2 * layer)
                attention(layer)
                norm_transposes(2 * layer + 1)
                pe.wait_ge(hT_ready, 4 * (2 * layer + 2))
                if layer % 2 == 0:
                    dense_ffn(layer)

            pe.wait_ge(router_loaded, 16)
            for b in range(BLOCKS):
                last = project(bank[0][:, b * EXPERTS:(b + 1) * EXPERTS], lambda c: hT[:, c, b * P:(b + 1) * P],
                               lambda c: router[:, c, :], DC)
            last.then_inc(logits_done, 1)
            pe.wait_ge(sel_ready, 1)
            sel = route_tile(6)
            nc.tensor.matmul(bank[1][:, 0:EXPERTS], tri, sel[:, 0, :], start=True, stop=True)
            nc.tensor.matmul(bank[1][:, EXPERTS:2 * EXPERTS], ones, sel[:, 0, :], start=True, stop=False)
            nc.tensor.matmul(bank[1][:, EXPERTS:2 * EXPERTS], tri, sel[:, 1, :], start=False, stop=True)
            nc.tensor.matmul(bank[1][:, 2 * EXPERTS:3 * EXPERTS], ones, sel[:, 0, :], start=True, stop=False)
            nc.tensor.matmul(bank[1][:, 2 * EXPERTS:3 * EXPERTS], ones, sel[:, 1, :], start=False, stop=True).then_inc(rank_done, 1)

            def expert(item, e):
                pe.wait_ge(choose_ready, item + 1)
                for c in range(DC):
                    for b in range(BLOCKS):
                        last = nc.tensor.matmul(bank[4 + c // 4][:, (c % 4) * SLOTS:(c % 4 + 1) * SLOTS],
                                                h[:, b, c * P:(c + 1) * P], choose[:, b, :],
                                                start=(b == 0), stop=(b == BLOCKS - 1))
                    if c % 4 == 3:
                        last.then_inc(picked_done, 1)
                for b in range(BLOCKS):
                    last = nc.tensor.transpose(bank[6][0:SLOTS, b * P:(b + 1) * P], weigh[:, b, :], ident)
                last.then_inc(weighT_done, 1)
                pe.wait_ge(picked_ready, item * 2 + 2)

                def gate_up(f):
                    moe_tile_wait(pe, item, moe.index(("g", f)))
                    moe_tile_wait(pe, item, moe.index(("u", f)))
                    w = [moe_slot(moe.index((k, f))).rearrange("p (c n) -> p c n", c=DC) for k in "gu"]
                    for j in range(JB):
                        i = f * JB + j
                        if i >= 2:
                            pe.wait_ge(act_ready, item * (FBLOCKS * JB) + i - 1)
                        for g in range(2):
                            last = project(bank[2 + i % 2][:, g * SLOTS:(g + 1) * SLOTS],
                                           lambda c: w[g][:, c, j * P:(j + 1) * P], lambda c: pickedT[:, c, :], DC)
                        last.then_inc(gu_done, 1)

                def down(f):
                    moe_tile_wait(pe, item, moe.index(("d", f)))
                    w = moe_slot(moe.index(("d", f))).rearrange("p (c n) -> p c n", c=JB)
                    pe.wait_ge(act_ready, item * (FBLOCKS * JB) + (f + 1) * JB)
                    for m in range(DC):
                        for j in range(JB):
                            last = nc.tensor.matmul(bank[m // 4][:, (m % 4) * SLOTS:(m % 4 + 1) * SLOTS],
                                                    w[:, j, m * P:(m + 1) * P], actT[:, f % 2, j, :],
                                                    start=(f == 0 and j == 0 and m % 4 == 0),
                                                    stop=(f == FBLOCKS - 1 and j == JB - 1), skip_group_check=True)
                    last.then_inc(down_done, 1)

                for f in range(FBLOCKS):
                    gate_up(f)
                    if f:
                        down(f - 1)
                down(FBLOCKS - 1)

                for g in range(2):
                    pe.wait_ge(yT_ready, item * 2 + g + 1)
                    for c in range(4):
                        last = nc.tensor.transpose(bank[4 + g][0:SLOTS, c * P:(c + 1) * P], yT[:, 4 * g + c, :], ident)
                    last.then_inc(ytok_done, 1)
                pe.wait_ge(weighT_ready, item + 1)
                pe.wait_ge(ytok_ready, item * 2 + 2)
                for i in range(4):
                    nc.tensor.matmul(bank[4 + i][:, :], weighT[0:SLOTS, (i // 2) * P:(i // 2 + 1) * P],
                                     y_sb[0:SLOTS, (i % 2) * 512:(i % 2 + 1) * 512], start=True, stop=True)\
                        .then_inc(scattered, 1)

            passes(pe, expert)


def constant_table():
    t = np.zeros((P, C_END), np.float32)
    p = np.arange(P)
    t[:, C_IDENT:C_IDENT + P] = np.eye(P)
    t[:, C_TRI:C_TRI + P] = p[:, None] < p[None, :]
    t[:, C_ONES:C_ONES + P] = 1
    t[:, C_IOTA:C_IOTA + SLOTS] = np.arange(SLOTS)
    t[:, C_IOTA8:C_IOTA8 + EXPERTS] = np.arange(EXPERTS)
    k = np.arange(SEQ)
    side = DIL_GROUPS[0][0] // 2
    for b in range(BLOCKS):
        near = np.abs(k[None, :] - (b * P + p)[:, None]) <= side
        t[:, C_BAND + b * SEQ:C_BAND + (b + 1) * SEQ] = np.where(near, 0, NEG)
    t[:, C_MOD4:C_MOD16] = np.where(np.arange(4)[None, :] == (p % 4)[:, None], 0, NEG)
    t[:, C_MOD16:C_COLM] = np.where(np.arange(16)[None, :] == (p % 16)[:, None], 0, NEG)
    c, kc = (p % GRID_W)[:, None], np.arange(GRID_W)[None, :]
    start = np.clip(c - NA_WIN_COLS // 2, 0, GRID_W - NA_WIN_COLS)
    t[:, C_COLM:C_ROPE] = np.where((kc >= start) & (kc < start + NA_WIN_COLS), 0, NEG)[:, ::-1]
    rope = np.zeros((P, 2, 2, BLOCKS, HEAD), np.float32)

    def angles(pos, dim):
        freq = (np.float32(10000.0) ** (-np.arange(0, dim, 2, dtype=np.float32) / np.float32(dim))).astype(np.float32)
        return pos.astype(np.float32)[:, None] * freq[None, :]

    for b in range(BLOCKS):
        pos = b * P + p
        row, col, line = angles(pos // GRID_W, HEAD // 2), angles(pos % GRID_W, HEAD // 2), angles(pos, HEAD)
        for r, parts in enumerate(([row, row, col, col], [line, line])):
            rope[:, r, 0, b] = np.cos(np.concatenate(parts, 1))
            sign = np.concatenate([np.full(a.shape, -1.0 if i % 2 == 0 else 1.0) for i, a in enumerate(parts)], 1)
            rope[:, r, 1, b] = sign * np.sin(np.concatenate(parts, 1))
    t[:, C_ROPE:C_END] = rope.reshape(P, -1)
    return t


_INS = ["x", "norm_gains", "w_in", "qk_gains", "na_rpb", "w_branch", "w_out", "ffn_w_gu", "ffn_w_down",
        "moe_router", "moe_w_gu", "moe_w_down"]


def kernel(**inputs):
    import concourse.bacc as bacc
    from concourse.bass_utils import run_bass_kernel_spmd

    nc = bacc.Bacc("TRN2", target_bir_lowering=False, num_devices=1)
    arrays, args = {}, []
    for name in _INS:
        a = np.ascontiguousarray(inputs[name])
        if name == "x":
            a = a.reshape(SEQ, D_MODEL)
        if name == "na_rpb":
            a = np.ascontiguousarray(a[..., ::-1, ::-1])
        arrays[f"in_{name}"] = a
    arrays["in_constants"] = constant_table()
    for name, a in arrays.items():
        args.append(nc.dram_tensor(name, a.shape, mybir.dt.from_np(a.dtype), kind="ExternalInput").ap())
    out = nc.dram_tensor("out_x", (SEQ, D_MODEL), F32, kind="ExternalOutput").ap()
    build(nc, *args, out)
    r = run_bass_kernel_spmd(nc, [arrays], core_ids=[0])
    return r.results[0]["out_x"].reshape(1, SEQ, D_MODEL)
```

```python
from contextlib import ExitStack

import numpy as np

import concourse.bass as bass
from concourse import mybir

F32 = mybir.dt.float32
F32R = mybir.dt.float32r
I32 = mybir.dt.int32
ALU = mybir.AluOpType
ACT = mybir.ActivationFunctionType
AX_X = mybir.AxisListType.X

P = 128
SEQ, D_MODEL, DEPTH = 256, 1024, 2
BLOCKS = SEQ // P
DC = D_MODEL // P
HEAD = 64
GRID_W = 64
GRID_ROWS = SEQ // GRID_W
EPS = 1e-6
SCALE = HEAD ** -0.5
NEG = -1e30
NA_HEADS, NA_WIN_ROWS, NA_WIN_COLS = 4, 8, 16
RPB_ROWS, RPB_COLS = 2 * NA_WIN_ROWS - 1, 2 * NA_WIN_COLS - 1
GQA_Q, GQA_KV = 6, 2
GQA_REP = GQA_Q // GQA_KV
DIL_GROUPS = ((128, 1), (512, 4), (2048, 16))
DIL_PER_GROUP = 2
DIL_HEADS = len(DIL_GROUPS) * DIL_PER_GROUP
Q_HEADS = NA_HEADS + GQA_Q + DIL_HEADS
K_HEADS = NA_HEADS + GQA_KV + DIL_HEADS
QK_HEADS = Q_HEADS + K_HEADS
Q_W, KV_W = Q_HEADS * HEAD, K_HEADS * HEAD
QK_W = Q_W + KV_W
QKV_W = Q_W + 2 * KV_W
GATE_W = 3 * D_MODEL
BRANCH_W = (NA_HEADS + GQA_Q + DIL_PER_GROUP) * HEAD
OC = BRANCH_W // P
FFN = 2816
EXPERTS, EXPERT_DIM = 8, 3584
SLOTS = 128
ROUNDS = -(-SEQ // SLOTS)

TILE = 2048
COLS = 512
QKV_TILES = 2 * QKV_W // COLS
GATE_TILES = GATE_W // 256
BRANCH_TILES = D_MODEL // 256
OUT_TILES = DC // 2
ATTN_TILES = QKV_TILES + GATE_TILES + BRANCH_TILES + OUT_TILES
FFN_COLS = 256
FFN_STEPS = FFN // FFN_COLS
FFN_TILES = 3 * FFN_STEPS
FBLOCKS = EXPERT_DIM // COLS
JB = COLS // P
MOE_TILES = 6 * FBLOCKS
DENSE_RING = 6
MOE_RING = 14
HI_RING = 3

C_IDENT = 0
C_TRI = C_IDENT + P
C_ONES = C_TRI + P
C_IOTA = C_ONES + P
C_IOTA8 = C_IOTA + SLOTS
C_BAND = C_IOTA8 + EXPERTS
C_MOD4 = C_BAND + BLOCKS * SEQ
C_MOD16 = C_MOD4 + 4
C_COLM = C_MOD16 + 16
C_ROPE = C_COLM + GRID_W
C_END = C_ROPE + 2 * 2 * BLOCKS * HEAD


def softmax_units():
    v0 = 0
    units = []
    for c in range(DIL_PER_GROUP):
        tiles = [((NA_HEADS + GQA_Q) // 2 + g, Q_HEADS // 2 + (NA_HEADS + GQA_KV) // 2 + g, c)
                 for g in range(len(DIL_GROUPS))]
        vcols = [v0 + (NA_HEADS + GQA_KV + g * DIL_PER_GROUP + c) * HEAD for g in range(len(DIL_GROUPS))]
        units.append((tiles, vcols, (NA_HEADS + GQA_Q + c) * HEAD, "C"))
    for h in range(NA_HEADS):
        units.append(([(h // 2, Q_HEADS // 2 + h // 2, h % 2)], [v0 + h * HEAD], h * HEAD, f"A{h}"))
    for j in range(GQA_REP):
        for kv in range(GQA_KV):
            units.append(([(NA_HEADS // 2 + j, (Q_HEADS + NA_HEADS) // 2, kv)],
                          [v0 + (NA_HEADS + kv) * HEAD],
                          (NA_HEADS + kv * GQA_REP + j) * HEAD, "B"))
    return units


UNITS = softmax_units()
NU = len(UNITS)
SCORE_TILES = [(u, g) for u, unit in enumerate(UNITS) for g in range(len(unit[0]))]
NS = len(SCORE_TILES)
MASKED_TILES = [i for i, (u, g) in enumerate(SCORE_TILES) if UNITS[u][3] != "B"]
GATE_PAIRS = GATE_W // (2 * P)
EARLY_PAIRS = 2


def dense_tiles():
    tiles = []
    for layer in range(DEPTH):
        tiles += [("qkv", layer, n) for n in range(QKV_TILES)]
        tiles += [("gate", layer, n) for n in range(GATE_TILES)]
        for n in range(BRANCH_TILES):
            tiles.append(("branch", layer, n))
            if n:
                tiles.append(("out", layer, n - 1))
        tiles.append(("out", layer, OUT_TILES - 1))
        if layer % 2 == 0:
            for s in range(FFN_STEPS):
                tiles += [("g", layer // 2, s), ("u", layer // 2, s)]
                if s:
                    tiles.append(("d", layer // 2, s - 1))
            tiles.append(("d", layer // 2, FFN_STEPS - 1))
    return tiles


def moe_tiles():
    tiles = []
    for f in range(FBLOCKS):
        tiles += [("g", f, 0), ("g", f, 1), ("u", f, 0), ("u", f, 1)]
        if f:
            tiles += [("d", f - 1, 0), ("d", f - 1, 1)]
    return tiles + [("d", FBLOCKS - 1, 0), ("d", FBLOCKS - 1, 1)]


DENSE = dense_tiles()
MOE = moe_tiles()
ND = len(DENSE)
PLACE = {t: n for n, t in enumerate(DENSE)}
WIDTH = [OC * 256 if kind == "branch" else TILE for kind, _, _ in DENSE] + [TILE] * len(MOE)
MOE_PLACE = {t: j for j, t in enumerate(MOE)}


def build(nc, x_in, norm_gains, w_in, qk_gains, na_rpb, w_branch, w_out, ffn_w_gu, ffn_w_down,
          moe_router, moe_w_gu, moe_w_down, constants, out):
    assert ND % HI_RING == 0 and MOE_TILES % HI_RING == 0 and MOE_TILES % MOE_RING == 0 and MOE_TILES % 2 == 0
    slot_order = list(range(DENSE_RING, MOE_RING)) + [(ND + j) % DENSE_RING for j in range(DENSE_RING)]
    dense_loads = [len([n for n in range(ND) if n % DENSE_RING == s]) for s in range(DENSE_RING)]
    dense_loads += [0] * (MOE_RING - DENSE_RING)

    with ExitStack() as ctx:
        def sb(name, cols, dt=F32, scope=ctx):
            return scope.enter_context(nc.sbuf_tensor(name, [P, cols], dt))

        def sb_split(name, cols):
            with ExitStack() as scope:
                raw = sb(name, cols, F32, scope)
            return raw, sb(name + "_lo", cols, F32R)

        def sem(name):
            return ctx.enter_context(nc.semaphore(name))

        bank = [ctx.enter_context(nc.psum_tensor(f"bank{i}", [P, 512], F32)) for i in range(8)]

        w_hi = sb("w_hi", HI_RING * TILE, F32R)
        slots = [sb_split(f"w_slot{i}", TILE) for i in range(DENSE_RING)]
        a_hi, a_lo = sb("a_hi", DC * SEQ, F32R), sb("a_lo", DC * SEQ, F32R)
        b_hi, b_lo = sb("b_hi", DC * SEQ, F32R), sb("b_lo", DC * SEQ, F32R)
        x_sb = sb("x_sb", BLOCKS * D_MODEL)
        h_sb = sb("h_sb", BLOCKS * D_MODEL)
        cst = sb("cst", C_END)
        qk_gain = sb("qk_gain", 6 * HEAD)
        gain_rows = sb("gain_rows", P)
        gainT = sb("gainT", 2 * DEPTH * DC)
        router_sb = sb("router_sb", DC * EXPERTS)
        neg_half = sb("neg_half", BLOCKS * QK_HEADS)
        sumsq = sb("sumsq", BLOCKS)
        rstd = sb("rstd", BLOCKS)
        head_ss = sb("head_ss", BLOCKS * QK_HEADS)
        head_rstd = sb("head_rstd", BLOCKS * QK_HEADS)
        neg_max = sb("neg_max", NU * BLOCKS)
        exp_sum = sb("exp_sum", NU * BLOCKS)
        exp_rsum = sb("exp_rsum", NU * BLOCKS)
        route = sb("route", 12 * BLOCKS * EXPERTS)
        pick = sb("pick", 9 * BLOCKS)
        most = sb("most", 1, I32)
        with ExitStack() as early:
            v_area = sb("v_area", BLOCKS * KV_W, F32, early)
            gate_area = sb("gate_area", 3 * DC * SEQ, F32, early)
            qkT_area = sb("qkT_area", QK_HEADS // 2 * SEQ, F32, early)
            bias_sb = sb("bias_sb", BLOCKS * NA_HEADS * SEQ, F32, early)
            score_area = sb("score_area", BLOCKS * 3 * SEQ, F32, early)
            prob_area = sb("prob_area", BLOCKS * 3 * SEQ, F32, early)
            probT_area = sb("probT_area", 6 * SEQ, F32, early)
            rope_tab = sb("rope_tab", 4 * 2 * BLOCKS * HEAD, F32, early)
        slots += [sb_split(f"w_slot{i}", TILE) for i in range(DENSE_RING, MOE_RING)]
        moe_area = sb("moe_area", 2 * COLS + D_MODEL + 2 * BLOCKS * SLOTS + SEQ + 2 * BLOCKS)

        raw_slot = [raw[:, :] for raw, _ in slots]
        lo_slot = [lo[:, :] for _, lo in slots]
        hi_slot = [w_hi[:, s * TILE:(s + 1) * TILE] for s in range(HI_RING)]
        v_sb = v_area[:, :].rearrange("p (b n) -> p b n", b=BLOCKS)
        gatesT = gate_area[:, :].rearrange("p (i t) -> p i t", t=SEQ)
        qk_sb = gate_area[:, 3 * DC * SEQ - BLOCKS * QK_W:].rearrange("p (b n) -> p b n", b=BLOCKS)
        x = x_sb[:, :].rearrange("p (b n) -> p b n", b=BLOCKS)
        h = h_sb[:, :].rearrange("p (b n) -> p b n", b=BLOCKS)
        o = h

        def pair(hi, lo, n, inner):
            return [v[:, 0:n].rearrange("p (c t) -> p c t", t=inner) for v in (hi, lo)]

        hT = [pair(a_hi, a_lo, DC * SEQ, SEQ), pair(b_hi, b_lo, DC * SEQ, SEQ)]
        oT = pair(b_hi, b_lo, OC * SEQ, SEQ)
        mergedT = pair(a_hi, a_lo, DC * SEQ, SEQ)
        ffn_actT = [v.rearrange("p (s j) t -> p s j t", s=2) for v in pair(a_hi, a_lo, 4 * SEQ, SEQ)]
        pickedT = pair(a_hi, a_lo, DC * SLOTS, SLOTS)
        actT = [v.rearrange("p (f j) t -> p f j t", f=2) for v in pair(b_hi, b_lo, 2 * JB * SLOTS, SLOTS)]
        qkT = qkT_area[:, :].rearrange("p (c t) -> p c t", t=SEQ)
        bias = bias_sb[:, :].rearrange("p (b h k) -> p b h k", b=BLOCKS, h=NA_HEADS)
        square = [score_area[:, i * COLS:(i + 1) * COLS] for i in range(2)]
        gate_y = [a[:, 0:2 * SEQ].rearrange("p (b t) -> p b t", b=2) for a in (score_area, prob_area)]
        gate_yc = [a[:, 2 * SEQ:3 * SEQ] for a in (score_area, prob_area)]
        gate_yab = [a[:, 3 * SEQ:4 * SEQ] for a in (score_area, prob_area)]
        gate_sum = [a[:, 4 * SEQ:5 * SEQ] for a in (score_area, prob_area)]
        rope_a, rope_b = prob_area[:, :], probT_area[:, :]
        probT = probT_area[:, :].rearrange("p (c t) -> p c t", t=SEQ)
        tab = rope_tab[:, :].rearrange("p (k s b d) -> p k s b d", k=4, s=2, b=BLOCKS)
        qkg = qk_gain[:, :].rearrange("p (a b d) -> p a b d", a=3, b=2)
        gains = gainT[:, :].rearrange("p (k c) -> p k c", c=DC)
        router = router_sb[:, :].rearrange("p (c e) -> p c e", c=DC)
        ss = head_ss[:, :].rearrange("p (b h) -> p b h", b=BLOCKS)
        hr = head_rstd[:, :].rearrange("p (b h) -> p b h", b=BLOCKS)
        nmax = neg_max[:, :].rearrange("p (u b) -> p u b", b=BLOCKS)
        esum = exp_sum[:, :].rearrange("p (u b) -> p u b", b=BLOCKS)
        rsum = exp_rsum[:, :].rearrange("p (u b) -> p u b", b=BLOCKS)
        ident = cst[:, C_IDENT:C_IDENT + P]
        tri = cst[:, C_TRI:C_TRI + P]
        ones = cst[:, C_ONES:C_ONES + P]
        iota = cst[:, C_IOTA:C_IOTA + SLOTS]
        iota8 = cst[:, C_IOTA8:C_IOTA8 + EXPERTS]
        band = cst[:, C_BAND:C_MOD4].rearrange("p (b k) -> p b k", b=BLOCKS)
        mod4 = cst[:, C_MOD4:C_MOD16]
        mod16 = cst[:, C_MOD16:C_COLM]
        colmask = cst[:, C_COLM:C_ROPE]
        rope_cs = cst[:, C_ROPE:C_END].rearrange("p (r s b d) -> p r s b d", r=2, s=2, b=BLOCKS)
        ffn_act = [score_area[:, i * 512:(i + 1) * 512] for i in range(2)]
        at = [0]

        def cut(n):
            at[0] += n
            return moe_area[:, at[0] - n:at[0]]

        moe_act = [cut(COLS) for _ in range(2)]
        y_sb = cut(D_MODEL)
        picked = y_sb.rearrange("p (c t) -> p c t", t=SLOTS)
        choose = cut(BLOCKS * SLOTS).rearrange("p (b t) -> p b t", b=BLOCKS)
        weigh = cut(BLOCKS * SLOTS).rearrange("p (b t) -> p b t", b=BLOCKS)
        weighT = cut(SEQ)
        rank_e, gate_e = cut(BLOCKS), cut(BLOCKS)

        def route_tile(i):
            return route[:, i * BLOCKS * EXPERTS:(i + 1) * BLOCKS * EXPERTS].rearrange("p (b e) -> p b e", b=BLOCKS)

        def pick_tile(i):
            return pick[:, i * BLOCKS:(i + 1) * BLOCKS]

        x_loaded, cst_loaded, gains_loaded = sem("x_loaded"), sem("cst_loaded"), sem("gains_loaded")
        router_loaded = sem("router_loaded")
        qk_gain_loaded, bias_loaded = sem("qk_gain_loaded"), sem("bias_loaded")
        slot_landed = [sem(f"slot{i}_landed") for i in range(MOE_RING)]
        hi_ready = sem("hi_ready")
        lo_ready = sem("lo_ready")
        w_used = sem("w_used")
        gainT_done, gainT_ready = sem("gainT_done"), sem("gainT_ready")
        sumsq_done, rstd_ready = sem("sumsq_done"), sem("rstd_ready")
        h_ready, xT_done = sem("h_ready"), sem("xT_done")
        hT_hi_ready, hT_ready = sem("hT_hi_ready"), sem("hT_ready")
        qkv_done, square_done, ss_done, qkv_copied = sem("qkv_done"), sem("square_done"), sem("ss_done"), sem("qkv_copied")
        head_rstd_ready = sem("head_rstd_ready")
        tab_ready, bias_ready = sem("tab_ready"), sem("bias_ready")
        qk_ready = sem("qk_ready")
        qkT_done, qkT_ready = sem("qkT_done"), sem("qkT_ready")
        gate_copied = sem("gate_copied")
        score_done, score_masked = sem("score_done"), sem("score_masked")
        max_ready, exp_done = sem("max_ready"), sem("exp_done")
        probT_done, probT_ready = sem("probT_done"), sem("probT_ready")
        pv_done, rsum_ready, o_ready = sem("pv_done"), sem("rsum_ready"), sem("o_ready")
        oT_done, oT_hi_ready, oT_ready = sem("oT_done"), sem("oT_hi_ready"), sem("oT_ready")
        sigmoid_done, y_done, y_read, merged_ready = sem("sigmoid_done"), sem("y_done"), sem("y_read"), sem("merged_ready")
        residual_done, x_ready = sem("residual_done"), sem("x_ready")
        ffn_silu_done, ffn_act_ready = sem("ffn_silu_done"), sem("ffn_act_ready")
        logits_done, gap_ready, gap_exp, sel_ready, rank_done, most_ready = (
            sem("logits_done"), sem("gap_ready"), sem("gap_exp"), sem("sel_ready"), sem("rank_done"), sem("most_ready"))
        expert_cols, choose_ready, picked_done, picked_ready = (
            sem("expert_cols"), sem("choose_ready"), sem("picked_done"), sem("picked_ready"))
        picked_read, picked_hi, act_hi = sem("picked_read"), sem("picked_hi"), sem("act_hi")
        weighT_done, weighT_ready = sem("weighT_done"), sem("weighT_ready")
        silu_done, act_ready, actT_done, actT_ready = sem("silu_done"), sem("act_ready"), sem("actT_done"), sem("actT_ready")
        ytok_ready, scattered = sem("ytok_ready"), sem("scattered")
        dve_step = sem("dve_step")
        pool_step = sem("pool_step")
        expert_rank = sem("expert_rank")
        x_final, stored = sem("x_final"), sem("stored")

        block = ctx.enter_context(nc.Block())
        OVER = ROUNDS > 1

        def used(layer, kind, i):
            return PLACE[(kind, layer, i)] + 1

        def moe_used(item, j):
            return item * MOE_TILES + (ND + j + 1)

        def moe_slot(j):
            return slot_order[j % MOE_RING]

        def split_hi(act, n, landed, raw, free):
            act.wait_ge(*landed)
            if free is not None:
                act.wait_ge(w_used, free)
            nc.scalar.copy(hi_slot[n % HI_RING][:, 0:WIDTH[n]], raw[:, 0:WIDTH[n]]).then_inc(hi_ready, 1)

        def split_lo(eng, n, slot, hi_count):
            eng.wait_ge(hi_ready, hi_count)
            raw, hi, lo = [v[:, 0:WIDTH[n]] for v in (raw_slot[slot], hi_slot[n % HI_RING], lo_slot[slot])]
            eng.tensor_tensor(lo, raw, hi, ALU.subtract).then_inc(lo_ready, 1)

        class Splitter:

            def __init__(self, eng, part):
                self.eng, self.part, self.next, self.next_moe = eng, part, 0, 0

            def dense(self, upto):
                for n in range(self.next, min(upto, ND)):
                    slot = n % DENSE_RING
                    if self.part == "hi":
                        split_hi(self.eng, n, (slot_landed[slot], 16 * (n // DENSE_RING + 1)), raw_slot[slot],
                                 n - HI_RING + 1 if n >= HI_RING else None)
                    else:
                        split_lo(self.eng, n, slot, n + 1)
                    self.next = n + 1

            def moe(self, item, upto):
                for j in range(self.next_moe, min(upto, MOE_TILES)):
                    n, slot = ND + j, moe_slot(j)
                    if self.part == "hi":
                        count = item * (16 * MOE_TILES // MOE_RING) + 16 * (dense_loads[slot] + j // MOE_RING + 1)
                        split_hi(self.eng, n, (slot_landed[slot], count), raw_slot[slot],
                                 item * MOE_TILES + (n - HI_RING + 1))
                    else:
                        split_lo(self.eng, n, slot, item * MOE_TILES + (n + 1))
                    self.next_moe = j + 1
                if upto >= MOE_TILES:
                    self.next_moe = 0

        def passes(eng, body):
            with eng.Fori(0, EXPERTS) as e:
                body(e, e)
            if OVER:
                eng.wait_ge(most_ready, 1)
                count = eng.value_load(most[0:1, 0:1], min_val=0, max_val=SEQ)
                with eng.If(count > SLOTS):
                    with eng.Fori(1, ROUNDS) as r:
                        with eng.Fori(0, EXPERTS) as e:
                            body(r * EXPERTS + e, e)

        @block.sync
        def _(sp):
            def source(kind, layer, n):
                def rows(w):
                    return w.rearrange("(c p) n -> p c n", p=P)
                if kind == "qkv":
                    col = n // 2 * COLS
                    return rows(w_in[layer])[:, n % 2 * 4:n % 2 * 4 + 4, col:col + COLS]
                if kind == "gate":
                    return rows(w_in[layer])[:, :, QKV_W + n * 256:QKV_W + (n + 1) * 256]
                if kind == "branch":
                    return rows(w_branch[layer])[:, :, n * 256:(n + 1) * 256]
                if kind == "out":
                    return rows(w_out[layer])[:, 2 * n:2 * n + 2, :]
                if kind == "d":
                    return rows(ffn_w_down[layer])[:, 2 * n:2 * n + 2, :]
                col = n * FFN_COLS + (FFN if kind == "u" else 0)
                return rows(ffn_w_gu[layer])[:, :, col:col + FFN_COLS]

            for n, tile in enumerate(DENSE):
                src = source(*tile)
                dst = raw_slot[n % DENSE_RING][:, 0:int(np.prod(src.shape[1:]))]
                if n >= DENSE_RING:
                    sp.wait_ge(w_used, n - DENSE_RING + 1)
                sp.dma_start(dst.rearrange("p (c n) -> p c n", c=src.shape[1]), src)\
                    .then_inc(slot_landed[n % DENSE_RING], 16)

            def load_tile(j, e):
                kind, f, half = MOE[j]
                if kind == "d":
                    w = moe_w_down[0, e].rearrange("(c p) n -> p c n", p=P)
                    src = w[:, f * JB + 2 * half:f * JB + 2 * half + 2, :]
                else:
                    col = f * COLS + (EXPERT_DIM if kind == "u" else 0)
                    w = moe_w_gu[0, e].rearrange("(c p) n -> p c n", p=P)
                    src = w[:, 4 * half:4 * half + 4, col:col + COLS]
                slot = moe_slot(j)
                sp.dma_start(raw_slot[slot].rearrange("p (c n) -> p c n", c=src.shape[1]), src)\
                    .then_inc(slot_landed[slot], 16)

            def load_first(before, e):
                for j in range(MOE_RING):
                    sp.wait_ge(w_used, moe_used(before, MOE_TILES - MOE_RING + j))
                    load_tile(j, e)

            def load_rest(item, e):
                for j in range(MOE_RING, MOE_TILES):
                    sp.wait_ge(w_used, moe_used(item, j - MOE_RING))
                    load_tile(j, e)

            def load_round(first_item):
                with sp.Fori(0, EXPERTS - 1) as e:
                    load_rest(first_item + e, e)
                    load_first(first_item + e, e + 1)
                load_rest(first_item + (EXPERTS - 1), EXPERTS - 1)

            sp.wait_ge(merged_ready, DEPTH * DC)
            for j in range(MOE_RING - DENSE_RING):
                load_tile(j, 0)
            for j in range(DENSE_RING):
                sp.wait_ge(w_used, ND - DENSE_RING + j + 1)
                load_tile(MOE_RING - DENSE_RING + j, 0)
            load_round(0)
            if OVER:
                sp.wait_ge(most_ready, 1)
                count = sp.value_load(most[0:1, 0:1], min_val=0, max_val=SEQ)
                with sp.If(count > SLOTS):
                    with sp.Fori(1, ROUNDS) as r:
                        load_first(r * EXPERTS - 1, 0)
                        load_round(r * EXPERTS)
            sp.wait_ge(x_final, 1)
            sp.dma_start(out.rearrange("(b p) n -> p b n", p=P), x).then_inc(stored, 16)
            sp.wait_ge(stored, 16)

        @block.gpsimd
        def _(pool):
            steps = [0]

            def own(ins):
                steps[0] += 1
                ins.then_inc(pool_step, 1)
                pool.wait_ge(pool_step, steps[0])

            own(nc.gpsimd.memset(neg_half[:, :], -0.5))

            def load_bias(layer):
                table = na_rpb[layer, 0:1, 0, 0:1]
                for b in range(BLOCKS):
                    for half in range(P // GRID_W):
                        r = b * (P // GRID_W) + half
                        for head in range(NA_HEADS):
                            offset = (layer * NA_HEADS + head) * RPB_ROWS * RPB_COLS \
                                + (NA_WIN_ROWS - GRID_ROWS + r) * RPB_COLS + NA_WIN_COLS - GRID_W
                            src = bass.AP(table.tensor, offset,
                                          [[1, GRID_W], [RPB_COLS, GRID_ROWS], [1, GRID_W]])
                            dst = bias[half * GRID_W:(half + 1) * GRID_W, b, head, :]
                            pool.dma_start(dst.rearrange("p (r c) -> p r c", c=GRID_W), src)\
                                .then_inc(bias_loaded, 16)

            def norm_power(k):
                pool.wait_ge(sumsq_done, BLOCKS * (k + 1))
                own(nc.gpsimd.tensor_scalar(sumsq[:, :], sumsq[:, :], 1.0 / D_MODEL, EPS, ALU.mult, ALU.add))
                nc.gpsimd.tensor_tensor(rstd[:, :], sumsq[:, :], neg_half[:, 0:BLOCKS], ALU.pow).then_inc(rstd_ready, 1)

            def head_power(layer, lo, hi, pieces):
                pool.wait_ge(ss_done, 8 * layer + pieces)
                v = ss[:, :, lo:hi]
                own(nc.gpsimd.tensor_scalar(v, v, 1.0 / HEAD, EPS, ALU.mult, ALU.add))
                half = neg_half[:, 0:BLOCKS * (hi - lo)].rearrange("p (b h) -> p b h", b=BLOCKS)
                nc.gpsimd.tensor_tensor(hr[:, :, lo:hi], v, half, ALU.pow).then_inc(head_rstd_ready, 1)

            def rope_tables(layer):
                pool.wait_ge(qk_gain_loaded, 16 * (layer + 1))
                if layer == 0:
                    pool.wait_ge(cst_loaded, 16)
                else:
                    pool.wait_ge(qk_ready, 4 * layer)
                last = None
                for br in range(2):
                    groups = 2 if br == 0 else 1
                    w = HEAD // groups // 2
                    for qk in range(2):
                        kind = 2 * br + qk
                        g = qkg[:, br + 1, qk, :]
                        nc.gpsimd.tensor_tensor(tab[:, kind, 0], rope_cs[:, br, 0],
                                                g.unsqueeze(1).broadcast_to([P, BLOCKS, HEAD]), ALU.mult)
                        for half in range(2):
                            for gr in range(groups):
                                a = gr * 2 * w + half * w
                                c = gr * 2 * w + (1 - half) * w
                                last = nc.gpsimd.tensor_tensor(
                                    tab[:, kind, 1, :, a:a + w], rope_cs[:, br, 1, :, a:a + w],
                                    g[:, c:c + w].unsqueeze(1).broadcast_to([P, BLOCKS, w]), ALU.mult)
                last.then_inc(tab_ready, 1)

            def bias_mask(layer):
                pool.wait_ge(bias_loaded, 16 * BLOCKS * 2 * NA_HEADS * (layer + 1))
                v = bias_sb[:, :].rearrange("p (n c) -> p n c", c=GRID_W)
                nc.gpsimd.tensor_tensor(v, v, colmask.unsqueeze(1).broadcast_to([P, v.shape[1], GRID_W]),
                                        ALU.add).then_inc(bias_ready, 1)

            load_bias(0)
            for layer in range(DEPTH):
                first = PLACE[("qkv", layer, 0)]
                norm_power(2 * layer)
                rope_tables(layer)
                head_power(layer, 0, Q_HEADS, 4)
                head_power(layer, Q_HEADS, QK_HEADS, 8)
                bias_mask(layer)
                if layer + 1 < DEPTH:
                    pool.wait_ge(score_masked, len(MASKED_TILES) * (layer + 1))
                    load_bias(layer + 1)
                norm_power(2 * layer + 1)

        @block.scalar
        def _(act):
            act.dma_start(x, x_in.rearrange("(b p) n -> p b n", p=P)).then_inc(x_loaded, 16)
            act.dma_start(gain_rows[0:2 * DEPTH * DC, :], norm_gains.rearrange("l k (c p) -> (l k c) p", p=P))\
                .then_inc(gains_loaded, 16)
            act.dma_start(cst[:, :], constants).then_inc(cst_loaded, 16)
            for_gain = qk_gains.rearrange("l a b d -> l (a b d)")
            act.dma_start(qk_gain[:, :], for_gain[0].partition_broadcast(P)).then_inc(qk_gain_loaded, 16)
            act.dma_start(router, moe_router[0].rearrange("(c p) e -> p c e", p=P)).then_inc(router_loaded, 16)

            split = Splitter(act, "hi")

            def norm_squares(k):
                if k == 0:
                    act.wait_ge(x_loaded, 16)
                for b in range(BLOCKS):
                    if k:
                        act.wait_ge(x_ready, 4 * (k - 1) + 2 * (b + 1))
                        act.wait_ge(rstd_ready, k)
                    nc.scalar.activation(h[:, b, :], x[:, b, :], ACT.Square,
                                         accum_out=sumsq[:, b:b + 1]).then_inc(sumsq_done, 1)

            def hT_hi(k):
                for c in range(DC):
                    if c < 4:
                        act.wait_ge(xT_done, 4 * k + c + 1)
                    else:
                        act.wait_ge(hT_ready, DC * k + c - 3)
                    if k == 0 and c == 0:
                        act.wait_ge(gainT_ready, 1)
                    nc.scalar.activation(hT[k % 2][0][:, c, :], bank[4 + c % 4][:, c // 4 * SEQ:(c // 4 + 1) * SEQ],
                                         ACT.Copy, scale=gains[:, k, c:c + 1]).then_inc(hT_hi_ready, 1)

            def qkv_out(layer):
                for i in range(QKV_TILES):
                    n, b = i // 2, i % 2
                    last_tile = used(layer, "qkv", 2 * n + 1)
                    split.dense(last_tile + 2)
                    if b == 0:
                        act.wait_ge(qkv_done, QKV_TILES // 2 * layer + n + 1)
                    else:
                        act.wait_ge(w_used, last_tile)
                    width = min(COLS, max(0, QK_W - n * COLS))
                    if width:
                        k = 8 * layer + i
                        if k >= 2:
                            act.wait_ge(ss_done, k - 1)
                        nc.scalar.activation(square[i % 2][:, 0:width], bank[i % 4][:, 0:width],
                                             ACT.Square).then_inc(square_done, 1)
                    if 0 < width < COLS:
                        nc.scalar.copy(qk_sb[:, b, n * COLS:QK_W], bank[i % 4][:, 0:width])
                        nc.scalar.copy(v_sb[:, b, 0:COLS - width], bank[i % 4][:, width:]).then_inc(qkv_copied, 1)
                    elif width:
                        nc.scalar.copy(qk_sb[:, b, n * COLS:(n + 1) * COLS], bank[i % 4][:, :]).then_inc(qkv_copied, 1)
                    else:
                        nc.scalar.copy(v_sb[:, b, n * COLS - QK_W:(n + 1) * COLS - QK_W],
                                       bank[i % 4][:, :]).then_inc(qkv_copied, 1)

            def gate_out(layer, p):
                last_tile = used(layer, "gate", p)
                split.dense(last_tile + 2)
                act.wait_ge(w_used, last_tile)
                nc.scalar.copy(gatesT[:, 2 * p:2 * p + 2, :].rearrange("p i t -> p (i t)"),
                               bank[4 + p % 2][:, :]).then_inc(gate_copied, 1)

            def exponents(layer, u):
                tiles, _, _, kind = UNITS[u]
                act.wait_ge(max_ready, NU * layer + u + 1)
                n = len(tiles) * SEQ
                for b in range(BLOCKS):
                    if kind == "B":
                        s = next(i for i, t in enumerate(SCORE_TILES) if t == (u, 0))
                        src, scale = bank[s % 3][:, b * SEQ:(b + 1) * SEQ], SCALE
                    else:
                        src, scale = score_area[:, b * n:(b + 1) * n], 1.0
                    last = nc.scalar.activation(prob_area[:, b * n:(b + 1) * n], src, ACT.Exp,
                                                bias=nmax[:, u, b:b + 1], scale=scale,
                                                accum_out=esum[:, u, b:b + 1])
                last.then_inc(exp_done, 1)

            def probT_out(layer, u):
                for g in range(len(UNITS[u][0])):
                    s = SCORE_TILES.index((u, g))
                    act.wait_ge(probT_done, NS * layer + s + 1)
                    if g == 0 and NU * layer + u:
                        act.wait_ge(pv_done, NU * layer + u)
                    nc.scalar.copy(probT[:, 2 * g:2 * g + 2, :].rearrange("p c t -> p (c t)"),
                                   bank[6 + s % 2][:, :]).then_inc(probT_ready, 1)

            def sigmoid(layer, m):
                v = gatesT[:, m:3 * DC:DC, :]
                nc.scalar.activation(v, v, ACT.Sigmoid).then_inc(sigmoid_done, 1)

            for layer in range(DEPTH):
                split.dense(PLACE[("qkv", layer, 0)] + 2)
                norm_squares(2 * layer)
                hT_hi(2 * layer)
                qkv_out(layer)
                if layer + 1 < DEPTH:
                    act.wait_ge(tab_ready, layer + 1)
                    act.wait_ge(qk_ready, 4 * (layer + 1))
                    act.dma_start(qk_gain[:, :], for_gain[layer + 1].partition_broadcast(P))\
                        .then_inc(qk_gain_loaded, 16)
                for p in range(EARLY_PAIRS):
                    gate_out(layer, p)
                for u in range(NU + 1):
                    if u:
                        probT_out(layer, u - 1)
                    if u < NU:
                        exponents(layer, u)
                    if EARLY_PAIRS + u < GATE_PAIRS:
                        gate_out(layer, EARLY_PAIRS + u)
                act.wait_ge(gate_copied, GATE_PAIRS * (layer + 1))
                for m in range(2):
                    sigmoid(layer, m)
                for g in range(OC // 2):
                    act.wait_ge(oT_done, OC // 2 * layer + g + 1)
                    nc.scalar.copy(oT[0][:, 2 * g:2 * g + 2, :].rearrange("p c t -> p (c t)"),
                                   bank[6 + g % 2][:, :]).then_inc(oT_hi_ready, 1)
                for m in range(2, DC):
                    if m % 2 == 0:
                        split.dense(used(layer, "branch", m // 2 - 1) + 2)
                    sigmoid(layer, m)
                split.dense(used(layer, "out", OUT_TILES - 1) + 2)
                norm_squares(2 * layer + 1)
                hT_hi(2 * layer + 1)
                if layer % 2 == 0:
                    for s in range(FFN_STEPS):
                        gate_tile = used(layer // 2, "g", s)
                        split.dense(gate_tile + 2)
                        act.wait_ge(w_used, gate_tile)
                        if s >= 2:
                            act.wait_ge(ffn_act_ready, s - 1)
                        nc.scalar.activation(ffn_act[s % 2], bank[4 + 2 * (s % 2)][:, :], ACT.Silu)\
                            .then_inc(ffn_silu_done, 1)
                    split.dense(used(layer // 2, "d", FFN_STEPS - 1))

            act.wait_ge(gap_ready, 1)
            nc.scalar.activation(pick_tile(5), pick_tile(4), ACT.Exp).then_inc(gap_exp, 1)

            def expert(item, e):
                def act_hi_part(f):
                    act.wait_ge(actT_done, item * FBLOCKS + f + 1)
                    if f >= 2:
                        act.wait_ge(w_used, moe_used(item, MOE_PLACE[("d", f - 2, 1)]))
                    nc.scalar.copy(actT[0][:, f % 2].rearrange("p j t -> p (j t)"), bank[6][:, :]).then_inc(act_hi, 1)

                for f in range(FBLOCKS):
                    gate_tile = MOE_PLACE[("g", f, 1)]
                    split.moe(item, gate_tile + 1 + 2)
                    act.wait_ge(w_used, moe_used(item, gate_tile))
                    if f >= 2:
                        act.wait_ge(actT_done, item * FBLOCKS + f - 1)
                    nc.scalar.activation(moe_act[f % 2], bank[2][:, :], ACT.Silu).then_inc(silu_done, 1)
                    if f:
                        act_hi_part(f - 1)
                split.moe(item, MOE_PLACE[("d", FBLOCKS - 2, 1)] + 1 + 1)
                act_hi_part(FBLOCKS - 1)
                split.moe(item, MOE_TILES)
                act.wait_ge(w_used, moe_used(item, MOE_TILES - 1))
                for g in range(2):
                    nc.scalar.copy(y_sb[:, g * 512:(g + 1) * 512], bank[g][:, :]).then_inc(ytok_ready, 1)

            passes(act, expert)

        @block.vector
        def _(dve):
            steps = [0]

            def own(ins):
                steps[0] += 1
                ins.then_inc(dve_step, 1)
                dve.wait_ge(dve_step, steps[0])

            def norm_apply(k):
                dve.wait_ge(rstd_ready, k + 1)
                for b in range(BLOCKS):
                    nc.vector.tensor_scalar(h[:, b, :], x[:, b, :], rstd[:, b:b + 1], None, ALU.mult).then_inc(h_ready, 1)
                if k == 0:
                    dve.wait_ge(gainT_done, 1)
                    nc.vector.tensor_copy(gainT[:, :], bank[0][:, 0:2 * DEPTH * DC]).then_inc(gainT_ready, 1)
                    dve.wait_ge(gainT_ready, 1)
                for c in range(DC):
                    dve.wait_ge(hT_hi_ready, DC * k + c + 1)
                    last = nc.vector.scalar_tensor_tensor(
                        out=hT[k % 2][1][:, c, :], in0=bank[4 + c % 4][:, c // 4 * SEQ:(c // 4 + 1) * SEQ],
                        scalar=gains[:, k, c:c + 1], in1=hT[k % 2][0][:, c, :], op0=ALU.mult, op1=ALU.subtract)
                    last.then_inc(hT_ready, 1)

            def head_sums(layer, i):
                n, b = i // 2, i % 2
                heads = min(8, QK_HEADS - 8 * n)
                dve.wait_ge(square_done, 8 * layer + i + 1)
                nc.vector.tensor_reduce(ss[:, b, 8 * n:8 * n + heads],
                                        square[i % 2][:, 0:heads * HEAD].rearrange("p (h d) -> p h d", d=HEAD),
                                        AX_X, ALU.add).then_inc(ss_done, 1)

            def rotate(src, dst, kind, groups, b):
                heads = src.shape[1]
                w = HEAD // groups // 2
                ra = rope_a[:, 0:heads * HEAD].rearrange("p (h d) -> p h d", d=HEAD)
                rb = rope_b[:, 0:heads * HEAD].rearrange("p (h d) -> p h d", d=HEAD)
                nc.vector.tensor_tensor(ra, src, tab[:, kind, 0, b].unsqueeze(1).broadcast_to([P, heads, HEAD]), ALU.mult)
                for gr in range(groups):
                    for half in range(2):
                        a = gr * 2 * w + half * w
                        c = gr * 2 * w + (1 - half) * w
                        last = nc.vector.tensor_tensor(
                            rb[:, :, a:a + w], src[:, :, c:c + w],
                            tab[:, kind, 1, b, a:a + w].unsqueeze(1).broadcast_to([P, heads, w]), ALU.mult)
                own(last)
                if kind == 0:
                    for kv in range(GQA_KV):
                        last = nc.vector.tensor_tensor(dst[:, kv:GQA_Q:GQA_KV, :], ra[:, kv * GQA_REP:(kv + 1) * GQA_REP, :],
                                                       rb[:, kv * GQA_REP:(kv + 1) * GQA_REP, :], ALU.add)
                    return last
                return nc.vector.tensor_tensor(dst, ra, rb, ALU.add)

            def qk_norm_rope(layer, qk):
                dve.wait_ge(head_rstd_ready, 2 * layer + qk + 1)
                dve.wait_ge(qkv_copied, QKV_TILES * layer + 4 * (qk + 1))
                if qk == 0:
                    dve.wait_ge(tab_ready, layer + 1)
                lo = 0 if qk == 0 else Q_HEADS
                na, nb, ncc = NA_HEADS, (GQA_Q if qk == 0 else GQA_KV), DIL_HEADS
                for b in range(BLOCKS):
                    v = qk_sb[:, b, lo * HEAD:(lo + na + nb + ncc) * HEAD].rearrange("p (h d) -> p h d", d=HEAD)
                    own(nc.vector.tensor_tensor(v, v, hr[:, b, lo:lo + na + nb + ncc].unsqueeze(2)
                                                .broadcast_to([P, na + nb + ncc, HEAD]), ALU.mult))
                    nc.vector.tensor_tensor(v[:, 0:na, :], v[:, 0:na, :],
                                            qkg[:, 0, qk, :].unsqueeze(1).broadcast_to([P, na, HEAD]), ALU.mult)
                    own(rotate(v[:, na:na + nb, :], v[:, na:na + nb, :], qk, 2, b))
                    rotate(v[:, na + nb:, :], v[:, na + nb:, :], 2 + qk, 1, b).then_inc(qk_ready, 1)
                    dve.wait_ge(qk_ready, 4 * layer + 2 * qk + b + 1)

            def masked_scores(layer, u):
                tiles, _, _, kind = UNITS[u]
                n = len(tiles) * SEQ
                if kind != "B":
                    if NU * layer + u:
                        dve.wait_ge(exp_done, NU * layer + u)
                    for g in range(len(tiles)):
                        s = SCORE_TILES.index((u, g))
                        dve.wait_ge(score_done, NS * layer + s + 1)
                        src = bank[s % 3][:, :].rearrange("p (b k) -> p b k", b=BLOCKS)
                        dst = score_area[:, 0:BLOCKS * n].rearrange("p (b k) -> p b k", b=BLOCKS)[:, :, g * SEQ:(g + 1) * SEQ]
                        if kind == "C" and DIL_GROUPS[g][1] > 1:
                            dil = DIL_GROUPS[g][1]
                            m = (mod4 if dil == 4 else mod16).unsqueeze(1).broadcast_to([P, SEQ // dil, dil])
                            for b in range(BLOCKS):
                                last = nc.vector.scalar_tensor_tensor(
                                    out=dst[:, b, :].rearrange("p (n m) -> p n m", m=dil),
                                    in0=src[:, b, :].rearrange("p (n m) -> p n m", m=dil), scalar=SCALE,
                                    in1=m, op0=ALU.mult, op1=ALU.add)
                        else:
                            if kind != "C" and u == DIL_PER_GROUP:
                                dve.wait_ge(bias_ready, layer + 1)
                            m = band if kind == "C" else bias[:, :, int(kind[1]), ::-1]
                            last = nc.vector.scalar_tensor_tensor(out=dst, in0=src, scalar=SCALE, in1=m,
                                                                  op0=ALU.mult, op1=ALU.add)
                        last.then_inc(score_masked, 1)
                    dve.wait_ge(score_masked, len(MASKED_TILES) * layer + MASKED_TILES.index(s) + 1)
                    nc.vector.tensor_reduce(nmax[:, u, :], score_area[:, 0:BLOCKS * n].rearrange("p (b k) -> p b k", b=BLOCKS),
                                            AX_X, ALU.max, negate=True).then_inc(max_ready, 1)
                else:
                    s = SCORE_TILES.index((u, 0))
                    dve.wait_ge(score_done, NS * layer + s + 1)
                    own(nc.vector.tensor_reduce(nmax[:, u, :], bank[s % 3][:, :].rearrange("p (b k) -> p b k", b=BLOCKS),
                                                AX_X, ALU.max, negate=True))
                    nc.vector.tensor_scalar(nmax[:, u, :], nmax[:, u, :], SCALE, None, ALU.mult).then_inc(max_ready, 1)

            def attention_out(layer, u):
                dve.wait_ge(exp_done, NU * layer + u + 1)
                own(nc.vector.reciprocal(rsum[:, u, :], esum[:, u, :]))
                dve.wait_ge(pv_done, NU * layer + u + 1)
                col = UNITS[u][2]
                for b in range(BLOCKS):
                    last = nc.vector.tensor_scalar(o[:, b, col:col + HEAD], bank[3][:, b * HEAD:(b + 1) * HEAD],
                                                   rsum[:, u, b:b + 1], None, ALU.mult)
                last.then_inc(o_ready, 1)

            def merge(layer, m):
                k = DC * layer + m
                split.dense(used(layer, "branch", m // 2) + 2)
                if m % 2 == 0:
                    dve.wait_ge(y_done, DC // 2 * layer + m // 2 + 1)
                else:
                    dve.wait_ge(w_used, used(layer, "branch", m // 2))
                dve.wait_ge(sigmoid_done, k + 1)
                if m >= 2:
                    dve.wait_ge(merged_ready, k - 1)
                ab, c, s = bank[4 + 2 * (m % 2)], bank[5 + 2 * (m % 2)], m % 2
                nc.vector.tensor_tensor(gate_y[s], ab[:, :].rearrange("p (b t) -> p b t", b=2),
                                        gatesT[:, m:2 * DC:DC, :], ALU.mult)
                nc.vector.tensor_tensor(gate_yc[s], c[:, 0:SEQ], gatesT[:, 2 * DC + m, :], ALU.mult).then_inc(y_read, 1)
                dve.wait_ge(y_read, k + 1)
                own(nc.vector.tensor_tensor(gate_yab[s], gate_y[s][:, 0, :], gate_y[s][:, 1, :], ALU.add))
                own(nc.vector.tensor_tensor(gate_sum[s], gate_yab[s], gate_yc[s], ALU.add))
                own(nc.vector.tensor_copy(mergedT[0][:, m, :], gate_sum[s]))
                nc.vector.tensor_tensor(mergedT[1][:, m, :], gate_sum[s], mergedT[0][:, m, :], ALU.subtract)\
                    .then_inc(merged_ready, 1)

            def add_residual(k, last_tile):
                for i in range(4):
                    if i < 3:
                        dve.wait_ge(residual_done, 3 * k + i + 1)
                    else:
                        dve.wait_ge(w_used, last_tile)
                    v = x[:, i // 2, (i % 2) * 512:(i % 2 + 1) * 512]
                    nc.vector.tensor_tensor(v, v, bank[i][:, :], ALU.add).then_inc(x_ready, 1)

            split = Splitter(dve, "lo")
            for layer in range(DEPTH):
                first = PLACE[("qkv", layer, 0)]
                split.dense(first + 2)
                norm_apply(2 * layer)
                for i in range(8):
                    split.dense(used(layer, "qkv", i // 2 * 2 + 1) + 2)
                    head_sums(layer, i)
                    if i == 5:
                        qk_norm_rope(layer, 0)
                split.dense(used(layer, "qkv", QKV_TILES - 1) + 2)
                qk_norm_rope(layer, 1)
                split.dense(used(layer, "gate", EARLY_PAIRS - 1) + 2)
                for g in range(QK_HEADS // 4):
                    dve.wait_ge(qkT_done, QK_HEADS // 4 * layer + g + 1)
                    nc.vector.tensor_copy(qkT[:, 2 * g:2 * g + 2, :].rearrange("p c t -> p (c t)"),
                                          bank[6 + g % 2][:, :]).then_inc(qkT_ready, 1)
                for u in range(NU + 1):
                    if u < NU:
                        masked_scores(layer, u)
                    if u:
                        attention_out(layer, u - 1)
                    split.dense(min(used(layer, "gate", 0) + EARLY_PAIRS + u, used(layer, "gate", GATE_TILES - 1)) + 2)
                for g in range(OC // 2):
                    dve.wait_ge(oT_hi_ready, OC // 2 * layer + g + 1)
                    nc.vector.tensor_tensor(oT[1][:, 2 * g:2 * g + 2, :].rearrange("p c t -> p (c t)"), bank[6 + g % 2][:, :],
                                            oT[0][:, 2 * g:2 * g + 2, :].rearrange("p c t -> p (c t)"),
                                            ALU.subtract).then_inc(oT_ready, 1)
                for m in range(DC):
                    merge(layer, m)
                last_tile = used(layer, "out", OUT_TILES - 1)
                split.dense(last_tile + 2)
                add_residual(2 * layer, last_tile)
                norm_apply(2 * layer + 1)
                if layer % 2 == 0:
                    for s in range(FFN_STEPS):
                        up_tile = used(layer // 2, "u", s)
                        split.dense(up_tile + 2)
                        dve.wait_ge(ffn_silu_done, s + 1)
                        dve.wait_ge(w_used, up_tile)
                        own(nc.vector.tensor_tensor(ffn_act[s % 2], ffn_act[s % 2], bank[5 + 2 * (s % 2)][:, :], ALU.mult))
                        if s >= 2:
                            dve.wait_ge(w_used, used(layer // 2, "d", s - 2))
                        hi, lo = [v[:, s % 2].rearrange("p j t -> p (j t)") for v in ffn_actT]
                        own(nc.vector.tensor_copy(hi, ffn_act[s % 2]))
                        nc.vector.tensor_tensor(lo, ffn_act[s % 2], hi, ALU.subtract).then_inc(ffn_act_ready, 1)
                    last_tile = used(layer // 2, "d", FFN_STEPS - 1)
                    split.dense(last_tile + 2)
                    add_residual(2 * layer + 1, last_tile)

            lg, eq, cand, first, lg2, second, sel, gate, rank, gate_t, rank_t, cnt = [route_tile(i) for i in range(12)]
            v0, i0, v1, i1, gap, ex, den, w0, w1 = [pick_tile(i) for i in range(9)]

            def spread(v):
                return v.unsqueeze(2).broadcast_to([P, BLOCKS, EXPERTS])

            def greatest(logits, value, index, onehot):
                own(nc.vector.tensor_reduce(value, logits, AX_X, ALU.max))
                own(nc.vector.tensor_tensor(eq, logits, spread(value), ALU.is_ge))
                own(nc.vector.scalar_tensor_tensor(out=cand, in0=eq, scalar=-float(EXPERTS),
                                                   in1=iota8.unsqueeze(1).broadcast_to([P, BLOCKS, EXPERTS]),
                                                   op0=ALU.mult, op1=ALU.add))
                own(nc.vector.tensor_reduce(index, cand, AX_X, ALU.min))
                own(nc.vector.tensor_tensor(onehot, cand, spread(index), ALU.is_equal))

            dve.wait_ge(logits_done, 1)
            own(nc.vector.tensor_copy(lg, bank[0][:, 0:BLOCKS * EXPERTS].rearrange("p (b e) -> p b e", b=BLOCKS)))
            greatest(lg, v0, i0, first)
            own(nc.vector.scalar_tensor_tensor(out=lg2, in0=first, scalar=-3e38, in1=lg, op0=ALU.mult, op1=ALU.add))
            greatest(lg2, v1, i1, second)
            nc.vector.tensor_tensor(gap, v1, v0, ALU.subtract).then_inc(gap_ready, 1)
            nc.vector.tensor_tensor(sel, first, second, ALU.add).then_inc(sel_ready, 1)
            dve.wait_ge(gap_exp, 1)
            own(nc.vector.tensor_scalar(den, ex, 1.0, None, ALU.add))
            own(nc.vector.reciprocal(w0, den))
            own(nc.vector.tensor_tensor(w1, ex, w0, ALU.mult))
            own(nc.vector.tensor_tensor(first, first, spread(w0), ALU.mult))
            own(nc.vector.tensor_tensor(second, second, spread(w1), ALU.mult))
            own(nc.vector.tensor_tensor(gate, first, second, ALU.add))
            dve.wait_ge(rank_done, 1)
            own(nc.vector.scalar_tensor_tensor(out=rank, in0=bank[1][:, 0:BLOCKS * EXPERTS].rearrange("p (b e) -> p b e", b=BLOCKS),
                                               scalar=1000.0, in1=sel, op0=ALU.add, op1=ALU.mult))
            by_expert = lambda v: v.rearrange("p b e -> p (b e)").rearrange("p (e b) -> p e b", b=BLOCKS)
            rank_x, gate_x = by_expert(rank_t), by_expert(gate_t)
            nc.vector.tensor_copy(gate_x, gate.rearrange("p b e -> p e b"))
            own(nc.vector.tensor_scalar(rank_x, rank.rearrange("p b e -> p e b"), -1000.0, None, ALU.add))
            nc.vector.tensor_reduce(most[:, 0:1], bank[1][:, BLOCKS * EXPERTS:(BLOCKS + 1) * EXPERTS],
                                    AX_X, ALU.max).then_inc(most_ready, 1)

            def expert(item, e):
                nc.vector.tensor_copy(rank_e, rank_x[:, e, :])
                nc.vector.tensor_copy(gate_e, gate_x[:, e, :]).then_inc(expert_cols, 1)
                dve.wait_ge(expert_cols, item + 1)
                for b in range(BLOCKS):
                    nc.vector.tensor_scalar(choose[:, b, :], iota, rank_e[:, b:b + 1], None, ALU.is_equal)
                    last = nc.vector.tensor_scalar(weigh[:, b, :], iota, rank_e[:, b:b + 1], gate_e[:, b:b + 1],
                                                   ALU.is_equal, ALU.mult)
                last.then_inc(choose_ready, 1)
                split.moe(item, 2)
                for g in range(2):
                    c = slice(4 * g, 4 * g + 4)
                    dve.wait_ge(picked_done, item * 2 + g + 1)
                    nc.vector.tensor_tensor(picked[:, c, :], bank[4 + g][:, :].rearrange("p (c t) -> p c t", c=4),
                                            gains[:, 3, c].unsqueeze(2).broadcast_to([P, 4, SLOTS]),
                                            ALU.mult).then_inc(picked_read, 1)
                    dve.wait_ge(picked_read, item * 2 + g + 1)
                    nc.vector.tensor_copy(pickedT[0][:, c, :], picked[:, c, :]).then_inc(picked_hi, 1)
                    dve.wait_ge(picked_hi, item * 2 + g + 1)
                    nc.vector.tensor_tensor(pickedT[1][:, c, :], picked[:, c, :], pickedT[0][:, c, :],
                                            ALU.subtract).then_inc(picked_ready, 1)
                dve.wait_ge(weighT_done, item + 1)
                nc.vector.tensor_copy(weighT, bank[7][:, 0:SEQ]).then_inc(weighT_ready, 1)

                def act_product(f):
                    up_tile = MOE_PLACE[("u", f, 1)]
                    split.moe(item, up_tile + 1 + 2)
                    dve.wait_ge(silu_done, item * FBLOCKS + f + 1)
                    dve.wait_ge(w_used, moe_used(item, up_tile))
                    nc.vector.tensor_tensor(moe_act[f % 2], moe_act[f % 2], bank[3][:, :], ALU.mult).then_inc(act_ready, 1)

                def act_split(f):
                    if f < FBLOCKS - 1:
                        split.moe(item, MOE_PLACE[("g", f + 1, 1)] + 1 + 2)
                    hi, lo = [v[:, f % 2].rearrange("p j t -> p (j t)") for v in actT]
                    dve.wait_ge(act_hi, item * FBLOCKS + f + 1)
                    nc.vector.tensor_tensor(lo, bank[6][:, :], hi, ALU.subtract).then_inc(actT_ready, 1)

                for f in range(FBLOCKS):
                    if f:
                        act_split(f - 1)
                    act_product(f)
                act_split(FBLOCKS - 1)
                split.moe(item, MOE_TILES)
                for i in range(4):
                    dve.wait_ge(scattered, item * 4 + i + 1)
                    v = x[:, i // 2, (i % 2) * 512:(i % 2 + 1) * 512]
                    last = nc.vector.tensor_tensor(v, v, bank[4 + i][:, :], ALU.add)

            with dve.Fori(0, EXPERTS) as e:
                expert(e, e)
            if OVER:
                count = dve.value_load(most[0:1, 0:1], min_val=0, max_val=SEQ)
                with dve.If(count > SLOTS):
                    with dve.Fori(1, ROUNDS) as r:
                        nc.vector.tensor_scalar(rank_t, rank_t, -float(SLOTS), None, ALU.add).then_inc(expert_rank, 1)
                        with dve.Fori(0, EXPERTS) as e:
                            dve.wait_ge(expert_rank, r)
                            expert(r * EXPERTS + e, e)
            dve.drain().then_inc(x_final, 1)

        @block.tensor
        def _(pe):
            def parts(n, slot, c, width):
                return [v[:, 0:width].rearrange("p (c n) -> p c n", c=c) for v in (hi_slot[n % HI_RING], lo_slot[slot])]

            def dense_tile(kind, layer, i, chunks):
                n = PLACE[(kind, layer, i)]
                pe.wait_ge(lo_ready, n + 1)
                return parts(n, n % DENSE_RING, chunks, WIDTH[n])

            def moe_tile(item, kind, f, half, chunks):
                j = MOE_PLACE[(kind, f, half)]
                n = ND + j
                pe.wait_ge(lo_ready, item * MOE_TILES + (n + 1))
                return parts(n, moe_slot(j), chunks, TILE)

            def product(place, lhs, rhs, first, last):
                nc.tensor.matmul(place, lhs[0], rhs[0], start=first, stop=False)
                nc.tensor.matmul(place, lhs[0], rhs[1], start=False, stop=False)
                return nc.tensor.matmul(place, lhs[1], rhs[0], start=False, stop=last)

            def norm_transposes(k):
                if k == 0:
                    pe.wait_ge(cst_loaded, 16)
                    pe.wait_ge(gains_loaded, 16)
                    rows = 2 * DEPTH * DC
                    nc.tensor.transpose(bank[0][:, 0:rows], gain_rows[0:rows, :], ident[0:rows, 0:rows]).then_inc(gainT_done, 1)
                for b in range(BLOCKS):
                    pe.wait_ge(h_ready, BLOCKS * k + b + 1)
                    for c in (0, 4, 1, 5, 2, 6, 3, 7):
                        last = nc.tensor.transpose(bank[4 + c % 4][:, (c // 4) * SEQ + b * P:(c // 4) * SEQ + (b + 1) * P],
                                                   h[:, b, c * P:(c + 1) * P], ident)
                        if b == BLOCKS - 1 and c >= 4:
                            last.then_inc(xT_done, 1)

            def project(out_ap, lhs, rhs, n):
                for c in range(n):
                    last = nc.tensor.matmul(out_ap, lhs(c), rhs(c), start=(c == 0), stop=(c == n - 1))
                return last

            def scores(layer, u):
                for g, (qc, kc, half) in enumerate(UNITS[u][0]):
                    s = SCORE_TILES.index((u, g))
                    if s >= 3:
                        pu, pg = SCORE_TILES[s - 3]
                        if UNITS[pu][3] == "B":
                            pe.wait_ge(exp_done, NU * layer + pu + 1)
                        else:
                            pe.wait_ge(score_masked, len(MASKED_TILES) * layer + MASKED_TILES.index(s - 3) + 1)
                    rows = slice(half * HEAD, (half + 1) * HEAD)
                    for b in range(BLOCKS):
                        last = nc.tensor.matmul(bank[s % 3][:, b * SEQ:(b + 1) * SEQ], qkT[rows, qc, b * P:(b + 1) * P],
                                                qkT[rows, kc, :], start=True, stop=True)
                    last.then_inc(score_done, 1)

            def prob_transposes(layer, u):
                tiles = UNITS[u][0]
                n = len(tiles) * SEQ
                pe.wait_ge(exp_done, NU * layer + u + 1)
                for g in range(len(tiles)):
                    s = SCORE_TILES.index((u, g))
                    if s >= 2:
                        pe.wait_ge(probT_ready, NS * layer + s - 1)
                    for kc in range(2):
                        for b in range(BLOCKS):
                            col = b * n + g * SEQ + kc * P
                            last = nc.tensor.transpose(bank[6 + s % 2][:, kc * SEQ + b * P:kc * SEQ + (b + 1) * P],
                                                       prob_area[:, col:col + P], ident)
                    last.then_inc(probT_done, 1)

            def values(layer, u):
                vcols = UNITS[u][1]
                pe.wait_ge(probT_ready, NS * layer + SCORE_TILES.index((u, len(vcols) - 1)) + 1)
                if NU * layer + u:
                    pe.wait_ge(o_ready, NU * layer + u)
                for b in range(BLOCKS):
                    last = project(bank[3][:, b * HEAD:(b + 1) * HEAD],
                                   lambda c: probT[:, c, b * P:(b + 1) * P],
                                   lambda c: v_sb[:, c % 2, vcols[c // 2]:vcols[c // 2] + HEAD], 2 * len(vcols))
                last.then_inc(pv_done, 1)

            def attention(layer):
                x_hi, x_lo = hT[0]
                for n in range(QKV_TILES // 2):
                    for half in range(2):
                        w = dense_tile("qkv", layer, 2 * n + half, 4)
                        if n == 0:
                            pe.wait_ge(hT_ready, DC * 2 * layer + 4 * (half + 1))
                        for b in range(BLOCKS):
                            i = 2 * n + b
                            if i >= 4 and half == 0:
                                pe.wait_ge(qkv_copied, QKV_TILES * layer + i - 3)
                            for c in range(4):
                                rows = 4 * half + c
                                tok = slice(b * P, (b + 1) * P)
                                last = product(bank[i % 4][:, :], (x_hi[:, rows, tok], x_lo[:, rows, tok]),
                                               (w[0][:, c, :], w[1][:, c, :]), rows == 0, rows == DC - 1)
                            if half and b == 0:
                                last.then_inc(qkv_done, 1)
                        last.then_inc(w_used, 1)

                gate_w = [None]

                def gates(i):
                    p, j = i // 2, i % 2
                    if j == 0:
                        gate_w[0] = dense_tile("gate", layer, p, DC)
                        if p >= 2:
                            pe.wait_ge(gate_copied, GATE_PAIRS * layer + p - 1)
                    w = gate_w[0]
                    for c in range(DC):
                        last = product(bank[4 + p % 2][:, j * SEQ:(j + 1) * SEQ],
                                       (w[0][:, c, j * P:(j + 1) * P], w[1][:, c, j * P:(j + 1) * P]),
                                       (x_hi[:, c, :], x_lo[:, c, :]), c == 0, c == DC - 1)
                    if j:
                        last.then_inc(w_used, 1)

                for i in range(2 * EARLY_PAIRS):
                    gates(i)
                for g in range(QK_HEADS // 4):
                    if g == 0:
                        pe.wait_ge(qk_ready, 4 * layer + 4)
                    if g >= 2:
                        pe.wait_ge(qkT_ready, QK_HEADS // 4 * layer + g - 1)
                    for c in range(2):
                        for b in range(BLOCKS):
                            last = nc.tensor.transpose(bank[6 + g % 2][:, c * SEQ + b * P:c * SEQ + (b + 1) * P],
                                                       qk_sb[:, b, (2 * g + c) * P:(2 * g + c + 1) * P], ident)
                    last.then_inc(qkT_done, 1)
                pe.wait_ge(qkT_ready, QK_HEADS // 4 * (layer + 1))
                pe.wait_ge(qkv_copied, QKV_TILES * (layer + 1))
                for u in range(NU + 1):
                    pair = EARLY_PAIRS + u
                    if u:
                        prob_transposes(layer, u - 1)
                    if u < NU:
                        scores(layer, u)
                    if pair < GATE_PAIRS:
                        gates(2 * pair)
                    if u:
                        values(layer, u - 1)
                    if pair < GATE_PAIRS:
                        gates(2 * pair + 1)
                pe.wait_ge(o_ready, NU * (layer + 1))
                pe.wait_ge(gate_copied, GATE_PAIRS * (layer + 1))
                for g in range(OC // 2):
                    if g >= 2:
                        pe.wait_ge(oT_ready, OC // 2 * layer + g - 1)
                    for c in range(2):
                        for b in range(BLOCKS):
                            last = nc.tensor.transpose(bank[6 + g % 2][:, c * SEQ + b * P:c * SEQ + (b + 1) * P],
                                                       o[:, b, (2 * g + c) * P:(2 * g + c + 1) * P], ident)
                    last.then_inc(oT_done, 1)
                pe.wait_ge(oT_ready, OC // 2 * (layer + 1))

                chunks = ((0, 2), (2, 5), (5, 6))

                def branch(n):
                    w = dense_tile("branch", layer, n, OC)
                    for j in range(2):
                        m = 2 * n + j
                        if m >= 2:
                            pe.wait_ge(y_read, DC * layer + m - 1)
                        places = (bank[4 + 2 * j][:, 0:SEQ], bank[4 + 2 * j][:, SEQ:2 * SEQ], bank[5 + 2 * j][:, 0:SEQ])
                        for place, (lo, hi) in zip(places, chunks):
                            for c in range(lo, hi):
                                last = product(place, (w[0][:, c, j * P:(j + 1) * P], w[1][:, c, j * P:(j + 1) * P]),
                                               (oT[0][:, c, :], oT[1][:, c, :]), c == lo, c == hi - 1)
                        last.then_inc(w_used if j else y_done, 1)

                def project_out(n):
                    w = dense_tile("out", layer, n, 2)
                    pe.wait_ge(merged_ready, DC * layer + 2 * n + 2)
                    rows_product(mergedT, w, (2 * n, 2 * n + 1), n == 0, n == OUT_TILES - 1)

                for n in range(BRANCH_TILES):
                    branch(n)
                    if n:
                        project_out(n - 1)
                project_out(OUT_TILES - 1)

            def rows_product(actT, w, chunks, first, last):
                for i in range(4):
                    tok, col = slice(i // 2 * P, (i // 2 + 1) * P), slice(i % 2 * 512, (i % 2 + 1) * 512)
                    for j in range(2):
                        ins = product(bank[i][:, :], (actT[0][:, chunks[j], tok], actT[1][:, chunks[j], tok]),
                                      (w[0][:, j, col], w[1][:, j, col]), first and j == 0, last and j == 1)
                    if last and i < 3:
                        ins.then_inc(residual_done, 1)
                ins.then_inc(w_used, 1)

            def dense_ffn(layer):
                def gate_up(s):
                    for g, kind in enumerate("gu"):
                        w = dense_tile(kind, layer, s, DC)
                        if s >= 2 and g == 0:
                            pe.wait_ge(ffn_act_ready, s - 1)
                        for j in range(2):
                            for c in range(DC):
                                last = product(bank[4 + 2 * (s % 2) + g][:, j * SEQ:(j + 1) * SEQ],
                                               (w[0][:, c, j * P:(j + 1) * P], w[1][:, c, j * P:(j + 1) * P]),
                                               (hT[1][0][:, c, :], hT[1][1][:, c, :]), c == 0, c == DC - 1)
                        last.then_inc(w_used, 1)

                def down(s):
                    w = dense_tile("d", layer, s, 2)
                    pe.wait_ge(ffn_act_ready, s + 1)
                    act = [v.rearrange("p s j t -> p (s j) t") for v in ffn_actT]
                    rows_product(act, w, (2 * (s % 2), 2 * (s % 2) + 1), s == 0, s == FFN_STEPS - 1)

                for s in range(FFN_STEPS):
                    gate_up(s)
                    if s:
                        down(s - 1)
                down(FFN_STEPS - 1)

            for layer in range(DEPTH):
                norm_transposes(2 * layer)
                attention(layer)
                norm_transposes(2 * layer + 1)
                pe.wait_ge(hT_ready, DC * (2 * layer + 2))
                if layer % 2 == 0:
                    dense_ffn(layer)

            pe.wait_ge(router_loaded, 16)
            for b in range(BLOCKS):
                last = project(bank[0][:, b * EXPERTS:(b + 1) * EXPERTS],
                               lambda c: hT[1][c % 2][:, c // 2, b * P:(b + 1) * P].bitcast(F32),
                               lambda c: router[:, c // 2, :], 2 * DC)
            last.then_inc(logits_done, 1)
            pe.wait_ge(sel_ready, 1)
            sel = route_tile(6)
            nc.tensor.matmul(bank[1][:, 0:EXPERTS], tri, sel[:, 0, :], start=True, stop=True)
            nc.tensor.matmul(bank[1][:, EXPERTS:2 * EXPERTS], ones, sel[:, 0, :], start=True, stop=False)
            nc.tensor.matmul(bank[1][:, EXPERTS:2 * EXPERTS], tri, sel[:, 1, :], start=False, stop=True)
            nc.tensor.matmul(bank[1][:, 2 * EXPERTS:3 * EXPERTS], ones, sel[:, 0, :], start=True, stop=False)
            nc.tensor.matmul(bank[1][:, 2 * EXPERTS:3 * EXPERTS], ones, sel[:, 1, :], start=False, stop=True).then_inc(rank_done, 1)

            def expert(item, e):
                pe.wait_ge(choose_ready, item + 1)
                for c in range(DC):
                    for b in range(BLOCKS):
                        last = nc.tensor.matmul(bank[4 + c // 4][:, (c % 4) * SLOTS:(c % 4 + 1) * SLOTS],
                                                h[:, b, c * P:(c + 1) * P], choose[:, b, :],
                                                start=(b == 0), stop=(b == BLOCKS - 1))
                    if c % 4 == 3:
                        last.then_inc(picked_done, 1)
                for b in range(BLOCKS):
                    last = nc.tensor.transpose(bank[7][:, b * P:(b + 1) * P], weigh[:, b, :], ident)
                last.then_inc(weighT_done, 1)

                def up(kind, f):
                    for half in range(2):
                        w = moe_tile(item, kind, f, half, 4)
                        if f == 0 and kind == "g":
                            pe.wait_ge(picked_ready, item * 2 + half + 1)
                        if f and half == 0:
                            if kind == "g":
                                pe.wait_ge(silu_done, item * FBLOCKS + f)
                            else:
                                pe.wait_ge(act_ready, item * FBLOCKS + f)
                        for c in range(4):
                            rows = 4 * half + c
                            last = product(bank[2 + "gu".index(kind)][:, :], (pickedT[0][:, rows, :], pickedT[1][:, rows, :]),
                                           (w[0][:, c, :], w[1][:, c, :]), rows == 0, rows == DC - 1)
                        last.then_inc(w_used, 1)

                def act_transposes(f):
                    pe.wait_ge(act_ready, item * FBLOCKS + f + 1)
                    if f:
                        pe.wait_ge(actT_ready, item * FBLOCKS + f)
                    for j in range(JB):
                        last = nc.tensor.transpose(bank[6][:, j * P:(j + 1) * P], moe_act[f % 2][:, j * P:(j + 1) * P], ident)
                    last.then_inc(actT_done, 1)

                def down(f):
                    for half in range(2):
                        w = moe_tile(item, "d", f, half, 2)
                        if half == 0:
                            pe.wait_ge(actT_ready, item * FBLOCKS + f + 1)
                        for i in range(2):
                            for c in range(2):
                                j = 2 * half + c
                                last = product(bank[i][:, :], (actT[0][:, f % 2, j, :], actT[1][:, f % 2, j, :]),
                                               (w[0][:, c, i * 512:(i + 1) * 512], w[1][:, c, i * 512:(i + 1) * 512]),
                                               f == 0 and j == 0, f == FBLOCKS - 1 and j == JB - 1)
                        last.then_inc(w_used, 1)

                for f in range(FBLOCKS):
                    up("g", f)
                    if f:
                        act_transposes(f - 1)
                    up("u", f)
                    if f:
                        down(f - 1)
                act_transposes(FBLOCKS - 1)
                down(FBLOCKS - 1)

                pe.wait_ge(weighT_ready, item + 1)
                for i in range(4):
                    if i < 2:
                        pe.wait_ge(ytok_ready, item * 2 + i + 1)
                    nc.tensor.matmul(bank[4 + i][:, :], weighT[:, (i // 2) * P:(i // 2 + 1) * P],
                                     y_sb[:, (i % 2) * 512:(i % 2 + 1) * 512], start=True, stop=True)\
                        .then_inc(scattered, 1)

            passes(pe, expert)


def constant_table():
    t = np.zeros((P, C_END), np.float32)
    p = np.arange(P)
    t[:, C_IDENT:C_IDENT + P] = np.eye(P)
    t[:, C_TRI:C_TRI + P] = p[:, None] < p[None, :]
    t[:, C_ONES:C_ONES + P] = 1
    t[:, C_IOTA:C_IOTA + SLOTS] = np.arange(SLOTS)
    t[:, C_IOTA8:C_IOTA8 + EXPERTS] = np.arange(EXPERTS)
    k = np.arange(SEQ)
    side = DIL_GROUPS[0][0] // 2
    for b in range(BLOCKS):
        near = np.abs(k[None, :] - (b * P + p)[:, None]) <= side
        t[:, C_BAND + b * SEQ:C_BAND + (b + 1) * SEQ] = np.where(near, 0, NEG)
    t[:, C_MOD4:C_MOD16] = np.where(np.arange(4)[None, :] == (p % 4)[:, None], 0, NEG)
    t[:, C_MOD16:C_COLM] = np.where(np.arange(16)[None, :] == (p % 16)[:, None], 0, NEG)
    c, kc = (p % GRID_W)[:, None], np.arange(GRID_W)[None, :]
    start = np.clip(c - NA_WIN_COLS // 2, 0, GRID_W - NA_WIN_COLS)
    t[:, C_COLM:C_ROPE] = np.where((kc >= start) & (kc < start + NA_WIN_COLS), 0, NEG)[:, ::-1]
    rope = np.zeros((P, 2, 2, BLOCKS, HEAD), np.float32)

    def angles(pos, dim):
        freq = (np.float32(10000.0) ** (-np.arange(0, dim, 2, dtype=np.float32) / np.float32(dim))).astype(np.float32)
        return pos.astype(np.float32)[:, None] * freq[None, :]

    for b in range(BLOCKS):
        pos = b * P + p
        row, col, line = angles(pos // GRID_W, HEAD // 2), angles(pos % GRID_W, HEAD // 2), angles(pos, HEAD)
        for r, parts in enumerate(([row, row, col, col], [line, line])):
            rope[:, r, 0, b] = np.cos(np.concatenate(parts, 1))
            sign = np.concatenate([np.full(a.shape, -1.0 if i % 2 == 0 else 1.0) for i, a in enumerate(parts)], 1)
            rope[:, r, 1, b] = sign * np.sin(np.concatenate(parts, 1))
    t[:, C_ROPE:C_END] = rope.reshape(P, -1)
    return t


_INS = ["x", "norm_gains", "w_in", "qk_gains", "na_rpb", "w_branch", "w_out", "ffn_w_gu", "ffn_w_down",
        "moe_router", "moe_w_gu", "moe_w_down"]


def kernel(**inputs):
    import concourse.bacc as bacc
    from concourse.bass_utils import run_bass_kernel_spmd

    nc = bacc.Bacc("TRN2", target_bir_lowering=False, num_devices=1)
    arrays, args = {}, []
    for name in _INS:
        a = np.ascontiguousarray(inputs[name])
        if name == "x":
            a = a.reshape(SEQ, D_MODEL)
        if name == "na_rpb":
            a = np.ascontiguousarray(a[..., ::-1, ::-1])
        arrays[f"in_{name}"] = a
    arrays["in_constants"] = constant_table()
    for name, a in arrays.items():
        args.append(nc.dram_tensor(name, a.shape, mybir.dt.from_np(a.dtype), kind="ExternalInput").ap())
    out = nc.dram_tensor("out_x", (SEQ, D_MODEL), F32, kind="ExternalOutput").ap()
    build(nc, *args, out)
    r = run_bass_kernel_spmd(nc, [arrays], core_ids=[0])
    return r.results[0]["out_x"].reshape(1, SEQ, D_MODEL)
```

```python
from contextlib import ExitStack

import numpy as np

import concourse.bass as bass
from concourse import mybir

F32 = mybir.dt.float32
F32R = mybir.dt.float32r
I32 = mybir.dt.int32
ALU = mybir.AluOpType
ACT = mybir.ActivationFunctionType
AX_X = mybir.AxisListType.X

P = 128
SEQ, D_MODEL, DEPTH = 256, 1024, 2
BLOCKS = SEQ // P
DC = D_MODEL // P
HEAD = 64
GRID_W = 64
GRID_ROWS = SEQ // GRID_W
EPS = 1e-6
SCALE = HEAD ** -0.5
NEG = -1e30
NA_HEADS, NA_WIN_ROWS, NA_WIN_COLS = 4, 8, 16
RPB_ROWS, RPB_COLS = 2 * NA_WIN_ROWS - 1, 2 * NA_WIN_COLS - 1
GQA_Q, GQA_KV = 6, 2
GQA_REP = GQA_Q // GQA_KV
DIL_GROUPS = ((128, 1), (512, 4), (2048, 16))
DIL_PER_GROUP = 2
DIL_HEADS = len(DIL_GROUPS) * DIL_PER_GROUP
Q_HEADS = NA_HEADS + GQA_Q + DIL_HEADS
K_HEADS = NA_HEADS + GQA_KV + DIL_HEADS
QK_HEADS = Q_HEADS + K_HEADS
Q_W, KV_W = Q_HEADS * HEAD, K_HEADS * HEAD
QK_W = Q_W + KV_W
QKV_W = Q_W + 2 * KV_W
GATE_W = 3 * D_MODEL
BRANCH_W = (NA_HEADS + GQA_Q + DIL_PER_GROUP) * HEAD
OC = BRANCH_W // P
FFN = 2816
EXPERTS, EXPERT_DIM = 8, 3584
SLOTS = 128
ROUNDS = -(-SEQ // SLOTS)

TILE = 2048
COLS = 512
QKV_TILES = 2 * QKV_W // COLS
GATE_TILES = GATE_W // 256
BRANCH_TILES = D_MODEL // 256
OUT_TILES = DC // 2
FFN_COLS = 256
FFN_STEPS = FFN // FFN_COLS
FBLOCKS = EXPERT_DIM // COLS
JB = COLS // P
MOE_TILES = 6 * FBLOCKS
DENSE_RING = 6
MOE_RING = 14
HI_RING = 3
SCATTER_BANKS = (2, 3, 6, 7)

C_IDENT = 0
C_TRI = C_IDENT + P
C_ONES = C_TRI + P
C_IOTA = C_ONES + P
C_IOTA8 = C_IOTA + SLOTS
C_BAND = C_IOTA8 + EXPERTS
C_MOD4 = C_BAND + BLOCKS * SEQ
C_MOD16 = C_MOD4 + 4
C_COLM = C_MOD16 + 16
C_ROPE = C_COLM + GRID_W
C_END = C_ROPE + 2 * 2 * BLOCKS * HEAD


def softmax_units():
    v0 = 0
    units = []
    for c in range(DIL_PER_GROUP):
        tiles = [((NA_HEADS + GQA_Q) // 2 + g, Q_HEADS // 2 + (NA_HEADS + GQA_KV) // 2 + g, c)
                 for g in range(len(DIL_GROUPS))]
        vcols = [v0 + (NA_HEADS + GQA_KV + g * DIL_PER_GROUP + c) * HEAD for g in range(len(DIL_GROUPS))]
        units.append((tiles, vcols, (NA_HEADS + GQA_Q + c) * HEAD, "C"))
    for h in range(NA_HEADS):
        units.append(([(h // 2, Q_HEADS // 2 + h // 2, h % 2)], [v0 + h * HEAD], h * HEAD, f"A{h}"))
    for j in range(GQA_REP):
        for kv in range(GQA_KV):
            units.append(([(NA_HEADS // 2 + j, (Q_HEADS + NA_HEADS) // 2, kv)],
                          [v0 + (NA_HEADS + kv) * HEAD],
                          (NA_HEADS + kv * GQA_REP + j) * HEAD, "B"))
    return units


UNITS = softmax_units()
NU = len(UNITS)
SCORE_TILES = [(u, g) for u, unit in enumerate(UNITS) for g in range(len(unit[0]))]
NS = len(SCORE_TILES)
MASKED_TILES = [i for i, (u, g) in enumerate(SCORE_TILES) if UNITS[u][3] != "B"]
QKT_PAIRS = QK_HEADS // 4
QKT_BANKS = (6, 7, 2, 3)
GATE_PAIRS = GATE_W // (2 * P)
EARLY_PAIRS = 2
GATE_CHUNKS = [3, 3, 2, 2, 2] + [1] * (NU + 1 - 5)
GATE_AT = [range(2 * EARLY_PAIRS + sum(GATE_CHUNKS[:u]), 2 * EARLY_PAIRS + sum(GATE_CHUNKS[:u + 1])) for u in range(NU + 1)]


def dense_tiles():
    tiles = []
    for layer in range(DEPTH):
        tiles += [("qkv", layer, n) for n in range(QKV_TILES)]
        tiles += [("gate", layer, n) for n in range(GATE_TILES)]
        for n in range(BRANCH_TILES):
            tiles.append(("branch", layer, n))
            if n:
                tiles.append(("out", layer, n - 1))
        tiles.append(("out", layer, OUT_TILES - 1))
        if layer % 2 == 0:
            for s in range(FFN_STEPS):
                tiles += [("g", layer // 2, s), ("u", layer // 2, s)]
                if s:
                    tiles.append(("d", layer // 2, s - 1))
            tiles.append(("d", layer // 2, FFN_STEPS - 1))
    return tiles


def moe_tiles():
    tiles = []
    for f in range(FBLOCKS):
        tiles += [("g", f, 0), ("g", f, 1), ("u", f, 0), ("u", f, 1)]
        if f:
            tiles += [("d", f - 1, 0), ("d", f - 1, 1)]
    return tiles + [("d", FBLOCKS - 1, 0), ("d", FBLOCKS - 1, 1)]


DENSE = dense_tiles()
MOE = moe_tiles()
ND = len(DENSE)
PLACE = {t: n for n, t in enumerate(DENSE)}
WIDTH = [OC * 256 if kind == "branch" else TILE for kind, _, _ in DENSE] + [TILE] * len(MOE)
MOE_PLACE = {t: j for j, t in enumerate(MOE)}


def build(nc, x_in, norm_gains, w_in, qk_gains, na_rpb, w_branch, w_out, ffn_w_gu, ffn_w_down,
          moe_router, moe_w_gu, moe_w_down, constants, out):
    assert GATE_AT[-1].stop == 2 * GATE_PAIRS
    assert ND % HI_RING == 0 and MOE_TILES % HI_RING == 0 and MOE_TILES % MOE_RING == 0 and MOE_TILES % 2 == 0
    attn_slots = (C_END - C_BAND + BLOCKS * KV_W + QK_HEADS // 2 * SEQ + BLOCKS * NA_HEADS * SEQ + 6 * SEQ
                  + 8 * BLOCKS * HEAD) // TILE
    before_merge = DENSE_RING - 2
    dense_order = [(ND + j) % DENSE_RING for j in range(DENSE_RING)]
    slot_order = [DENSE_RING + j for j in range(attn_slots)] + dense_order[:before_merge] \
        + list(range(DENSE_RING + attn_slots, MOE_RING)) + dense_order[before_merge:]
    dense_loads = [len([n for n in range(ND) if n % DENSE_RING == s]) for s in range(DENSE_RING)]
    dense_loads += [0] * (MOE_RING - DENSE_RING)

    with ExitStack() as ctx:
        def sb(name, cols, dt=F32, scope=ctx):
            return scope.enter_context(nc.sbuf_tensor(name, [P, cols], dt))

        def sb_split(name, cols):
            with ExitStack() as scope:
                raw = sb(name, cols, F32, scope)
            return raw, sb(name + "_lo", cols, F32R)

        def sem(name):
            return ctx.enter_context(nc.semaphore(name))

        bank = [ctx.enter_context(nc.psum_tensor(f"bank{i}", [P, 512], F32)) for i in range(8)]

        w_hi = sb("w_hi", HI_RING * TILE, F32R)
        slots = [sb_split(f"w_slot{i}", TILE) for i in range(DENSE_RING)]
        a_hi, a_lo = sb("a_hi", DC * SEQ, F32R), sb("a_lo", DC * SEQ, F32R)
        b_hi, b_lo = sb("b_hi", DC * SEQ, F32R), sb("b_lo", DC * SEQ, F32R)
        x_sb = sb("x_sb", BLOCKS * D_MODEL)
        h_sb = sb("h_sb", BLOCKS * D_MODEL)
        cst = sb("cst", C_BAND)
        qk_gain = sb("qk_gain", 6 * HEAD)
        gain_rows = sb("gain_rows", P)
        gainT = sb("gainT", 2 * DEPTH * DC)
        router_sb = sb("router_sb", DC * EXPERTS)
        router_hi, router_lo = sb("router_hi", DC * EXPERTS, F32R), sb("router_lo", DC * EXPERTS, F32R)
        neg_half = sb("neg_half", BLOCKS * QK_HEADS)
        sumsq = sb("sumsq", 2 * BLOCKS)
        rstd = sb("rstd", BLOCKS)
        head_ss = sb("head_ss", BLOCKS * QK_HEADS)
        head_rstd = sb("head_rstd", BLOCKS * QK_HEADS)
        neg_max = sb("neg_max", NU * BLOCKS)
        exp_sum = sb("exp_sum", NU * BLOCKS)
        exp_rsum = sb("exp_rsum", NU * BLOCKS)
        route = sb("route", 11 * BLOCKS * EXPERTS)
        pick = sb("pick", 9 * BLOCKS)
        most = sb("most", 1, I32)
        with ExitStack() as early:
            attn_cst = sb("attn_cst", C_END - C_BAND, F32, early)
            v_area = sb("v_area", BLOCKS * KV_W, F32, early)
            qkT_area = sb("qkT_area", QK_HEADS // 2 * SEQ, F32, early)
            bias_sb = sb("bias_sb", BLOCKS * NA_HEADS * SEQ, F32, early)
            probT_area = sb("probT_area", 6 * SEQ, F32, early)
            rope_tab = sb("rope_tab", 4 * 2 * BLOCKS * HEAD, F32, early)
            gate_area = sb("gate_area", 3 * DC * SEQ, F32, early)
            score_area = sb("score_area", BLOCKS * 3 * SEQ, F32, early)
            prob_area = sb("prob_area", BLOCKS * 3 * SEQ, F32, early)
        slots += [sb_split(f"w_slot{i}", TILE) for i in range(DENSE_RING, MOE_RING)]
        moe_area = sb("moe_area", 2 * COLS + 2 * BLOCKS * SLOTS + 1)
        y_hi, y_lo = sb("y_hi", D_MODEL, F32R), sb("y_lo", D_MODEL, F32R)
        placeT = sb("placeT", SEQ, F32R)

        raw_slot = [raw[:, :] for raw, _ in slots]
        lo_slot = [lo[:, :] for _, lo in slots]
        hi_slot = [w_hi[:, s * TILE:(s + 1) * TILE] for s in range(HI_RING)]
        v_sb = v_area[:, :].rearrange("p (b n) -> p b n", b=BLOCKS)
        gatesT = gate_area[:, :].rearrange("p (i t) -> p i t", t=SEQ)
        qk_sb = gate_area[:, 3 * DC * SEQ - BLOCKS * QK_W:].rearrange("p (b n) -> p b n", b=BLOCKS)
        x = x_sb[:, :].rearrange("p (b n) -> p b n", b=BLOCKS)
        h = h_sb[:, :].rearrange("p (b n) -> p b n", b=BLOCKS)

        def pair(hi, lo, n, inner):
            return [v[:, 0:n].rearrange("p (c t) -> p c t", t=inner) for v in (hi, lo)]

        hT = [pair(a_hi, a_lo, DC * SEQ, SEQ), pair(b_hi, b_lo, DC * SEQ, SEQ)]
        oT = pair(b_hi, b_lo, OC * SEQ, SEQ)
        mergedT = pair(a_hi, a_lo, DC * SEQ, SEQ)
        ffn_actT = [v.rearrange("p (s j) t -> p s j t", s=2) for v in pair(a_hi, a_lo, 4 * SEQ, SEQ)]
        pickedT = pair(a_hi, a_lo, DC * SLOTS, SLOTS)
        actT = [v.rearrange("p (f j) t -> p f j t", f=2) for v in pair(b_hi, b_lo, 2 * JB * SLOTS, SLOTS)]
        qkT = qkT_area[:, :].rearrange("p (c t) -> p c t", t=SEQ)
        bias = bias_sb[:, :].rearrange("p (b h k) -> p b h k", b=BLOCKS, h=NA_HEADS)
        square = [score_area[:, i * COLS:(i + 1) * COLS] for i in range(2)]
        gate_y = [a[:, 0:2 * SEQ].rearrange("p (b t) -> p b t", b=2) for a in (score_area, prob_area)]
        gate_yc = [a[:, 2 * SEQ:3 * SEQ] for a in (score_area, prob_area)]
        gate_yab = [a[:, 3 * SEQ:4 * SEQ] for a in (score_area, prob_area)]
        gate_sum = [a[:, 4 * SEQ:5 * SEQ] for a in (score_area, prob_area)]
        rope_a, rope_b = prob_area[:, :], probT_area[:, :]
        probT = probT_area[:, :].rearrange("p (c t) -> p c t", t=SEQ)
        tab = rope_tab[:, :].rearrange("p (k s b d) -> p k s b d", k=4, s=2, b=BLOCKS)
        qkg = qk_gain[:, :].rearrange("p (a b d) -> p a b d", a=3, b=2)
        gains = gainT[:, :].rearrange("p (k c) -> p k c", c=DC)
        router, *router_parts = [v[:, :].rearrange("p (c e) -> p c e", c=DC) for v in (router_sb, router_hi, router_lo)]
        ss = head_ss[:, :].rearrange("p (b h) -> p b h", b=BLOCKS)
        hr = head_rstd[:, :].rearrange("p (b h) -> p b h", b=BLOCKS)
        nmax = neg_max[:, :].rearrange("p (u b) -> p u b", b=BLOCKS)
        esum = exp_sum[:, :].rearrange("p (u b) -> p u b", b=BLOCKS)
        rsum = exp_rsum[:, :].rearrange("p (u b) -> p u b", b=BLOCKS)
        ident = cst[:, C_IDENT:C_IDENT + P]
        tri = cst[:, C_TRI:C_TRI + P]
        ones = cst[:, C_ONES:C_ONES + P]
        iota = cst[:, C_IOTA:C_IOTA + SLOTS]
        iota8 = cst[:, C_IOTA8:C_IOTA8 + EXPERTS]
        band = attn_cst[:, 0:C_MOD4 - C_BAND].rearrange("p (b k) -> p b k", b=BLOCKS)
        mod4 = attn_cst[:, C_MOD4 - C_BAND:C_MOD16 - C_BAND]
        mod16 = attn_cst[:, C_MOD16 - C_BAND:C_COLM - C_BAND]
        colmask = attn_cst[:, C_COLM - C_BAND:C_ROPE - C_BAND]
        rope_cs = attn_cst[:, C_ROPE - C_BAND:].rearrange("p (r s b d) -> p r s b d", r=2, s=2, b=BLOCKS)
        ffn_act = [score_area[:, i * 512:(i + 1) * 512] for i in range(2)]
        at = [0]

        def cut(n):
            at[0] += n
            return moe_area[:, at[0] - n:at[0]]

        moe_act = [cut(COLS) for _ in range(2)]
        gain_row = moe_area[:, 0:D_MODEL]
        choose = cut(BLOCKS * SLOTS).rearrange("p (b t) -> p b t", b=BLOCKS)
        weigh = cut(BLOCKS * SLOTS).rearrange("p (b t) -> p b t", b=BLOCKS)
        slot_weight = cut(1)
        logitsT = weigh.rearrange("p b t -> p (b t)")[0:EXPERTS, :]

        def route_tile(i):
            return route[:, i * BLOCKS * EXPERTS:(i + 1) * BLOCKS * EXPERTS].rearrange("p (b e) -> p b e", b=BLOCKS)

        lg, eq, cand, is_first, lg2, is_second, sel, gate, rank, gate_t, rank_t = [route_tile(i) for i in range(11)]
        rank_x, gate_x = [v.rearrange("p b e -> p (b e)").rearrange("p (e b) -> p e b", b=BLOCKS) for v in (rank_t, gate_t)]

        def pick_tile(i):
            return pick[:, i * BLOCKS:(i + 1) * BLOCKS]

        x_loaded, ident_loaded, gains_loaded, cst_loaded = [sem(f"x_block{b}_loaded") for b in range(BLOCKS)], sem("ident_loaded"), sem("gains_loaded"), sem("cst_loaded")
        router_loaded, router_hi_ready, router_ready = sem("router_loaded"), sem("router_hi_ready"), sem("router_ready")
        logitsT_done, logitsT_ready = sem("logitsT_done"), sem("logitsT_ready")
        qk_gain_loaded, bias_loaded = sem("qk_gain_loaded"), sem("bias_loaded")
        slot_landed = [sem(f"slot{i}_landed") for i in range(MOE_RING)]
        hi_ready = sem("hi_ready")
        lo_ready = sem("lo_ready")
        w_used = sem("w_used")
        gainT_done, gainT_ready = sem("gainT_done"), sem("gainT_ready")
        sumsq_done, rstd_ready = sem("sumsq_done"), sem("rstd_ready")
        h_ready, xT_done = sem("h_ready"), sem("xT_done")
        hT_hi_ready, hT_ready = sem("hT_hi_ready"), sem("hT_ready")
        qkv_done, square_done, ss_done, qkv_copied = sem("qkv_done"), sem("square_done"), sem("ss_done"), sem("qkv_copied")
        head_rstd_ready = sem("head_rstd_ready")
        tab_ready, bias_ready = sem("tab_ready"), sem("bias_ready")
        qk_ready = sem("qk_ready")
        qkT_done = sem("qkT_done")
        qkT_ready = [sem("qkT_even_ready"), sem("qkT_odd_ready")]
        gate_copied = sem("gate_copied")
        score_done, score_masked = sem("score_done"), sem("score_masked")
        max_ready, exp_done = sem("max_ready"), sem("exp_done")
        probT_done, probT_ready = sem("probT_done"), sem("probT_ready")
        prob_ready, pv_done, oT_hi_ready, oT_ready = sem("prob_ready"), sem("pv_done"), sem("oT_hi_ready"), sem("oT_ready")
        sigmoid_done, y_done, y_read = sem("sigmoid_done"), sem("y_done"), sem("y_read")
        merged_sum, merged_hi_ready, merged_ready = sem("merged_sum"), sem("merged_hi_ready"), sem("merged_ready")
        residual_done, x_ready = sem("residual_done"), sem("x_ready")
        ffn_silu_done, ffn_act_ready = sem("ffn_silu_done"), sem("ffn_act_ready")
        logits_done, gap_ready, gap_exp, sel_ready, rank_done, most_ready = (
            sem("logits_done"), sem("gap_ready"), sem("gap_exp"), sem("sel_ready"), sem("rank_done"), sem("most_ready"))
        choose_ready, weigh_ready, picked_done, picked_ready = (
            sem("weigh_ready"), sem("choose_ready"), sem("picked_done"), sem("picked_ready"))
        picked_hi, act_hi = sem("picked_hi"), sem("act_hi")
        gain_row_loaded, h_scaled = sem("gain_row_loaded"), sem("h_scaled")
        banks_read = sem("banks_read")
        placeT_done, placeT_ready = sem("placeT_done"), sem("placeT_ready")
        silu_done, act_ready, actT_done, actT_ready = sem("silu_done"), sem("act_ready"), sem("actT_done"), sem("actT_ready")
        y_hi_ready, y_ready, scattered = sem("y_hi_ready"), sem("y_ready"), sem("scattered")
        dve_step = sem("dve_step")
        pool_step = sem("pool_step")
        expert_rank = sem("expert_rank")
        x_final, stored = sem("x_final"), sem("stored")

        block = ctx.enter_context(nc.Block())
        OVER = ROUNDS > 1

        def used(layer, kind, i):
            return PLACE[(kind, layer, i)] + 1

        def moe_used(item, j):
            return item * MOE_TILES + (ND + j + 1)

        def ffn_bank(s, g):
            return bank[g] if s == 0 else bank[4 + 2 * (s % 2) + g]

        def o_place(u):
            col = UNITS[u][2]
            return slice(col % P, col % P + HEAD), col // P

        def moe_slot(j):
            return slot_order[j % MOE_RING]

        def split_hi(act, n, landed, raw, free):
            act.wait_ge(*landed)
            if free is not None:
                act.wait_ge(w_used, free)
            nc.scalar.copy(hi_slot[n % HI_RING][:, 0:WIDTH[n]], raw[:, 0:WIDTH[n]]).then_inc(hi_ready, 1)

        def split_lo(eng, n, slot, hi_count, begun=False):
            eng.wait_ge(hi_ready, hi_count)
            cols = slice(WIDTH[n] // 2 if begun else 0, WIDTH[n])
            raw, hi, lo = [v[:, cols] for v in (raw_slot[slot], hi_slot[n % HI_RING], lo_slot[slot])]
            eng.tensor_tensor(lo, raw, hi, ALU.subtract).then_inc(lo_ready, 1)

        class Splitter:

            def __init__(self, eng, part):
                self.eng, self.part, self.next, self.next_moe, self.begun = eng, part, 0, 0, False

            def dense(self, upto):
                for n in range(self.next, min(upto, ND)):
                    slot = n % DENSE_RING
                    if self.part == "hi":
                        split_hi(self.eng, n, (slot_landed[slot], 16 * (n // DENSE_RING + 1)), raw_slot[slot],
                                 n - HI_RING + 1 if n >= HI_RING else None)
                    else:
                        split_lo(self.eng, n, slot, n + 1, self.begun)
                    self.next, self.begun = n + 1, False

            def dense_half(self, upto):
                self.dense(upto - 1)
                n = self.next
                if n < upto and not self.begun:
                    self.eng.wait_ge(hi_ready, n + 1)
                    cols = slice(0, WIDTH[n] // 2)
                    self.eng.tensor_tensor(lo_slot[n % DENSE_RING][:, cols], raw_slot[n % DENSE_RING][:, cols],
                                           hi_slot[n % HI_RING][:, cols], ALU.subtract)
                    self.begun = True

            def moe(self, item, upto):
                for j in range(self.next_moe, min(upto, MOE_TILES)):
                    n, slot = ND + j, moe_slot(j)
                    if self.part == "hi":
                        count = item * (16 * MOE_TILES // MOE_RING) + 16 * (dense_loads[slot] + j // MOE_RING + 1)
                        split_hi(self.eng, n, (slot_landed[slot], count), raw_slot[slot],
                                 item * MOE_TILES + (n - HI_RING + 1))
                    else:
                        split_lo(self.eng, n, slot, item * MOE_TILES + (n + 1))
                    self.next_moe = j + 1
                if upto >= MOE_TILES:
                    self.next_moe = 0

        def passes(eng, first_picks, body, next_round=None):
            def one_round(first_item):
                first_picks(first_item)
                with eng.Fori(0, EXPERTS - 1) as e:
                    body(first_item + e, e, True)
                body(first_item + (EXPERTS - 1), EXPERTS - 1, False)

            one_round(0)
            if OVER:
                eng.wait_ge(most_ready, 1)
                count = eng.value_load(most[0:1, 0:1], min_val=0, max_val=SEQ)
                with eng.If(count > SLOTS):
                    with eng.Fori(1, ROUNDS) as r:
                        if next_round is not None:
                            next_round(r)
                        one_round(r * EXPERTS)

        @block.sync
        def _(sp):
            def source(kind, layer, n):
                def rows(w):
                    return w.rearrange("(c p) n -> p c n", p=P)
                if kind == "qkv":
                    col = n // 2 * COLS
                    return rows(w_in[layer])[:, n % 2 * 4:n % 2 * 4 + 4, col:col + COLS]
                if kind == "gate":
                    return rows(w_in[layer])[:, :, QKV_W + n * 256:QKV_W + (n + 1) * 256]
                if kind == "branch":
                    return rows(w_branch[layer])[:, :, n * 256:(n + 1) * 256]
                if kind == "out":
                    return rows(w_out[layer])[:, 2 * n:2 * n + 2, :]
                if kind == "d":
                    return rows(ffn_w_down[layer])[:, 2 * n:2 * n + 2, :]
                col = n * FFN_COLS + (FFN if kind == "u" else 0)
                return rows(ffn_w_gu[layer])[:, :, col:col + FFN_COLS]

            for b in range(BLOCKS):
                sp.dma_start(x[:, b, :], x_in[b * P:(b + 1) * P, :]).then_inc(x_loaded[b], 16)
            sp.dma_start(cst[:, C_IDENT:C_TRI], constants[:, C_IDENT:C_TRI]).then_inc(ident_loaded, 16)
            sp.dma_start(gain_rows[0:2 * DEPTH * DC, :], norm_gains.rearrange("l k (c p) -> (l k c) p", p=P))\
                .then_inc(gains_loaded, 16)
            for n, tile in enumerate(DENSE):
                if n == 2:
                    gains_by_layer = qk_gains.rearrange("l a b d -> l (a b d)")
                    sp.dma_start(qk_gain[:, :], gains_by_layer[0].partition_broadcast(P))\
                        .then_inc(qk_gain_loaded, 16)
                    sp.dma_start(attn_cst[:, :], constants[:, C_BAND:]).then_inc(cst_loaded, 16)
                    sp.dma_start(cst[:, C_TRI:], constants[:, C_TRI:C_BAND]).then_inc(cst_loaded, 16)
                    sp.dma_start(router, moe_router[0].rearrange("(c p) e -> p c e", p=P)).then_inc(router_loaded, 16)
                src = source(*tile)
                dst = raw_slot[n % DENSE_RING][:, 0:int(np.prod(src.shape[1:]))]
                if n >= DENSE_RING:
                    sp.wait_ge(w_used, n - DENSE_RING + 1)
                sp.dma_start(dst.rearrange("p (c n) -> p c n", c=src.shape[1]), src)\
                    .then_inc(slot_landed[n % DENSE_RING], 16)

            def load_tile(j, e):
                kind, f, half = MOE[j]
                if kind == "d":
                    w = moe_w_down[0, e].rearrange("(c p) n -> p c n", p=P)
                    src = w[:, f * JB + 2 * half:f * JB + 2 * half + 2, :]
                else:
                    col = f * COLS + (EXPERT_DIM if kind == "u" else 0)
                    w = moe_w_gu[0, e].rearrange("(c p) n -> p c n", p=P)
                    src = w[:, 4 * half:4 * half + 4, col:col + COLS]
                slot = moe_slot(j)
                sp.dma_start(raw_slot[slot].rearrange("p (c n) -> p c n", c=src.shape[1]), src)\
                    .then_inc(slot_landed[slot], 16)

            def load_first(before, e):
                for j in range(MOE_RING):
                    sp.wait_ge(w_used, moe_used(before, MOE_TILES - MOE_RING + j))
                    load_tile(j, e)

            def load_rest(item, e):
                for j in range(MOE_RING, MOE_TILES):
                    sp.wait_ge(w_used, moe_used(item, j - MOE_RING))
                    load_tile(j, e)

            def load_round(first_item):
                with sp.Fori(0, EXPERTS - 1) as e:
                    load_rest(first_item + e, e)
                    load_first(first_item + e, e + 1)
                load_rest(first_item + (EXPERTS - 1), EXPERTS - 1)

            for j in range(MOE_RING):
                slot = slot_order[j]
                if slot < DENSE_RING:
                    sp.wait_ge(w_used, ND - DENSE_RING + dense_order.index(slot) + 1)
                elif slot < DENSE_RING + attn_slots:
                    sp.wait_ge(oT_ready, DEPTH * NU)
                else:
                    sp.wait_ge(merged_ready, DEPTH * DC)
                load_tile(j, 0)
            load_round(0)
            if OVER:
                sp.wait_ge(most_ready, 1)
                count = sp.value_load(most[0:1, 0:1], min_val=0, max_val=SEQ)
                with sp.If(count > SLOTS):
                    with sp.Fori(1, ROUNDS) as r:
                        load_first(r * EXPERTS - 1, 0)
                        load_round(r * EXPERTS)
            sp.wait_ge(x_final, 1)
            sp.dma_start(out.rearrange("(b p) n -> p b n", p=P), x).then_inc(stored, 16)
            sp.wait_ge(stored, 16)

        @block.gpsimd
        def _(pool):
            steps = [0]

            def own(ins):
                steps[0] += 1
                ins.then_inc(pool_step, 1)
                pool.wait_ge(pool_step, steps[0])

            own(nc.gpsimd.memset(neg_half[:, :], -0.5))

            def load_bias(layer):
                table = na_rpb[layer, 0:1, 0, 0:1]
                for b in range(BLOCKS):
                    for half in range(P // GRID_W):
                        r = b * (P // GRID_W) + half
                        for head in range(NA_HEADS):
                            offset = (layer * NA_HEADS + head) * RPB_ROWS * RPB_COLS \
                                + (NA_WIN_ROWS - GRID_ROWS + r) * RPB_COLS + NA_WIN_COLS - GRID_W
                            src = bass.AP(table.tensor, offset,
                                          [[1, GRID_W], [RPB_COLS, GRID_ROWS], [1, GRID_W]])
                            dst = bias[half * GRID_W:(half + 1) * GRID_W, b, head, :]
                            pool.dma_start(dst.rearrange("p (r c) -> p r c", c=GRID_W), src)\
                                .then_inc(bias_loaded, 16)

            def norm_power(k):
                for b in range(BLOCKS):
                    first, second = [sumsq[:, 2 * b + half:2 * b + half + 1] for half in range(2)]
                    pool.wait_ge(sumsq_done, 2 * BLOCKS * k + 2 * b + 2)
                    own(nc.gpsimd.tensor_scalar(first, first, second, EPS, ALU.add, ALU.add))
                    nc.gpsimd.tensor_tensor(rstd[:, b:b + 1], first, neg_half[:, 0:1], ALU.pow).then_inc(rstd_ready, 1)

            def head_power(layer, lo, hi, pieces):
                pool.wait_ge(ss_done, 8 * layer + pieces)
                v = ss[:, :, lo:hi]
                own(nc.gpsimd.tensor_scalar(v, v, 1.0 / HEAD, EPS, ALU.mult, ALU.add))
                half = neg_half[:, 0:BLOCKS * (hi - lo)].rearrange("p (b h) -> p b h", b=BLOCKS)
                nc.gpsimd.tensor_tensor(hr[:, :, lo:hi], v, half, ALU.pow).then_inc(head_rstd_ready, 1)

            def rope_tables(layer):
                pool.wait_ge(qk_gain_loaded, 16 * (layer + 1))
                if layer == 0:
                    pool.wait_ge(cst_loaded, 2 * 16)
                else:
                    pool.wait_ge(qk_ready, 4 * layer)
                last = None
                for br in range(2):
                    groups = 2 if br == 0 else 1
                    w = HEAD // groups // 2
                    for qk in range(2):
                        kind = 2 * br + qk
                        g = qkg[:, br + 1, qk, :]
                        nc.gpsimd.tensor_tensor(tab[:, kind, 0], rope_cs[:, br, 0],
                                                g.unsqueeze(1).broadcast_to([P, BLOCKS, HEAD]), ALU.mult)
                        for half in range(2):
                            for gr in range(groups):
                                a = gr * 2 * w + half * w
                                c = gr * 2 * w + (1 - half) * w
                                last = nc.gpsimd.tensor_tensor(
                                    tab[:, kind, 1, :, a:a + w], rope_cs[:, br, 1, :, a:a + w],
                                    g[:, c:c + w].unsqueeze(1).broadcast_to([P, BLOCKS, w]), ALU.mult)
                last.then_inc(tab_ready, 1)

            def bias_mask(layer):
                pool.wait_ge(bias_loaded, 16 * BLOCKS * 2 * NA_HEADS * (layer + 1))
                v = bias_sb[:, :].rearrange("p (n c) -> p n c", c=GRID_W)
                nc.gpsimd.tensor_tensor(v, v, colmask.unsqueeze(1).broadcast_to([P, v.shape[1], GRID_W]),
                                        ALU.add).then_inc(bias_ready, 1)

            for layer in range(DEPTH):
                first = PLACE[("qkv", layer, 0)]
                norm_power(2 * layer)
                if layer == 0:
                    load_bias(0)
                rope_tables(layer)
                head_power(layer, 0, Q_HEADS, 4)
                head_power(layer, Q_HEADS, QK_HEADS, 8)
                bias_mask(layer)
                if layer + 1 < DEPTH:
                    pool.wait_ge(score_masked, len(MASKED_TILES) * (layer + 1))
                    load_bias(layer + 1)
                norm_power(2 * layer + 1)

            pool.wait_ge(gain_row_loaded, 16)
            pool.wait_ge(xT_done, 4 * 2 * DEPTH)
            for b in range(BLOCKS):
                nc.gpsimd.tensor_tensor(h[:, b, :], h[:, b, :], gain_row, ALU.mult).then_inc(h_scaled, 1)

        @block.scalar
        def _(act):
            gains_by_layer = qk_gains.rearrange("l a b d -> l (a b d)")

            split = Splitter(act, "hi")

            def norm_squares(k):
                for b in range(BLOCKS):
                    if k == 0:
                        act.wait_ge(x_loaded[b], 16)
                    for half in range(2):
                        if k:
                            act.wait_ge(x_ready, 4 * (k - 1) + 2 * b + half + 1)
                            act.wait_ge(rstd_ready, BLOCKS * k)
                        cols = slice(half * 512, (half + 1) * 512)
                        nc.scalar.activation(h[:, b, cols], x[:, b, cols], ACT.Square, scale=D_MODEL ** -0.5,
                                             accum_out=sumsq[:, 2 * b + half:2 * b + half + 1]).then_inc(sumsq_done, 1)

            def hT_hi(k):
                for c in range(DC):
                    if c < 4:
                        act.wait_ge(xT_done, 4 * k + c + 1)
                    else:
                        act.wait_ge(hT_ready, DC * k + c - 3)
                    if k == 0 and c == 0:
                        act.wait_ge(gainT_ready, 1)
                    nc.scalar.activation(hT[k % 2][0][:, c, :], bank[4 + c % 4][:, c // 4 * SEQ:(c // 4 + 1) * SEQ],
                                         ACT.Copy, scale=gains[:, k, c:c + 1]).then_inc(hT_hi_ready, 1)

            def qkv_out(layer):
                for i in range(QKV_TILES):
                    n, b = i // 2, i % 2
                    last_tile = used(layer, "qkv", 2 * n + 1)
                    split.dense(last_tile + 2)
                    if b == 0:
                        act.wait_ge(qkv_done, QKV_TILES // 2 * layer + n + 1)
                    else:
                        act.wait_ge(w_used, last_tile)
                    width = min(COLS, max(0, QK_W - n * COLS))
                    if width:
                        k = 8 * layer + i
                        if k >= 2:
                            act.wait_ge(ss_done, k - 1)
                        nc.scalar.activation(square[i % 2][:, 0:width], bank[i % 4][:, 0:width],
                                             ACT.Square).then_inc(square_done, 1)
                    if 0 < width < COLS:
                        nc.scalar.copy(qk_sb[:, b, n * COLS:QK_W], bank[i % 4][:, 0:width])
                        nc.scalar.copy(v_sb[:, b, 0:COLS - width], bank[i % 4][:, width:]).then_inc(qkv_copied, 1)
                    elif width:
                        nc.scalar.copy(qk_sb[:, b, n * COLS:(n + 1) * COLS], bank[i % 4][:, :]).then_inc(qkv_copied, 1)
                    else:
                        nc.scalar.copy(v_sb[:, b, n * COLS - QK_W:(n + 1) * COLS - QK_W],
                                       bank[i % 4][:, :]).then_inc(qkv_copied, 1)

            def gate_out(layer, p):
                last_tile = used(layer, "gate", p)
                split.dense(last_tile + 1)
                act.wait_ge(w_used, last_tile)
                nc.scalar.copy(gatesT[:, 2 * p:2 * p + 2, :].rearrange("p i t -> p (i t)"),
                               bank[4 + p % 2][:, :]).then_inc(gate_copied, 1)

            def exponents(layer, u):
                tiles, _, _, kind = UNITS[u]
                act.wait_ge(max_ready, NU * layer + u + 1)
                n = len(tiles) * SEQ
                for b in range(BLOCKS):
                    if kind == "B":
                        s = next(i for i, t in enumerate(SCORE_TILES) if t == (u, 0))
                        src, scale = bank[s % 3][:, b * SEQ:(b + 1) * SEQ], SCALE
                    else:
                        src, scale = score_area[:, b * n:(b + 1) * n], 1.0
                    last = nc.scalar.activation(prob_area[:, b * n:(b + 1) * n], src, ACT.Exp,
                                                bias=nmax[:, u, b:b + 1], scale=scale,
                                                accum_out=esum[:, u, b:b + 1])
                last.then_inc(exp_done, 1)

            def probT_out(layer, u):
                for g in range(len(UNITS[u][0])):
                    s = SCORE_TILES.index((u, g))
                    act.wait_ge(probT_done, NS * layer + s + 1)
                    if g == 0 and NU * layer + u:
                        act.wait_ge(pv_done, NU * layer + u)
                    nc.scalar.copy(probT[:, 2 * g:2 * g + 2, :].rearrange("p c t -> p (c t)"),
                                   bank[6 + s % 2][:, :]).then_inc(probT_ready, 1)

            def oT_hi_part(layer, u):
                rows, chunk = o_place(u)
                act.wait_ge(pv_done, NU * layer + u + 1)
                nc.scalar.copy(oT[0][rows, chunk, :], bank[3][rows, 0:SEQ]).then_inc(oT_hi_ready, 1)

            def sigmoid(layer, m):
                v = gatesT[:, m:3 * DC:DC, :]
                nc.scalar.activation(v, v, ACT.Sigmoid).then_inc(sigmoid_done, 1)

            def merged_hi_part(layer, m):
                act.wait_ge(merged_sum, DC * layer + m + 1)
                nc.scalar.copy(mergedT[0][:, m, :], gate_sum[m % 2]).then_inc(merged_hi_ready, 1)

            for layer in range(DEPTH):
                norm_squares(2 * layer)
                split.dense(PLACE[("qkv", layer, 0)] + 1)
                hT_hi(2 * layer)
                qkv_out(layer)
                if layer + 1 < DEPTH:
                    act.wait_ge(tab_ready, layer + 1)
                    act.wait_ge(qk_ready, 4 * (layer + 1))
                    act.dma_start(qk_gain[:, :], gains_by_layer[layer + 1].partition_broadcast(P))\
                        .then_inc(qk_gain_loaded, 16)
                for p in range(EARLY_PAIRS):
                    gate_out(layer, p)
                for g in range(1, QKT_PAIRS, 2):
                    act.wait_ge(qkT_done, QKT_PAIRS * layer + g + 1)
                    nc.scalar.copy(qkT[:, 2 * g:2 * g + 2, :].rearrange("p c t -> p (c t)"),
                                   bank[QKT_BANKS[g % 4]][:, :]).then_inc(qkT_ready[1], 1)
                for u in range(NU + 1):
                    if u:
                        probT_out(layer, u - 1)
                    split.dense(used(layer, "gate", GATE_AT[u][-1] // 2) + 1)
                    if u < NU:
                        exponents(layer, u)
                    else:
                        act.wait_ge(gate_copied, GATE_PAIRS * layer + DC + 1)
                        sigmoid(layer, 0)
                    if u:
                        oT_hi_part(layer, u - 1)
                    for i in GATE_AT[u]:
                        if i % 2:
                            gate_out(layer, i // 2)
                act.wait_ge(gate_copied, GATE_PAIRS * (layer + 1))
                split.dense(used(layer, "branch", 1))
                sigmoid(layer, 1)
                for m in range(2, DC):
                    if m % 2 == 0:
                        split.dense(used(layer, "branch", m // 2 - 1) + (3 if m == 4 else 2))
                    sigmoid(layer, m)
                    merged_hi_part(layer, m - 2)
                split.dense(used(layer, "out", OUT_TILES - 1))
                for m in range(DC - 2, DC):
                    merged_hi_part(layer, m)
                split.dense(used(layer, "out", OUT_TILES - 1) + 2)
                if layer == DEPTH - 1:
                    act.wait_ge(merged_ready, DEPTH * DC)
                    act.dma_start(gain_row, norm_gains[layer, 1].partition_broadcast(P)).then_inc(gain_row_loaded, 16)
                norm_squares(2 * layer + 1)
                hT_hi(2 * layer + 1)
                if layer % 2 == 0:
                    for s in range(FFN_STEPS):
                        gate_tile = used(layer // 2, "g", s)
                        split.dense(gate_tile + 2)
                        act.wait_ge(w_used, gate_tile)
                        if s >= 2:
                            act.wait_ge(ffn_act_ready, s - 1)
                        nc.scalar.activation(ffn_act[s % 2], ffn_bank(s, 0)[:, :], ACT.Silu)\
                            .then_inc(ffn_silu_done, 1)
                    split.dense(used(layer // 2, "d", FFN_STEPS - 1) + 2)

            split.moe(0, 2)
            act.wait_ge(gap_ready, 1)
            nc.scalar.activation(pick_tile(5), pick_tile(4), ACT.Exp).then_inc(gap_exp, 1)

            def picked_hi_part(item):
                for g in range(2):
                    act.wait_ge(picked_done, item * 2 + (g + 1))
                    nc.scalar.copy(pickedT[0][:, 4 * g:4 * g + 4, :].rearrange("p c t -> p (c t)"),
                                   bank[4 + g][:, :]).then_inc(picked_hi, 1)

            def first_picks(item):
                split.moe(item, 3)
                picked_hi_part(item)

            def expert(item, e, more):
                def act_hi_part(f):
                    act.wait_ge(actT_done, item * FBLOCKS + f + 1)
                    if f >= 2:
                        act.wait_ge(w_used, moe_used(item, MOE_PLACE[("d", f - 2, 1)]))
                    nc.scalar.copy(actT[0][:, f % 2].rearrange("p j t -> p (j t)"), bank[6][:, :]).then_inc(act_hi, 1)

                for f in range(FBLOCKS):
                    gate_tile = MOE_PLACE[("g", f, 1)]
                    split.moe(item, gate_tile + 1 + 2)
                    act.wait_ge(w_used, moe_used(item, gate_tile))
                    if f >= 2:
                        act.wait_ge(actT_done, item * FBLOCKS + f - 1)
                    nc.scalar.activation(moe_act[f % 2], bank[2][:, :], ACT.Silu).then_inc(silu_done, 1)
                    if f:
                        act_hi_part(f - 1)
                split.moe(item, MOE_PLACE[("d", FBLOCKS - 2, 0)] + 1 + 2)
                act_hi_part(FBLOCKS - 1)
                split.moe(item, MOE_TILES)
                if more:
                    split.moe(item + 1, 2)
                act.wait_ge(w_used, moe_used(item, MOE_TILES - 1))
                act.wait_ge(placeT_ready, item + 1)
                for g in range(2):
                    nc.scalar.activation(y_hi[:, g * 512:(g + 1) * 512], bank[g][:, :], ACT.Copy,
                                         scale=slot_weight).then_inc(y_hi_ready, 1)
                if more:
                    split.moe(item + 1, 3)
                    picked_hi_part(item + 1)

            passes(act, first_picks, expert)

        @block.vector
        def _(dve):
            steps = [0]

            def own(ins):
                steps[0] += 1
                ins.then_inc(dve_step, 1)
                dve.wait_ge(dve_step, steps[0])

            def norm_apply(k):
                for b in range(BLOCKS):
                    dve.wait_ge(rstd_ready, BLOCKS * k + b + 1)
                    for half in range(2):
                        cols = slice(half * 512, (half + 1) * 512)
                        nc.vector.tensor_scalar(h[:, b, cols], x[:, b, cols], rstd[:, b:b + 1], None, ALU.mult)\
                            .then_inc(h_ready, 1)
                if k == 0:
                    dve.wait_ge(gainT_done, 1)
                    nc.vector.tensor_copy(gainT[:, :], bank[0][:, 0:2 * DEPTH * DC]).then_inc(gainT_ready, 1)
                    dve.wait_ge(gainT_ready, 1)
                    split.dense(1)
                for c in range(DC):
                    dve.wait_ge(hT_hi_ready, DC * k + c + 1)
                    last = nc.vector.scalar_tensor_tensor(
                        out=hT[k % 2][1][:, c, :], in0=bank[4 + c % 4][:, c // 4 * SEQ:(c // 4 + 1) * SEQ],
                        scalar=gains[:, k, c:c + 1], in1=hT[k % 2][0][:, c, :], op0=ALU.mult, op1=ALU.subtract)
                    last.then_inc(hT_ready, 1)

            def head_sums(layer, i):
                n, b = i // 2, i % 2
                heads = min(8, QK_HEADS - 8 * n)
                dve.wait_ge(square_done, 8 * layer + i + 1)
                nc.vector.tensor_reduce(ss[:, b, 8 * n:8 * n + heads],
                                        square[i % 2][:, 0:heads * HEAD].rearrange("p (h d) -> p h d", d=HEAD),
                                        AX_X, ALU.add).then_inc(ss_done, 1)

            def rotate(src, dst, kind, groups, b):
                heads = src.shape[1]
                w = HEAD // groups // 2
                ra = rope_a[:, 0:heads * HEAD].rearrange("p (h d) -> p h d", d=HEAD)
                rb = rope_b[:, 0:heads * HEAD].rearrange("p (h d) -> p h d", d=HEAD)
                nc.vector.tensor_tensor(ra, src, tab[:, kind, 0, b].unsqueeze(1).broadcast_to([P, heads, HEAD]), ALU.mult)
                for gr in range(groups):
                    for half in range(2):
                        a = gr * 2 * w + half * w
                        c = gr * 2 * w + (1 - half) * w
                        last = nc.vector.tensor_tensor(
                            rb[:, :, a:a + w], src[:, :, c:c + w],
                            tab[:, kind, 1, b, a:a + w].unsqueeze(1).broadcast_to([P, heads, w]), ALU.mult)
                own(last)
                if kind == 0:
                    for kv in range(GQA_KV):
                        last = nc.vector.tensor_tensor(dst[:, kv:GQA_Q:GQA_KV, :], ra[:, kv * GQA_REP:(kv + 1) * GQA_REP, :],
                                                       rb[:, kv * GQA_REP:(kv + 1) * GQA_REP, :], ALU.add)
                    return last
                return nc.vector.tensor_tensor(dst, ra, rb, ALU.add)

            def qk_norm_rope(layer, qk, splits_to):
                dve.wait_ge(head_rstd_ready, 2 * layer + qk + 1)
                dve.wait_ge(qkv_copied, QKV_TILES * layer + 4 * (qk + 1))
                if qk == 0:
                    dve.wait_ge(tab_ready, layer + 1)
                lo = 0 if qk == 0 else Q_HEADS
                na, nb, ncc = NA_HEADS, (GQA_Q if qk == 0 else GQA_KV), DIL_HEADS
                for b in range(BLOCKS):
                    if b:
                        split.dense(splits_to)
                    v = qk_sb[:, b, lo * HEAD:(lo + na + nb + ncc) * HEAD].rearrange("p (h d) -> p h d", d=HEAD)
                    own(nc.vector.tensor_tensor(v, v, hr[:, b, lo:lo + na + nb + ncc].unsqueeze(2)
                                                .broadcast_to([P, na + nb + ncc, HEAD]), ALU.mult))
                    nc.vector.tensor_tensor(v[:, 0:na, :], v[:, 0:na, :],
                                            qkg[:, 0, qk, :].unsqueeze(1).broadcast_to([P, na, HEAD]), ALU.mult)
                    own(rotate(v[:, na:na + nb, :], v[:, na:na + nb, :], qk, 2, b))
                    rotate(v[:, na + nb:, :], v[:, na + nb:, :], 2 + qk, 1, b).then_inc(qk_ready, 1)
                    dve.wait_ge(qk_ready, 4 * layer + 2 * qk + b + 1)

            def masked_scores(layer, u):
                tiles, _, _, kind = UNITS[u]
                n = len(tiles) * SEQ
                if kind != "B":
                    if NU * layer + u:
                        dve.wait_ge(exp_done, NU * layer + u)
                    for g in range(len(tiles)):
                        s = SCORE_TILES.index((u, g))
                        dve.wait_ge(score_done, NS * layer + s + 1)
                        src = bank[s % 3][:, :].rearrange("p (b k) -> p b k", b=BLOCKS)
                        dst = score_area[:, 0:BLOCKS * n].rearrange("p (b k) -> p b k", b=BLOCKS)[:, :, g * SEQ:(g + 1) * SEQ]
                        if kind == "C" and DIL_GROUPS[g][1] > 1:
                            dil = DIL_GROUPS[g][1]
                            m = (mod4 if dil == 4 else mod16).unsqueeze(1).broadcast_to([P, SEQ // dil, dil])
                            for b in range(BLOCKS):
                                last = nc.vector.scalar_tensor_tensor(
                                    out=dst[:, b, :].rearrange("p (n m) -> p n m", m=dil),
                                    in0=src[:, b, :].rearrange("p (n m) -> p n m", m=dil), scalar=SCALE,
                                    in1=m, op0=ALU.mult, op1=ALU.add)
                        else:
                            if kind != "C" and u == DIL_PER_GROUP:
                                dve.wait_ge(bias_ready, layer + 1)
                            m = band if kind == "C" else bias[:, :, int(kind[1]), ::-1]
                            last = nc.vector.scalar_tensor_tensor(out=dst, in0=src, scalar=SCALE, in1=m,
                                                                  op0=ALU.mult, op1=ALU.add)
                        last.then_inc(score_masked, 1)
                    dve.wait_ge(score_masked, len(MASKED_TILES) * layer + MASKED_TILES.index(s) + 1)
                    nc.vector.tensor_reduce(nmax[:, u, :], score_area[:, 0:BLOCKS * n].rearrange("p (b k) -> p b k", b=BLOCKS),
                                            AX_X, ALU.max, negate=True).then_inc(max_ready, 1)
                else:
                    s = SCORE_TILES.index((u, 0))
                    dve.wait_ge(score_done, NS * layer + s + 1)
                    own(nc.vector.tensor_reduce(nmax[:, u, :], bank[s % 3][:, :].rearrange("p (b k) -> p b k", b=BLOCKS),
                                                AX_X, ALU.max, negate=True))
                    nc.vector.tensor_scalar(nmax[:, u, :], nmax[:, u, :], SCALE, None, ALU.mult).then_inc(max_ready, 1)

            def normalise(layer, u):
                n = len(UNITS[u][0]) * SEQ
                dve.wait_ge(exp_done, NU * layer + u + 1)
                own(nc.vector.reciprocal(rsum[:, u, :], esum[:, u, :]))
                for b in range(BLOCKS):
                    v = prob_area[:, b * n:(b + 1) * n]
                    last = nc.vector.tensor_scalar(v, v, rsum[:, u, b:b + 1], None, ALU.mult)
                last.then_inc(prob_ready, 1)

            def oT_lo_part(layer, u):
                rows, chunk = o_place(u)
                dve.wait_ge(oT_hi_ready, NU * layer + u + 1)
                nc.vector.tensor_tensor(oT[1][rows, chunk, :], bank[3][rows, 0:SEQ], oT[0][rows, chunk, :],
                                        ALU.subtract).then_inc(oT_ready, 1)

            def merge(layer, m):
                k = DC * layer + m
                if m % 2 == 0:
                    dve.wait_ge(y_done, DC // 2 * layer + m // 2 + 1)
                else:
                    dve.wait_ge(w_used, used(layer, "branch", m // 2))
                dve.wait_ge(sigmoid_done, k + 1)
                if m >= 2:
                    dve.wait_ge(merged_ready, k - 1)
                ab, c, s = bank[4 + 2 * (m % 2)], bank[5 + 2 * (m % 2)], m % 2
                nc.vector.tensor_tensor(gate_y[s], ab[:, :].rearrange("p (b t) -> p b t", b=2),
                                        gatesT[:, m:2 * DC:DC, :], ALU.mult)
                nc.vector.tensor_tensor(gate_yc[s], c[:, 0:SEQ], gatesT[:, 2 * DC + m, :], ALU.mult).then_inc(y_read, 1)
                dve.wait_ge(y_read, k + 1)
                own(nc.vector.tensor_tensor(gate_yab[s], gate_y[s][:, 0, :], gate_y[s][:, 1, :], ALU.add))
                nc.vector.tensor_tensor(gate_sum[s], gate_yab[s], gate_yc[s], ALU.add).then_inc(merged_sum, 1)

            def merged_lo_part(layer, m):
                dve.wait_ge(merged_hi_ready, DC * layer + m + 1)
                nc.vector.tensor_tensor(mergedT[1][:, m, :], gate_sum[m % 2], mergedT[0][:, m, :], ALU.subtract)\
                    .then_inc(merged_ready, 1)

            def split_router():
                dve.wait_ge(router_loaded, 16)
                nc.vector.tensor_copy(router_hi[:, :], router_sb[:, :]).then_inc(router_hi_ready, 1)
                dve.wait_ge(router_hi_ready, 1)
                nc.vector.tensor_tensor(router_lo[:, :], router_sb[:, :], router_hi[:, :], ALU.subtract).then_inc(router_ready, 1)

            def add_residual(k, last_tile):
                for i in range(4):
                    if i < 3:
                        dve.wait_ge(residual_done, 3 * k + i + 1)
                    else:
                        dve.wait_ge(w_used, last_tile)
                    v = x[:, i // 2, (i % 2) * 512:(i % 2 + 1) * 512]
                    nc.vector.tensor_tensor(v, v, bank[i][:, :], ALU.add).then_inc(x_ready, 1)

            split = Splitter(dve, "lo")
            for layer in range(DEPTH):
                first = PLACE[("qkv", layer, 0)]
                norm_apply(2 * layer)
                for i in range(8):
                    split.dense(used(layer, "qkv", i // 2 * 2 + 1) + 2)
                    head_sums(layer, i)
                    if i == 5:
                        qk_norm_rope(layer, 0, used(layer, "qkv", 7) + 1)
                split.dense(used(layer, "qkv", QKV_TILES - 1) + 2)
                qk_norm_rope(layer, 1, used(layer, "gate", 0) + 1)
                split.dense(used(layer, "gate", EARLY_PAIRS - 1))
                for g in range(0, QKT_PAIRS, 2):
                    dve.wait_ge(qkT_done, QKT_PAIRS * layer + g + 1)
                    nc.vector.tensor_copy(qkT[:, 2 * g:2 * g + 2, :].rearrange("p c t -> p (c t)"),
                                          bank[QKT_BANKS[g % 4]][:, :]).then_inc(qkT_ready[0], 1)
                split.dense(used(layer, "gate", EARLY_PAIRS - 1) + 1)
                for u in range(NU + 1):
                    if u < NU:
                        masked_scores(layer, u)
                        if len(GATE_AT[u]) > 1:
                            split.dense(used(layer, "gate", GATE_AT[u][-1] // 2) + 1)
                        normalise(layer, u)
                    tile_after = used(layer, "gate", GATE_AT[u][-1] // 2) + 1
                    if u < NU and GATE_AT[u][-1] % 2 == 0:
                        split.dense_half(tile_after)
                    else:
                        split.dense(tile_after)
                    if u:
                        oT_lo_part(layer, u - 1)
                for m in range(0, DC, 2):
                    last = m == DC - 2
                    split.dense(used(layer, "branch", m // 2) + (2 if last else 1))
                    merge(layer, m)
                    merge(layer, m + 1)
                    if not last:
                        split.dense(used(layer, "branch", m // 2) + 2)
                    merged_lo_part(layer, m)
                    merged_lo_part(layer, m + 1)
                last_tile = used(layer, "out", OUT_TILES - 1)
                split.dense(last_tile + 1)
                add_residual(2 * layer, last_tile)
                norm_apply(2 * layer + 1)
                if layer % 2 == 0:
                    for s in range(FFN_STEPS):
                        up_tile = used(layer // 2, "u", s)
                        split.dense(up_tile + 2)
                        if layer == 0 and s == 0:
                            split_router()
                        dve.wait_ge(ffn_silu_done, s + 1)
                        dve.wait_ge(w_used, up_tile)
                        own(nc.vector.tensor_tensor(ffn_act[s % 2], ffn_act[s % 2], ffn_bank(s, 1)[:, :], ALU.mult))
                        if s >= 2:
                            dve.wait_ge(w_used, used(layer // 2, "d", s - 2))
                        hi, lo = [v[:, s % 2].rearrange("p j t -> p (j t)") for v in ffn_actT]
                        own(nc.vector.tensor_copy(hi, ffn_act[s % 2]))
                        nc.vector.tensor_tensor(lo, ffn_act[s % 2], hi, ALU.subtract).then_inc(ffn_act_ready, 1)
                    last_tile = used(layer // 2, "d", FFN_STEPS - 1)
                    split.dense(last_tile + 1)
                    add_residual(2 * layer + 1, last_tile)

            v0, i0, v1, i1, gap, ex, den, w0, w1 = [pick_tile(i) for i in range(9)]

            def spread(v):
                return v.unsqueeze(2).broadcast_to([P, BLOCKS, EXPERTS])

            def greatest(logits, value, index, onehot):
                own(nc.vector.tensor_reduce(value, logits, AX_X, ALU.max))
                own(nc.vector.tensor_tensor(eq, logits, spread(value), ALU.is_ge))
                own(nc.vector.scalar_tensor_tensor(out=cand, in0=eq, scalar=-float(EXPERTS),
                                                   in1=iota8.unsqueeze(1).broadcast_to([P, BLOCKS, EXPERTS]),
                                                   op0=ALU.mult, op1=ALU.add))
                own(nc.vector.tensor_reduce(index, cand, AX_X, ALU.min))
                own(nc.vector.tensor_tensor(onehot, cand, spread(index), ALU.is_equal))

            dve.wait_ge(logitsT_done, 1)
            nc.vector.tensor_copy(logitsT, bank[0][0:EXPERTS, 0:SEQ]).then_inc(logitsT_ready, 1)
            dve.wait_ge(logits_done, 1)
            own(nc.vector.tensor_copy(lg, bank[0][:, SEQ:SEQ + BLOCKS * EXPERTS].rearrange("p (b e) -> p b e", b=BLOCKS)))
            greatest(lg, v0, i0, is_first)
            own(nc.vector.scalar_tensor_tensor(out=lg2, in0=is_first, scalar=-3e38, in1=lg, op0=ALU.mult, op1=ALU.add))
            greatest(lg2, v1, i1, is_second)
            nc.vector.tensor_tensor(gap, v1, v0, ALU.subtract).then_inc(gap_ready, 1)
            nc.vector.tensor_tensor(sel, is_first, is_second, ALU.add).then_inc(sel_ready, 1)
            dve.wait_ge(gap_exp, 1)
            own(nc.vector.tensor_scalar(den, ex, 1.0, None, ALU.add))
            own(nc.vector.reciprocal(w0, den))
            own(nc.vector.tensor_tensor(w1, ex, w0, ALU.mult))
            own(nc.vector.tensor_tensor(is_first, is_first, spread(w0), ALU.mult))
            own(nc.vector.tensor_tensor(is_second, is_second, spread(w1), ALU.mult))
            own(nc.vector.tensor_tensor(gate, is_first, is_second, ALU.add))
            nc.vector.tensor_copy(gate_x, gate.rearrange("p b e -> p e b")).then_inc(banks_read, 4)
            dve.wait_ge(rank_done, 1)
            own(nc.vector.scalar_tensor_tensor(out=rank, in0=bank[1][:, 0:BLOCKS * EXPERTS].rearrange("p (b e) -> p b e", b=BLOCKS),
                                               scalar=1000.0, in1=sel, op0=ALU.add, op1=ALU.mult))
            own(nc.vector.tensor_scalar(rank_x, rank.rearrange("p b e -> p e b"), -1000.0, None, ALU.add))
            nc.vector.tensor_reduce(most[:, 0:1], bank[1][:, BLOCKS * EXPERTS:(BLOCKS + 1) * EXPERTS],
                                    AX_X, ALU.max).then_inc(most_ready, 1)

            def over_slots(v):
                return v.unsqueeze(2).broadcast_to([P, BLOCKS, SLOTS])

            def choose_tokens(item, e):
                nc.vector.tensor_tensor(choose, iota.unsqueeze(1).broadcast_to([P, BLOCKS, SLOTS]),
                                        over_slots(rank_x[:, e, :]), ALU.is_equal).then_inc(choose_ready, 1)

            def weigh_tokens(item, e):
                dve.wait_ge(choose_ready, item + 1)
                nc.vector.tensor_tensor(weigh, choose, over_slots(gate_x[:, e, :]), ALU.mult).then_inc(weigh_ready, 1)

            def picked_lo_part(item, g):
                hi, lo = [v[:, 4 * g:4 * g + 4, :].rearrange("p c t -> p (c t)") for v in pickedT]
                dve.wait_ge(picked_hi, item * 2 + (g + 1))
                nc.vector.tensor_tensor(lo, bank[4 + g][:, :], hi, ALU.subtract).then_inc(picked_ready, 1)

            def first_picks(item):
                choose_tokens(item, 0)
                split.moe(item, 1)
                picked_lo_part(item, 0)
                split.moe(item, 2)
                picked_lo_part(item, 1)
                weigh_tokens(item, 0)
                split.moe(item, 3)

            def expert(item, e, more):
                def act_product(f):
                    up_tile = MOE_PLACE[("u", f, 1)]
                    split.moe(item, up_tile + 1 + 2)
                    dve.wait_ge(silu_done, item * FBLOCKS + f + 1)
                    dve.wait_ge(w_used, moe_used(item, up_tile))
                    nc.vector.tensor_tensor(moe_act[f % 2], moe_act[f % 2], bank[3][:, :], ALU.mult).then_inc(act_ready, 1)

                def act_split(f):
                    if f < FBLOCKS - 1:
                        split.moe(item, MOE_PLACE[("g", f + 1, 1)] + 1 + 2)
                    hi, lo = [v[:, f % 2].rearrange("p j t -> p (j t)") for v in actT]
                    dve.wait_ge(act_hi, item * FBLOCKS + f + 1)
                    nc.vector.tensor_tensor(lo, bank[6][:, :], hi, ALU.subtract).then_inc(actT_ready, 1)

                def add_rows(first, end):
                    for i in range(first, end):
                        dve.wait_ge(scattered, item * 4 + (i + 1))
                        v = x[:, i // 2, (i % 2) * 512:(i % 2 + 1) * 512]
                        nc.vector.tensor_tensor(v, v, bank[SCATTER_BANKS[i]][:, :], ALU.add).then_inc(banks_read, 1)

                for f in range(FBLOCKS):
                    if f:
                        act_split(f - 1)
                    act_product(f)
                    if f == 0:
                        dve.wait_ge(placeT_done, item + 1)
                        nc.vector.tensor_copy(placeT[:, :], bank[7][:, 0:SEQ])
                        nc.vector.tensor_reduce(slot_weight, bank[7][:, SEQ:], AX_X, ALU.add).then_inc(placeT_ready, 1)
                    if f == 1 and more:
                        choose_tokens(item + 1, e + 1)
                    if f == 3 and more:
                        weigh_tokens(item + 1, e + 1)
                split.moe(item, MOE_PLACE[("d", FBLOCKS - 2, 0)] + 1 + 2)
                act_split(FBLOCKS - 1)
                split.moe(item, MOE_TILES)
                if more:
                    split.moe(item + 1, 2)
                dve.wait_ge(placeT_ready, item + 1)
                for g in range(2):
                    col = slice(g * 512, (g + 1) * 512)
                    dve.wait_ge(y_hi_ready, item * 2 + (g + 1))
                    nc.vector.scalar_tensor_tensor(out=y_lo[:, col], in0=bank[g][:, :], scalar=slot_weight,
                                                   in1=y_hi[:, col], op0=ALU.mult, op1=ALU.subtract).then_inc(y_ready, 1)
                for g in range(2):
                    if more:
                        picked_lo_part(item + 1, g)
                    add_rows(g, g + 1)
                if more:
                    split.moe(item + 1, 3)
                add_rows(2, 4)

            def next_round(r):
                nc.vector.tensor_scalar(rank_t, rank_t, -float(SLOTS), None, ALU.add).then_inc(expert_rank, 1)
                dve.wait_ge(expert_rank, r)

            passes(dve, first_picks, expert, next_round)
            dve.drain().then_inc(x_final, 1)

        @block.tensor
        def _(pe):
            def parts(n, slot, c, width):
                return [v[:, 0:width].rearrange("p (c n) -> p c n", c=c) for v in (hi_slot[n % HI_RING], lo_slot[slot])]

            def dense_tile(kind, layer, i, chunks):
                n = PLACE[(kind, layer, i)]
                pe.wait_ge(lo_ready, n + 1)
                return parts(n, n % DENSE_RING, chunks, WIDTH[n])

            def moe_tile(item, kind, f, half, chunks):
                j = MOE_PLACE[(kind, f, half)]
                n = ND + j
                pe.wait_ge(lo_ready, item * MOE_TILES + (n + 1))
                return parts(n, moe_slot(j), chunks, TILE)

            def product(place, lhs, rhs, first, last):
                nc.tensor.matmul(place, lhs[0], rhs[0], start=first, stop=False)
                nc.tensor.matmul(place, lhs[0], rhs[1], start=False, stop=False)
                return nc.tensor.matmul(place, lhs[1], rhs[0], start=False, stop=last)

            def norm_transposes(k):
                if k == 0:
                    pe.wait_ge(ident_loaded, 16)
                    pe.wait_ge(gains_loaded, 16)
                    rows = 2 * DEPTH * DC
                    nc.tensor.transpose(bank[0][:, 0:rows], gain_rows[0:rows, :], ident[0:rows, 0:rows]).then_inc(gainT_done, 1)
                for b in range(BLOCKS):
                    for c in range(DC):
                        if c % 4 == 0:
                            pe.wait_ge(h_ready, 2 * BLOCKS * k + 2 * b + c // 4 + 1)
                        last = nc.tensor.transpose(bank[4 + c % 4][:, (c // 4) * SEQ + b * P:(c // 4) * SEQ + (b + 1) * P],
                                                   h[:, b, c * P:(c + 1) * P], ident)
                        if b == BLOCKS - 1 and c >= 4:
                            last.then_inc(xT_done, 1)

            def project(out_ap, lhs, rhs, n):
                for c in range(n):
                    last = nc.tensor.matmul(out_ap, lhs(c), rhs(c), start=(c == 0), stop=(c == n - 1))
                return last

            def scores(layer, u):
                for g, (qc, kc, half) in enumerate(UNITS[u][0]):
                    s = SCORE_TILES.index((u, g))
                    if s >= 3:
                        pu, _ = SCORE_TILES[s - 3]
                        if UNITS[pu][3] == "B":
                            pe.wait_ge(exp_done, NU * layer + pu + 1)
                        else:
                            pe.wait_ge(score_masked, len(MASKED_TILES) * layer + MASKED_TILES.index(s - 3) + 1)
                    rows = slice(half * HEAD, (half + 1) * HEAD)
                    for b in range(BLOCKS):
                        last = nc.tensor.matmul(bank[s % 3][:, b * SEQ:(b + 1) * SEQ], qkT[rows, qc, b * P:(b + 1) * P],
                                                qkT[rows, kc, :], start=True, stop=True)
                    last.then_inc(score_done, 1)

            def prob_transposes(layer, u):
                tiles = UNITS[u][0]
                n = len(tiles) * SEQ
                pe.wait_ge(prob_ready, NU * layer + u + 1)
                for g in range(len(tiles)):
                    s = SCORE_TILES.index((u, g))
                    if s >= 2:
                        pe.wait_ge(probT_ready, NS * layer + s - 1)
                    for kc in range(2):
                        for b in range(BLOCKS):
                            col = b * n + g * SEQ + kc * P
                            last = nc.tensor.transpose(bank[6 + s % 2][:, kc * SEQ + b * P:kc * SEQ + (b + 1) * P],
                                                       prob_area[:, col:col + P], ident)
                    last.then_inc(probT_done, 1)

            def values(layer, u):
                vcols = UNITS[u][1]
                pe.wait_ge(probT_ready, NS * layer + SCORE_TILES.index((u, len(vcols) - 1)) + 1)
                if NU * layer + u:
                    pe.wait_ge(oT_ready, NU * layer + u)
                rows, _ = o_place(u)
                project(bank[3][rows, 0:SEQ],
                        lambda c: v_sb[:, c % 2, vcols[c // 2]:vcols[c // 2] + HEAD],
                        lambda c: probT[:, c, :], 2 * len(vcols)).then_inc(pv_done, 1)

            def attention(layer):
                x_hi, x_lo = hT[0]
                for n in range(QKV_TILES // 2):
                    for half in range(2):
                        w = dense_tile("qkv", layer, 2 * n + half, 4)
                        for b in range(BLOCKS):
                            i = 2 * n + b
                            if i >= 4 and half == 0:
                                pe.wait_ge(qkv_copied, QKV_TILES * layer + i - 3)
                            for c in range(4):
                                rows = 4 * half + c
                                tok = slice(b * P, (b + 1) * P)
                                if n == 0 and b == 0:
                                    pe.wait_ge(hT_ready, DC * 2 * layer + rows + 1)
                                last = product(bank[i % 4][:, :], (x_hi[:, rows, tok], x_lo[:, rows, tok]),
                                               (w[0][:, c, :], w[1][:, c, :]), rows == 0, rows == DC - 1)
                            if half and b == 0:
                                last.then_inc(qkv_done, 1)
                        last.then_inc(w_used, 1)

                gate_w = [None]

                def gates(i):
                    p, j = i // 2, i % 2
                    if j == 0:
                        gate_w[0] = dense_tile("gate", layer, p, DC)
                        if p >= 2:
                            pe.wait_ge(gate_copied, GATE_PAIRS * layer + p - 1)
                    w = gate_w[0]
                    for c in range(DC):
                        last = product(bank[4 + p % 2][:, j * SEQ:(j + 1) * SEQ],
                                       (w[0][:, c, j * P:(j + 1) * P], w[1][:, c, j * P:(j + 1) * P]),
                                       (x_hi[:, c, :], x_lo[:, c, :]), c == 0, c == DC - 1)
                    if j:
                        last.then_inc(w_used, 1)

                for i in range(2 * EARLY_PAIRS):
                    gates(i)
                copied = [(QKT_PAIRS + 1) // 2 * layer, QKT_PAIRS // 2 * layer]
                for g in range(QKT_PAIRS):
                    if g == 0:
                        pe.wait_ge(qk_ready, 4 * layer + 4)
                        pe.wait_ge(qkv_copied, QKV_TILES * (layer + 1))
                    if g >= 4:
                        pe.wait_ge(qkT_ready[g % 2], copied[g % 2] + g // 2 - 1)
                    for c in range(2):
                        for b in range(BLOCKS):
                            last = nc.tensor.transpose(bank[QKT_BANKS[g % 4]][:, c * SEQ + b * P:c * SEQ + (b + 1) * P],
                                                       qk_sb[:, b, (2 * g + c) * P:(2 * g + c + 1) * P], ident)
                    last.then_inc(qkT_done, 1)
                pe.wait_ge(qkT_ready[0], (QKT_PAIRS + 1) // 2 * (layer + 1))
                pe.wait_ge(qkT_ready[1], QKT_PAIRS // 2 * (layer + 1))
                for u in range(NU + 1):
                    if u:
                        prob_transposes(layer, u - 1)
                    if u < NU:
                        scores(layer, u)
                    gates(GATE_AT[u][0])
                    if u:
                        values(layer, u - 1)
                    for i in GATE_AT[u][1:]:
                        gates(i)
                pe.wait_ge(gate_copied, GATE_PAIRS * (layer + 1))
                pe.wait_ge(oT_ready, NU * (layer + 1) - 1)

                chunks = ((0, 2), (2, 5), (5, 6))

                def branch(n):
                    w = dense_tile("branch", layer, n, OC)
                    for j in range(2):
                        m = 2 * n + j
                        if m >= 2:
                            pe.wait_ge(y_read, DC * layer + m - 1)
                        places = (bank[4 + 2 * j][:, 0:SEQ], bank[4 + 2 * j][:, SEQ:2 * SEQ], bank[5 + 2 * j][:, 0:SEQ])
                        for i in (0, 2, 1):
                            place, (lo, hi) = places[i], chunks[i]
                            for c in range(lo, hi):
                                if m == 0 and c == o_place(NU - 1)[1]:
                                    pe.wait_ge(oT_ready, NU * (layer + 1))
                                last = product(place, (w[0][:, c, j * P:(j + 1) * P], w[1][:, c, j * P:(j + 1) * P]),
                                               (oT[0][:, c, :], oT[1][:, c, :]), c == lo, c == hi - 1)
                        last.then_inc(w_used if j else y_done, 1)

                def project_out(n):
                    w = dense_tile("out", layer, n, 2)
                    pe.wait_ge(merged_ready, DC * layer + 2 * n + 2)
                    rows_product(mergedT, w, (2 * n, 2 * n + 1), n == 0, n == OUT_TILES - 1)

                for n in range(BRANCH_TILES):
                    branch(n)
                    if n:
                        project_out(n - 1)
                project_out(OUT_TILES - 1)

            def rows_product(actT, w, chunks, first, last):
                for i in range(4):
                    tok, col = slice(i // 2 * P, (i // 2 + 1) * P), slice(i % 2 * 512, (i % 2 + 1) * 512)
                    for j in range(2):
                        ins = product(bank[i][:, :], (actT[0][:, chunks[j], tok], actT[1][:, chunks[j], tok]),
                                      (w[0][:, j, col], w[1][:, j, col]), first and j == 0, last and j == 1)
                    if last and i < 3:
                        ins.then_inc(residual_done, 1)
                ins.then_inc(w_used, 1)

            def dense_ffn(layer):
                def gate_up(s):
                    for g, kind in enumerate("gu"):
                        w = dense_tile(kind, layer, s, DC)
                        if s >= 2 and g == 0:
                            pe.wait_ge(ffn_act_ready, s - 1)
                        for j in range(2):
                            for c in range(DC):
                                if s == 0 and g == 0 and j == 0:
                                    pe.wait_ge(hT_ready, DC * (2 * layer + 1) + c + 1)
                                last = product(ffn_bank(s, g)[:, j * SEQ:(j + 1) * SEQ],
                                               (w[0][:, c, j * P:(j + 1) * P], w[1][:, c, j * P:(j + 1) * P]),
                                               (hT[1][0][:, c, :], hT[1][1][:, c, :]), c == 0, c == DC - 1)
                        last.then_inc(w_used, 1)

                def down(s):
                    w = dense_tile("d", layer, s, 2)
                    pe.wait_ge(ffn_act_ready, s + 1)
                    act = [v.rearrange("p s j t -> p (s j) t") for v in ffn_actT]
                    rows_product(act, w, (2 * (s % 2), 2 * (s % 2) + 1), s == 0, s == FFN_STEPS - 1)

                for s in range(FFN_STEPS):
                    gate_up(s)
                    if s:
                        down(s - 1)
                down(FFN_STEPS - 1)

            for layer in range(DEPTH):
                norm_transposes(2 * layer)
                attention(layer)
                norm_transposes(2 * layer + 1)
                if layer % 2 == 0:
                    dense_ffn(layer)

            pe.wait_ge(router_ready, 1)
            for c in range(DC):
                pe.wait_ge(hT_ready, DC * (2 * DEPTH - 1) + c + 1)
                last = product(bank[0][0:EXPERTS, 0:SEQ], [v[:, c, :] for v in router_parts],
                               [v[:, c, :] for v in hT[1]], c == 0, c == DC - 1)
            last.then_inc(logitsT_done, 1)
            pe.wait_ge(logitsT_ready, 1)
            for b in range(BLOCKS):
                last = nc.tensor.transpose(bank[0][:, SEQ + b * EXPERTS:SEQ + (b + 1) * EXPERTS],
                                           logitsT[:, b * P:(b + 1) * P], ident[0:EXPERTS, 0:EXPERTS])
            last.then_inc(logits_done, 1)
            pe.wait_ge(sel_ready, 1)
            sel = route_tile(6)
            nc.tensor.matmul(bank[1][:, 0:EXPERTS], tri, sel[:, 0, :], start=True, stop=True)
            nc.tensor.matmul(bank[1][:, EXPERTS:2 * EXPERTS], ones, sel[:, 0, :], start=True, stop=False)
            nc.tensor.matmul(bank[1][:, EXPERTS:2 * EXPERTS], tri, sel[:, 1, :], start=False, stop=True)
            nc.tensor.matmul(bank[1][:, 2 * EXPERTS:3 * EXPERTS], ones, sel[:, 0, :], start=True, stop=False)
            nc.tensor.matmul(bank[1][:, 2 * EXPERTS:3 * EXPERTS], ones, sel[:, 1, :], start=False, stop=True).then_inc(rank_done, 1)

            def gather(item):
                pe.wait_ge(choose_ready, item + 1)
                for c in range(DC):
                    for b in range(BLOCKS):
                        last = nc.tensor.matmul(bank[4 + c // 4][:, (c % 4) * SLOTS:(c % 4 + 1) * SLOTS],
                                                h[:, b, c * P:(c + 1) * P], choose[:, b, :],
                                                start=(b == 0), stop=(b == BLOCKS - 1))
                    if c % 4 == 3:
                        last.then_inc(picked_done, 1)

            def first_picks(item):
                pe.wait_ge(h_scaled, BLOCKS)
                gather(item)

            def expert(item, e, more):
                def up(kind, f):
                    for half in range(2):
                        w = moe_tile(item, kind, f, half, 4)
                        if f == 0 and kind == "g":
                            pe.wait_ge(picked_ready, item * 2 + half + 1)
                        if f == 0 and half == 0:
                            pe.wait_ge(banks_read, item * 4 + 1 + "gu".index(kind))
                        if f and half == 0:
                            if kind == "g":
                                pe.wait_ge(silu_done, item * FBLOCKS + f)
                            else:
                                pe.wait_ge(act_ready, item * FBLOCKS + f)
                        for c in range(4):
                            rows = 4 * half + c
                            last = product(bank[2 + "gu".index(kind)][:, :], (pickedT[0][:, rows, :], pickedT[1][:, rows, :]),
                                           (w[0][:, c, :], w[1][:, c, :]), rows == 0, rows == DC - 1)
                        last.then_inc(w_used, 1)

                def act_transposes(f):
                    pe.wait_ge(act_ready, item * FBLOCKS + f + 1)
                    if f:
                        pe.wait_ge(actT_ready, item * FBLOCKS + f)
                    else:
                        pe.wait_ge(banks_read, item * 4 + 3)
                    for j in range(JB):
                        last = nc.tensor.transpose(bank[6][:, j * P:(j + 1) * P], moe_act[f % 2][:, j * P:(j + 1) * P], ident)
                    last.then_inc(actT_done, 1)

                def down(f, half):
                    w = moe_tile(item, "d", f, half, 2)
                    if half == 0:
                        pe.wait_ge(actT_ready, item * FBLOCKS + f + 1)
                    for i in range(2):
                        for c in range(2):
                            j = 2 * half + c
                            last = product(bank[i][:, :], (actT[0][:, f % 2, j, :], actT[1][:, f % 2, j, :]),
                                           (w[0][:, c, i * 512:(i + 1) * 512], w[1][:, c, i * 512:(i + 1) * 512]),
                                           f == 0 and j == 0, f == FBLOCKS - 1 and j == JB - 1)
                    last.then_inc(w_used, 1)

                for f in range(FBLOCKS):
                    up("g", f)
                    if f:
                        act_transposes(f - 1)
                    up("u", f)
                    if f == 0:
                        pe.wait_ge(banks_read, item * 4 + 4)
                        pe.wait_ge(weigh_ready, item + 1)
                        for i, table in enumerate((choose, weigh)):
                            for b in range(BLOCKS):
                                last = nc.tensor.transpose(bank[7][:, i * SEQ + b * P:i * SEQ + (b + 1) * P], table[:, b, :], ident)
                        last.then_inc(placeT_done, 1)
                    else:
                        down(f - 1, 0)
                        if f == FBLOCKS - 1:
                            act_transposes(f)
                        down(f - 1, 1)
                down(FBLOCKS - 1, 0)
                down(FBLOCKS - 1, 1)
                if more:
                    gather(item + 1)

                for i in range(4):
                    if i < 2:
                        pe.wait_ge(y_ready, item * 2 + i + 1)
                    for y in (y_hi, y_lo):
                        last = nc.tensor.matmul(bank[SCATTER_BANKS[i]][:, :], placeT[:, (i // 2) * P:(i // 2 + 1) * P],
                                                y[:, (i % 2) * 512:(i % 2 + 1) * 512], start=y is y_hi, stop=y is y_lo)
                    last.then_inc(scattered, 1)

            passes(pe, first_picks, expert)


def constant_table():
    t = np.zeros((P, C_END), np.float32)
    p = np.arange(P)
    t[:, C_IDENT:C_IDENT + P] = np.eye(P)
    t[:, C_TRI:C_TRI + P] = p[:, None] < p[None, :]
    t[:, C_ONES:C_ONES + P] = 1
    t[:, C_IOTA:C_IOTA + SLOTS] = np.arange(SLOTS)
    t[:, C_IOTA8:C_IOTA8 + EXPERTS] = np.arange(EXPERTS)
    k = np.arange(SEQ)
    side = DIL_GROUPS[0][0] // 2
    for b in range(BLOCKS):
        near = np.abs(k[None, :] - (b * P + p)[:, None]) <= side
        t[:, C_BAND + b * SEQ:C_BAND + (b + 1) * SEQ] = np.where(near, 0, NEG)
    t[:, C_MOD4:C_MOD16] = np.where(np.arange(4)[None, :] == (p % 4)[:, None], 0, NEG)
    t[:, C_MOD16:C_COLM] = np.where(np.arange(16)[None, :] == (p % 16)[:, None], 0, NEG)
    c, kc = (p % GRID_W)[:, None], np.arange(GRID_W)[None, :]
    start = np.clip(c - NA_WIN_COLS // 2, 0, GRID_W - NA_WIN_COLS)
    t[:, C_COLM:C_ROPE] = np.where((kc >= start) & (kc < start + NA_WIN_COLS), 0, NEG)[:, ::-1]
    rope = np.zeros((P, 2, 2, BLOCKS, HEAD), np.float32)

    def angles(pos, dim):
        freq = (np.float32(10000.0) ** (-np.arange(0, dim, 2, dtype=np.float32) / np.float32(dim))).astype(np.float32)
        return pos.astype(np.float32)[:, None] * freq[None, :]

    for b in range(BLOCKS):
        pos = b * P + p
        row, col, line = angles(pos // GRID_W, HEAD // 2), angles(pos % GRID_W, HEAD // 2), angles(pos, HEAD)
        for r, parts in enumerate(([row, row, col, col], [line, line])):
            rope[:, r, 0, b] = np.cos(np.concatenate(parts, 1))
            sign = np.concatenate([np.full(a.shape, -1.0 if i % 2 == 0 else 1.0) for i, a in enumerate(parts)], 1)
            rope[:, r, 1, b] = sign * np.sin(np.concatenate(parts, 1))
    t[:, C_ROPE:C_END] = rope.reshape(P, -1)
    return t


_INS = ["x", "norm_gains", "w_in", "qk_gains", "na_rpb", "w_branch", "w_out", "ffn_w_gu", "ffn_w_down",
        "moe_router", "moe_w_gu", "moe_w_down"]


def kernel(**inputs):
    import concourse.bacc as bacc
    from concourse.bass_utils import run_bass_kernel_spmd

    nc = bacc.Bacc("TRN2", target_bir_lowering=False, num_devices=1)
    arrays, args = {}, []
    for name in _INS:
        a = np.ascontiguousarray(inputs[name])
        if name == "x":
            a = a.reshape(SEQ, D_MODEL)
        if name == "na_rpb":
            a = np.ascontiguousarray(a[..., ::-1, ::-1])
        arrays[f"in_{name}"] = a
    arrays["in_constants"] = constant_table()
    for name, a in arrays.items():
        args.append(nc.dram_tensor(name, a.shape, mybir.dt.from_np(a.dtype), kind="ExternalInput").ap())
    out = nc.dram_tensor("out_x", (SEQ, D_MODEL), F32, kind="ExternalOutput").ap()
    build(nc, *args, out)
    r = run_bass_kernel_spmd(nc, [arrays], core_ids=[0])
    return r.results[0]["out_x"].reshape(1, SEQ, D_MODEL)
```
